# Optimizing a Trainium2 kernel written in Bass

```python
import math
import jax, jax.numpy as jnp
from jax import lax
import numpy as np

D_MODEL = 1024
BATCH = 1
SEQ = 256
DEPTH = 2

MOBA_HEADS = 8
HEAD_DIM = 64
MOBA_BLOCK = 256
MOBA_TOPK = 3
MOBA_Q_CHUNK = 16
MLA_HEADS = 8
MLA_Q_LORA = 384
MLA_KV_LORA = 256
MLA_NOPE = 64
MLA_ROPE = 32
MLA_V = 64
ROPE_THETA = 10000.0
DIFF_HEADS = 4
DIFF_QK = 64
DIFF_V = 2 * DIFF_QK
PLE_DIM = 256
Q_BLOCK = 128
NORM_EPS = 1e-5
NEG = -1e30

MOBA_W = MOBA_HEADS * HEAD_DIM
MLA_W = MLA_HEADS * MLA_V
DIFF_W = DIFF_HEADS * DIFF_V
DIFF_QK_W = DIFF_HEADS * 2 * DIFF_QK
IN_SIZES = (MOBA_W, MOBA_W, MOBA_W, MOBA_W,
            MLA_Q_LORA, MLA_KV_LORA, MLA_ROPE, MLA_W,
            DIFF_QK_W, DIFF_QK_W, DIFF_W, DIFF_W)
IN_WIDTH = sum(IN_SIZES)
N_BRANCH = 3
ALPHA = (2 * DEPTH) ** 0.25
BETA = (8 * DEPTH) ** -0.25


def _split_points():
    return [int(v) for v in np.cumsum(np.array(IN_SIZES))[:-1]]

def _alibi_slopes():
    n = MOBA_HEADS + DIFF_HEADS
    s = 2.0 ** (-8.0 * (np.arange(n) + 1) / n)
    diff_idx = np.arange(DIFF_HEADS) * (n // DIFF_HEADS)
    moba_idx = np.setdiff1d(np.arange(n), diff_idx)
    return (jnp.asarray(s[moba_idx], dtype=jnp.float32),
            jnp.asarray(s[diff_idx], dtype=jnp.float32))

def _rmsnorm(x, g, eps=1e-6):
    xf = x.astype(jnp.float32)
    y = xf * lax.rsqrt(jnp.mean(xf * xf, axis=-1, keepdims=True) + eps)
    return (y * g.astype(jnp.float32)).astype(x.dtype)

def _layernorm(x, g, b):
    xf = x.astype(jnp.float32)
    mu = jnp.mean(xf, axis=-1, keepdims=True)
    var = jnp.mean(jnp.square(xf - mu), axis=-1, keepdims=True)
    y = (xf - mu) * lax.rsqrt(var + NORM_EPS)
    return (y * g.astype(jnp.float32) + b.astype(jnp.float32)).astype(x.dtype)

def _rope(t, pos):
    d = t.shape[-1]
    freqs = ROPE_THETA ** (-jnp.arange(0, d, 2, dtype=jnp.float32) / d)
    ang = pos.astype(jnp.float32)[:, None] * freqs[None, :]
    cos, sin = jnp.cos(ang), jnp.sin(ang)
    tf = t.astype(jnp.float32)
    t1, t2 = tf[..., : d // 2], tf[..., d // 2:]
    return jnp.concatenate([t1 * cos - t2 * sin, t1 * sin + t2 * cos], axis=-1).astype(t.dtype)

def _split_heads(t, n):
    B, S, _ = t.shape
    return t.reshape(B, S, n, -1).transpose(0, 2, 1, 3)

def _merge_heads(t):
    B, H, S, d = t.shape
    return t.transpose(0, 2, 1, 3).reshape(B, S, H * d)

def moba_attention(q, k, v, slopes):
    B, H, S, dh = q.shape
    blk = MOBA_BLOCK
    nb = -(-S // blk)
    s_pad = nb * blk
    padw = ((0, 0), (0, 0), (0, s_pad - S), (0, 0))
    kp = jnp.pad(k, padw)
    vp = jnp.pad(v, padw)
    kb = kp.reshape(B, H, nb, blk, dh)
    vb = vp.reshape(B, H, nb, blk, dh)
    kmean = jnp.mean(kb.astype(jnp.float32), axis=3)
    pos = jnp.arange(S)
    gate = jnp.einsum('bhsd,bhnd->bhsn', q.astype(jnp.float32), kmean)
    past = jnp.arange(nb)[None, :] < (pos // blk)[:, None]
    gate = jnp.where(past, gate, -jnp.inf)
    kk = min(MOBA_TOPK, nb)
    _, sel = lax.top_k(gate, kk)

    C = MOBA_Q_CHUNK
    nc = S // C
    qc = q.reshape(B, H, nc, C, dh).transpose(2, 0, 1, 3, 4)
    selc = sel.reshape(B, H, nc, C, kk).transpose(2, 0, 1, 3, 4)
    bi = jnp.arange(B)[:, None, None, None]
    hi = jnp.arange(H)[None, :, None, None]
    scale = dh ** -0.5
    offs = jnp.arange(blk)

    def one(args):
        qi, si, c = args
        qpos = c * C + jnp.arange(C)
        ob = (c * C) // blk
        kg = kb[bi, hi, si]
        vg = vb[bi, hi, si]
        s_sel = jnp.einsum('bhqd,bhqjkd->bhqjk', qi, kg).astype(jnp.float32) * scale
        kpos_sel = si[..., None] * blk + offs
        dist_sel = (qpos[None, None, :, None, None] - kpos_sel).astype(jnp.float32)
        s_sel = s_sel - slopes[None, :, None, None, None] * dist_sel
        valid = jnp.arange(kk)[None, :] < (qpos // blk)[:, None]
        s_sel = jnp.where(valid[None, None, :, :, None], s_sel, NEG)
        ko = lax.dynamic_slice_in_dim(kp, ob * blk, blk, axis=2)
        vo = lax.dynamic_slice_in_dim(vp, ob * blk, blk, axis=2)
        dist_own = (qpos[:, None] - (ob * blk + offs)[None, :]).astype(jnp.float32)
        s_own = jnp.einsum('bhqd,bhkd->bhqk', qi, ko).astype(jnp.float32) * scale
        s_own = s_own - slopes[None, :, None, None] * dist_own
        s_own = jnp.where(dist_own >= 0, s_own, NEG)
        s_all = jnp.concatenate([s_sel.reshape(B, H, C, kk * blk), s_own], axis=-1)
        pr = jax.nn.softmax(s_all, axis=-1).astype(v.dtype)
        p_sel = pr[..., : kk * blk].reshape(B, H, C, kk, blk)
        p_own = pr[..., kk * blk:]
        return (jnp.einsum('bhqjk,bhqjkd->bhqd', p_sel, vg)
                + jnp.einsum('bhqk,bhkd->bhqd', p_own, vo))

    out = lax.map(one, (qc, selc, jnp.arange(nc)))
    return out.transpose(1, 2, 0, 3, 4).reshape(B, H, S, dh)

def mla_attention(q, k, v):
    B, H, S, dq = q.shape
    nq = S // Q_BLOCK
    scale = dq ** -0.5
    qb = q.reshape(B, H, nq, Q_BLOCK, dq).transpose(2, 0, 1, 3, 4)
    kpos = jnp.arange(S)

    def one(args):
        qi, i = args
        qpos = i * Q_BLOCK + jnp.arange(Q_BLOCK)
        s = jnp.einsum('bhqd,bhkd->bhqk', qi, k).astype(jnp.float32) * scale
        s = jnp.where(kpos[None, :] <= qpos[:, None], s, NEG)
        pr = jax.nn.softmax(s, axis=-1).astype(v.dtype)
        return jnp.einsum('bhqk,bhkd->bhqd', pr, v)

    out = lax.map(one, (qb, jnp.arange(nq)))
    return out.transpose(1, 2, 0, 3, 4).reshape(B, H, S, -1)

def diff_attention(q, k, v, slopes, lam):
    B, H, S = q.shape[:3]
    nq = S // Q_BLOCK
    scale = DIFF_QK ** -0.5
    qb = q.reshape(B, H, nq, Q_BLOCK, 2, DIFF_QK).transpose(2, 0, 1, 3, 4, 5)
    kpos = jnp.arange(S)

    def one(args):
        qi, i = args
        qpos = i * Q_BLOCK + jnp.arange(Q_BLOCK)
        dist = (qpos[:, None] - kpos[None, :]).astype(jnp.float32)
        s = jnp.einsum('bhqcd,bhkcd->bhcqk', qi, k).astype(jnp.float32) * scale
        s = s - slopes[None, :, None, None, None] * dist
        s = jnp.where(dist >= 0, s, NEG)
        pr = jax.nn.softmax(s, axis=-1)
        a = (pr[:, :, 0] - lam * pr[:, :, 1]).astype(v.dtype)
        return jnp.einsum('bhqk,bhkd->bhqd', a, v)

    out = lax.map(one, (qb, jnp.arange(nq)))
    return out.transpose(1, 2, 0, 3, 4).reshape(B, H, S, -1)

def _layer(x, p_i, li, w_in, gq, gkv, w_uq, w_ukv, lam_p, subln_g, w_a, w_b, w_c,
           w_m, b_m, w_o, ln_g, ln_b, w_pg, w_p, slopes_a, slopes_c):
    B, S, D = x.shape
    pos = jnp.arange(S)
    h = x @ w_in
    (a_q, a_k, a_v, a_z, b_cq, b_ckv, b_kr, b_z,
     c_q, c_k, c_v, c_z) = jnp.split(h, _split_points(), axis=-1)

    ya = moba_attention(_split_heads(a_q, MOBA_HEADS), _split_heads(a_k, MOBA_HEADS),
                        _split_heads(a_v, MOBA_HEADS), slopes_a)
    ya = _merge_heads(ya) * jax.nn.silu(a_z)

    cq = _rmsnorm(b_cq, gq)
    ckv = _rmsnorm(b_ckv, gkv)
    qh = _split_heads(cq @ w_uq, MLA_HEADS)
    q_b = jnp.concatenate([qh[..., :MLA_NOPE], _rope(qh[..., MLA_NOPE:], pos)], axis=-1)
    kvh = _split_heads(ckv @ w_ukv, MLA_HEADS)
    k_rope = _rope(b_kr[:, None], pos)
    k_b = jnp.concatenate([kvh[..., :MLA_NOPE],
                           jnp.broadcast_to(k_rope, (B, MLA_HEADS, S, MLA_ROPE))], axis=-1)
    yb = mla_attention(q_b, k_b, kvh[..., MLA_NOPE:])
    yb = _merge_heads(yb) * jax.nn.silu(b_z)

    lam_init = 0.8 - 0.6 * math.exp(-0.3 * li)
    lf = lam_p.astype(jnp.float32)
    lam = (jnp.exp(jnp.sum(lf[0] * lf[1])) - jnp.exp(jnp.sum(lf[2] * lf[3])) + lam_init)
    qc = c_q.reshape(B, S, DIFF_HEADS, 2, DIFF_QK).transpose(0, 2, 1, 3, 4)
    kc = c_k.reshape(B, S, DIFF_HEADS, 2, DIFF_QK).transpose(0, 2, 1, 3, 4)
    yc = diff_attention(qc, kc, _split_heads(c_v, DIFF_HEADS), slopes_c, lam)
    yc = _rmsnorm(yc, subln_g, eps=1e-5) * (1.0 - lam_init)
    yc = _merge_heads(yc) * jax.nn.silu(c_z)

    g = jax.nn.sigmoid(x @ w_m + b_m)
    ga, gb, gc = jnp.split(g, N_BRANCH, axis=-1)
    merged = ga * (ya @ w_a) + gb * (yb @ w_b) + gc * (yc @ w_c)
    out = merged @ w_o

    r = ALPHA * x + out
    r = r + jax.nn.sigmoid(r @ w_pg) * (p_i @ w_p)
    return _layernorm(r, ln_g, ln_b)

def first_inputs(seed: int = 0) -> dict:
    key = jax.random.key(seed)
    ks = jax.random.split(key, 20)
    f32 = jnp.float32

    def nrm(k, shape, scale):
        return jax.random.normal(k, shape, f32) * scale

    L, D = DEPTH, D_MODEL
    return {
        'x': nrm(ks[0], (BATCH, SEQ, D), 1.0),
        'p': nrm(ks[1], (L, BATCH, SEQ, PLE_DIM), 1.0),
        'w_in': nrm(ks[2], (L, D, IN_WIDTH), D ** -0.5),
        'mla_q_norm_g': 1.0 + nrm(ks[3], (L, MLA_Q_LORA), 0.01),
        'mla_kv_norm_g': 1.0 + nrm(ks[4], (L, MLA_KV_LORA), 0.01),
        'mla_w_uq': nrm(ks[5], (L, MLA_Q_LORA, MLA_HEADS * (MLA_NOPE + MLA_ROPE)), MLA_Q_LORA ** -0.5),
        'mla_w_ukv': nrm(ks[6], (L, MLA_KV_LORA, MLA_HEADS * (MLA_NOPE + MLA_V)), MLA_KV_LORA ** -0.5),
        'diff_lambda': nrm(ks[7], (L, 4, DIFF_QK), 0.1),
        'diff_subln_g': 1.0 + nrm(ks[8], (L, DIFF_V), 0.01),
        'w_branch_a': nrm(ks[9], (L, MOBA_W, D), BETA * MOBA_W ** -0.5),
        'w_branch_b': nrm(ks[10], (L, MLA_W, D), BETA * MLA_W ** -0.5),
        'w_branch_c': nrm(ks[11], (L, DIFF_W, D), BETA * DIFF_W ** -0.5),
        'w_merge': nrm(ks[12], (L, D, N_BRANCH * D), D ** -0.5),
        'b_merge': nrm(ks[13], (L, N_BRANCH * D), 0.01),
        'w_out': nrm(ks[14], (L, D, D), BETA * D ** -0.5),
        'ln_g': 1.0 + nrm(ks[15], (L, D), 0.01),
        'ln_b': nrm(ks[16], (L, D), 0.01),
        'w_ple_gate': nrm(ks[17], (L, D, D), D ** -0.5),
        'w_ple': nrm(ks[18], (L, PLE_DIM, D), BETA * PLE_DIM ** -0.5),
    }

def first_block(x, p, w_in, mla_q_norm_g, mla_kv_norm_g, mla_w_uq, mla_w_ukv, diff_lambda,
              diff_subln_g, w_branch_a, w_branch_b, w_branch_c, w_merge, b_merge, w_out,
              ln_g, ln_b, w_ple_gate, w_ple):
    slopes_a, slopes_c = _alibi_slopes()
    h = x
    for i in range(DEPTH):
        h = _layer(h, p[i], i, w_in[i], mla_q_norm_g[i], mla_kv_norm_g[i], mla_w_uq[i],
                   mla_w_ukv[i], diff_lambda[i], diff_subln_g[i], w_branch_a[i], w_branch_b[i],
                   w_branch_c[i], w_merge[i], b_merge[i], w_out[i], ln_g[i], ln_b[i],
                   w_ple_gate[i], w_ple[i], slopes_a, slopes_c)
    return h


D_MIX = D_MODEL
GROUP_DIM = 64
W_A = D_MIX // 4
W_SSD = D_MIX // 2
W_CONF = D_MIX - W_A - W_SSD
A_CONV = 3
SSD_HEAD_DIM = 64
SSD_HEADS = W_SSD // SSD_HEAD_DIM
SSD_GROUPS = 2
SSD_STATE = 128
SSD_CONV = 4
SSD_CHUNK = 128
SSD_XBC = W_SSD + 2 * SSD_GROUPS * SSD_STATE
CONF_KERNEL = 31
IN_COLS = 3 * W_A + W_SSD + SSD_XBC + SSD_HEADS + 2 * W_CONF
D_FF = ((8 * D_MODEL // 3 + 127) // 128) * 128
N_EXPERTS = 8
TOP_K = 2
D_FF_EXPERT = 7 * D_MODEL // 2
MOE_BLOCK = 128
N_DENSE = (DEPTH + 1) // 2
N_MOE = DEPTH // 2
EPS = 1e-5

_SPLITS = list(np.cumsum([W_A, W_A, W_A, W_SSD, SSD_XBC, SSD_HEADS])[:])


def rmsnorm(x, w):
    xf = x.astype(jnp.float32)
    y = xf * lax.rsqrt(jnp.mean(xf * xf, axis=-1, keepdims=True) + EPS)
    return (y * w.astype(jnp.float32)).astype(x.dtype)

def layernorm(x, g, b):
    xf = x.astype(jnp.float32)
    mu = jnp.mean(xf, axis=-1, keepdims=True)
    var = jnp.mean(jnp.square(xf - mu), axis=-1, keepdims=True)
    y = (xf - mu) * lax.rsqrt(var + EPS)
    return (y * g.astype(jnp.float32) + b.astype(jnp.float32)).astype(x.dtype)

def causal_dwconv(u, w, b=None):
    k, c = w.shape
    y = lax.conv_general_dilated(
        u, w[:, None, :].astype(u.dtype), window_strides=(1,), padding=[(k - 1, 0)],
        dimension_numbers=('NWC', 'WIO', 'NWC'), feature_group_count=c)
    return y if b is None else y + b

def ssd_chunked(xh, dt, a, bm, cm):
    bsz, seq = xh.shape[:2]
    nc = seq // SSD_CHUNK
    r = SSD_HEADS // SSD_GROUPS
    f32 = jnp.float32
    xc = xh.reshape(bsz, nc, SSD_CHUNK, SSD_GROUPS, r, SSD_HEAD_DIM).astype(f32)
    dtc = dt.reshape(bsz, nc, SSD_CHUNK, SSD_GROUPS, r)
    bc = bm.reshape(bsz, nc, SSD_CHUNK, SSD_GROUPS, SSD_STATE).astype(f32)
    cc = cm.reshape(bsz, nc, SSD_CHUNK, SSD_GROUPS, SSD_STATE).astype(f32)
    xdt = xc * dtc[..., None]
    a_cum = jnp.cumsum(dtc * a.reshape(SSD_GROUPS, r), axis=2)
    causal = jnp.tril(jnp.ones((SSD_CHUNK, SSD_CHUNK), dtype=bool))
    seg = a_cum[:, :, :, None] - a_cum[:, :, None, :]
    decay_ls = jnp.exp(jnp.where(causal[:, :, None, None], seg, -jnp.inf))
    cb = jnp.einsum('bclgn,bcsgn->bclsg', cc, bc)
    y_diag = jnp.einsum('bclsg,bclsgr,bcsgrp->bclgrp', cb, decay_ls, xdt)
    decay_to_end = jnp.exp(a_cum[:, :, -1:] - a_cum)
    states = jnp.einsum('bclgn,bclgr,bclgrp->bcgrpn', bc, decay_to_end, xdt)
    chunk_decay = jnp.exp(a_cum[:, :, -1])

    def step(h, inp):
        dec, st = inp
        return dec[..., None, None] * h + st, h

    h0 = jnp.zeros_like(states[:, 0])
    _, h_prev = lax.scan(step, h0, (jnp.moveaxis(chunk_decay, 1, 0), jnp.moveaxis(states, 1, 0)))
    h_prev = jnp.moveaxis(h_prev, 0, 1)
    y_off = jnp.einsum('bclgn,bcgrpn,bclgr->bclgrp', cc, h_prev, jnp.exp(a_cum))
    return (y_diag + y_off).reshape(bsz, seq, SSD_HEADS, SSD_HEAD_DIM)

def gated_rmsnorm(y, z, w):
    yz = (y * jax.nn.silu(z)).astype(jnp.float32)
    shp = yz.shape
    yg = yz.reshape(shp[:-1] + (SSD_GROUPS, shp[-1] // SSD_GROUPS))
    yg = yg * lax.rsqrt(jnp.mean(yg * yg, axis=-1, keepdims=True) + EPS)
    return (yg.reshape(shp) * w.astype(jnp.float32)).astype(y.dtype)

def hybrid_mixer(h, w_in, conv_a_w, conv_ssd_w, conv_ssd_b, dt_bias, a_log, d_skip,
                 ssd_norm_w, conv_conf_w, conv_conf_b, conf_ln_g, conf_ln_b, w_out):
    bsz, seq, _ = h.shape
    proj = h @ w_in
    a_b, a_c, a_x, s_z, s_xbc, s_dt, c_glu = jnp.split(proj, _SPLITS, axis=-1)
    y_a = a_b * causal_dwconv(a_c * a_x, conv_a_w)
    xbc = jax.nn.silu(causal_dwconv(s_xbc, conv_ssd_w, conv_ssd_b))
    s_x, s_b, s_c = jnp.split(xbc, [W_SSD, W_SSD + SSD_GROUPS * SSD_STATE], axis=-1)
    dt = jax.nn.softplus(s_dt.astype(jnp.float32) + dt_bias.astype(jnp.float32))
    a = -jnp.exp(a_log.astype(jnp.float32))
    xh = s_x.reshape(bsz, seq, SSD_HEADS, SSD_HEAD_DIM)
    y_s = ssd_chunked(xh, dt, a,
                      s_b.reshape(bsz, seq, SSD_GROUPS, SSD_STATE),
                      s_c.reshape(bsz, seq, SSD_GROUPS, SSD_STATE)).astype(h.dtype)
    y_s = (y_s + d_skip[:, None] * xh).reshape(bsz, seq, W_SSD)
    y_s = gated_rmsnorm(y_s, s_z, ssd_norm_w)
    g = c_glu[..., :W_CONF] * jax.nn.sigmoid(c_glu[..., W_CONF:])
    g = causal_dwconv(g, conv_conf_w, conv_conf_b)
    y_c = jax.nn.silu(layernorm(g, conf_ln_g, conf_ln_b))
    return jnp.concatenate([y_a, y_s, y_c], axis=-1) @ w_out

def swiglu(h, w_gate, w_up, w_down):
    return (jax.nn.silu(h @ w_gate) * (h @ w_up)) @ w_down

def moe_swiglu(h, w_router, w_gate, w_up, w_down):
    bsz, seq, d = h.shape
    t = bsz * seq
    m = t * TOP_K
    hf = h.reshape(t, d)
    logits = (hf @ w_router).astype(jnp.float32)
    top_vals, top_idx = lax.top_k(logits, TOP_K)
    gates = jax.nn.softmax(top_vals, axis=-1)
    flat_e = top_idx.reshape(m)
    order = jnp.argsort(flat_e)
    sorted_e = flat_e[order]
    tok = order // TOP_K
    sizes = jnp.bincount(flat_e, length=N_EXPERTS).astype(jnp.int32)
    padded = ((sizes + MOE_BLOCK - 1) // MOE_BLOCK) * MOE_BLOCK
    ends = jnp.cumsum(padded)
    starts_pad = ends - padded
    starts_sorted = jnp.cumsum(sizes) - sizes
    dest = starts_pad[sorted_e] + (jnp.arange(m, dtype=jnp.int32) - starts_sorted[sorted_e])
    cap = m + N_EXPERTS * MOE_BLOCK
    n_blocks = cap // MOE_BLOCK
    buf = jnp.zeros((cap, d), hf.dtype).at[dest].set(hf[tok])
    blk_e = jnp.minimum(jnp.searchsorted(ends, jnp.arange(n_blocks, dtype=jnp.int32) * MOE_BLOCK,
                                         side='right'), N_EXPERTS - 1)

    def expert_block(args):
        xb, e = args
        return (jax.nn.silu(xb @ w_gate[e]) * (xb @ w_up[e])) @ w_down[e]

    ybuf = lax.map(expert_block, (buf.reshape(n_blocks, MOE_BLOCK, d), blk_e)).reshape(cap, d)
    y = ybuf[dest] * gates.reshape(m)[order][:, None].astype(ybuf.dtype)
    out = jnp.zeros_like(hf).at[tok].add(y)
    return out.reshape(bsz, seq, d)

def second_inputs(seed: int = 0) -> dict:
    key = jax.random.key(seed)
    ks = jax.random.split(key, 32)
    f32 = jnp.float32

    def nrm(k, shape, scale):
        return jax.random.normal(k, shape, f32) * scale

    def gain(k, shape):
        return 1.0 + 0.02 * jax.random.normal(k, shape, f32)

    dt0 = jnp.exp(jax.random.uniform(ks[5], (DEPTH, SSD_HEADS), f32,
                                     math.log(1e-3), math.log(1e-1)))
    dt_bias = dt0 + jnp.log(-jnp.expm1(-dt0))
    a_log = jnp.log(jax.random.uniform(ks[6], (DEPTH, SSD_HEADS), f32, 1.0, 16.0))
    return {
        'x': jax.random.normal(ks[0], (BATCH, SEQ, D_MODEL), f32),
        'norm_mix': gain(ks[1], (DEPTH, D_MODEL)),
        'w_in': nrm(ks[2], (DEPTH, D_MODEL, IN_COLS), D_MODEL ** -0.5),
        'conv_a_w': nrm(ks[3], (DEPTH, A_CONV, W_A), A_CONV ** -0.5),
        'conv_ssd_w': nrm(ks[4], (DEPTH, SSD_CONV, SSD_XBC), SSD_CONV ** -0.5),
        'conv_ssd_b': nrm(ks[7], (DEPTH, SSD_XBC), 0.02),
        'dt_bias': dt_bias,
        'a_log': a_log,
        'd_skip': 1.0 + 0.1 * jax.random.normal(ks[8], (DEPTH, SSD_HEADS), f32),
        'ssd_norm_w': gain(ks[9], (DEPTH, W_SSD)),
        'conv_conf_w': nrm(ks[10], (DEPTH, CONF_KERNEL, W_CONF), CONF_KERNEL ** -0.5),
        'conv_conf_b': nrm(ks[11], (DEPTH, W_CONF), 0.02),
        'conf_ln_g': gain(ks[12], (DEPTH, W_CONF)),
        'conf_ln_b': nrm(ks[13], (DEPTH, W_CONF), 0.02),
        'w_out': nrm(ks[14], (DEPTH, D_MIX, D_MODEL), D_MIX ** -0.5),
        'norm_ffn': gain(ks[15], (DEPTH, D_MODEL)),
        'ffn_w_gate': nrm(ks[16], (N_DENSE, D_MODEL, D_FF), D_MODEL ** -0.5),
        'ffn_w_up': nrm(ks[17], (N_DENSE, D_MODEL, D_FF), D_MODEL ** -0.5),
        'ffn_w_down': nrm(ks[18], (N_DENSE, D_FF, D_MODEL), D_FF ** -0.5),
        'moe_router': nrm(ks[19], (N_MOE, D_MODEL, N_EXPERTS), D_MODEL ** -0.5),
        'moe_w_gate': nrm(ks[20], (N_MOE, N_EXPERTS, D_MODEL, D_FF_EXPERT), D_MODEL ** -0.5),
        'moe_w_up': nrm(ks[21], (N_MOE, N_EXPERTS, D_MODEL, D_FF_EXPERT), D_MODEL ** -0.5),
        'moe_w_down': nrm(ks[22], (N_MOE, N_EXPERTS, D_FF_EXPERT, D_MODEL), D_FF_EXPERT ** -0.5),
        'norm_final': gain(ks[23], (D_MODEL,)),
    }

def second_block(x, norm_mix, w_in, conv_a_w, conv_ssd_w, conv_ssd_b, dt_bias, a_log, d_skip,
              ssd_norm_w, conv_conf_w, conv_conf_b, conf_ln_g, conf_ln_b, w_out, norm_ffn,
              ffn_w_gate, ffn_w_up, ffn_w_down, moe_router, moe_w_gate, moe_w_up, moe_w_down,
              norm_final):
    for i in range(DEPTH):
        h = rmsnorm(x, norm_mix[i])
        x = x + hybrid_mixer(h, w_in[i], conv_a_w[i], conv_ssd_w[i], conv_ssd_b[i], dt_bias[i],
                             a_log[i], d_skip[i], ssd_norm_w[i], conv_conf_w[i], conv_conf_b[i],
                             conf_ln_g[i], conf_ln_b[i], w_out[i])
        h = rmsnorm(x, norm_ffn[i])
        j = i // 2
        if i % 2 == 0:
            x = x + swiglu(h, ffn_w_gate[j], ffn_w_up[j], ffn_w_down[j])
        else:
            x = x + moe_swiglu(h, moe_router[j], moe_w_gate[j], moe_w_up[j], moe_w_down[j])
    return rmsnorm(x, norm_final)


def setup_inputs(seed=0):
    out = dict(first_inputs(seed))
    for name, value in second_inputs(seed + 1).items():
        if name != "x":
            out[name + "_2"] = value
    return out


def reference(
    x, p, w_in, mla_q_norm_g, mla_kv_norm_g, mla_w_uq, mla_w_ukv, diff_lambda, diff_subln_g,
    w_branch_a, w_branch_b, w_branch_c, w_merge, b_merge, w_out, ln_g, ln_b, w_ple_gate, w_ple,
    norm_mix_2, w_in_2, conv_a_w_2, conv_ssd_w_2, conv_ssd_b_2, dt_bias_2, a_log_2, d_skip_2,
    ssd_norm_w_2, conv_conf_w_2, conv_conf_b_2, conf_ln_g_2, conf_ln_b_2, w_out_2, norm_ffn_2,
    ffn_w_gate_2, ffn_w_up_2, ffn_w_down_2, moe_router_2, moe_w_gate_2, moe_w_up_2,
    moe_w_down_2, norm_final_2,
):
    x = first_block(
        x, p, w_in, mla_q_norm_g, mla_kv_norm_g, mla_w_uq, mla_w_ukv, diff_lambda, diff_subln_g,
        w_branch_a, w_branch_b, w_branch_c, w_merge, b_merge, w_out, ln_g, ln_b, w_ple_gate,
        w_ple,
    )
    return second_block(
        x, norm_mix_2, w_in_2, conv_a_w_2, conv_ssd_w_2, conv_ssd_b_2, dt_bias_2, a_log_2,
        d_skip_2, ssd_norm_w_2, conv_conf_w_2, conv_conf_b_2, conf_ln_g_2, conf_ln_b_2, w_out_2,
        norm_ffn_2, ffn_w_gate_2, ffn_w_up_2, ffn_w_down_2, moe_router_2, moe_w_gate_2,
        moe_w_up_2, moe_w_down_2, norm_final_2,
    )


_drawn_inputs = setup_inputs


def setup_inputs(seed=0):
    import zlib

    import numpy as np

    out = dict(_drawn_inputs(seed))
    spreads = {}
    factors = {'mla_q_norm_g': 8.0,
     'mla_kv_norm_g': 8.0,
     'diff_lambda': 2.862,
     'diff_subln_g': 8.0,
     'b_merge': 8.0,
     'conf_ln_g_2': 4.339,
     'conf_ln_b_2': 5.741,
     'norm_final_2': 8.107,
     'conv_ssd_b_2': 3.349,
     'ssd_norm_w_2': 3.432,
     'norm_ffn_2': 2.703}
    for name, (base, spread) in spreads.items():
        noise = np.random.default_rng([zlib.crc32(name.encode()), seed]).standard_normal(out[name].shape)
        drawn = base * np.exp(spread * noise) if base else spread * noise
        out[name] = __import__('jax').numpy.asarray(drawn.astype(out[name].dtype))
    for name, factor in factors.items():
        out[name] = (out[name] * factor).astype(out[name].dtype)
    return out
```

```python
from contextlib import ExitStack

import numpy as np

import concourse.bass as bass
from concourse import mybir

F32 = mybir.dt.float32
ACT = mybir.ActivationFunctionType
ALU = mybir.AluOpType
AX = mybir.AxisListType

P = 128
S = 256
TT = S // P
D = 1024
DT = D // P
LAYERS = 2
HEADS = 8
HD = 64
ROPE = 32
MLA_D = HD + ROPE
DIFF_HEADS = 4
ALPHA = (2 * LAYERS) ** 0.25
Q_LORA, KV_LORA, PLE = 384, 256, 256
FF = 2816
EXPERTS = 8
FFE = 3584
CONF_TAPS, SSD_TAPS, A_TAPS = 31, 4, 3
RING = 6
SLOT = 2048
BANKS = 4
NEG = -1e30

_n = HEADS + DIFF_HEADS
_slopes = [2.0 ** (-8.0 * (i + 1) / _n) for i in range(_n)]
_diff_at = [i * (_n // DIFF_HEADS) for i in range(DIFF_HEADS)]
DIFF_SLOPES = [_slopes[i] for i in _diff_at]
MOBA_SLOPES = [s for i, s in enumerate(_slopes) if i not in _diff_at]

C_IDENT, C_DIST, C_MASK, C_TRI, C_MASKT, C_ROT, C_COS, C_SIN, C_LAM, C_DESC, C_END = (
    int(v) for v in np.cumsum([0, P, S, S, S, S, MLA_D, S, S, 4, 8]))


P_GQ, P_GKV, P_SUB, P_BM, P_LG, P_LB, P_LAM, P_LQK, P1_END = (
    int(v) for v in np.cumsum([0, 3, 2, 1, 24, 8, 8, 2, 4 * HD]))
Q_NM, Q_CA, Q_CS, Q_CSB, Q_DS, Q_NW, Q_CC, Q_CCB, Q_CG, Q_CB, Q_NF, Q_NL, Q_BC, P2_END = (
    int(v) for v in np.cumsum([0, 8, 2 * A_TAPS, 8 * SSD_TAPS, 8, 4, 4, 2 * CONF_TAPS, 2, 2, 2, 8, 8, 16]))


def by_feature(v):
    if v.ndim == 2:
        v = v[:, None, :]
    layers, taps, n = v.shape
    return v.reshape(layers, taps, n // P, P).transpose(0, 3, 2, 1).reshape(layers, P, -1)


def on_all(v):
    return np.broadcast_to(v[:, None, :], (v.shape[0], P, v.shape[1]))


def constants():
    c = np.zeros((P, C_END), np.float32)
    p, k = np.arange(P)[:, None], np.arange(P)[None, :]
    c[:, C_IDENT:C_IDENT + P] = p == k
    c[:, C_DIST:C_DIST + P] = k - P - p
    c[:, C_DIST + P:C_DIST + S] = np.where(k <= p, k - p, NEG)
    c[:, C_MASK + P:C_MASK + S] = np.where(k <= p, 0.0, NEG)
    c[:, C_TRI:C_TRI + P] = p <= k
    c[:, C_TRI + P:C_TRI + S] = 1.0
    c[:, C_MASKT:C_MASKT + P] = np.where(k >= p, 0.0, NEG)
    half = ROPE // 2
    for m in range(ROPE):
        if m < half:
            c[HD + m + half, C_ROT + HD + m] = -1.0
        else:
            c[HD + m - half, C_ROT + HD + m] = 1.0
    freqs = np.float32(10000.0) ** (-np.arange(0, ROPE, 2, dtype=np.float32) / np.float32(ROPE))
    ang = np.arange(S, dtype=np.float32)[None, :] * freqs[:, None].astype(np.float32)
    c[HD:MLA_D, C_COS:C_COS + S] = np.tile(np.cos(ang), (2, 1))
    c[HD:MLA_D, C_SIN:C_SIN + S] = np.tile(np.sin(ang), (2, 1))
    for li in range(LAYERS):
        lam = 0.8 - 0.6 * np.exp(-0.3 * li)
        c[:, C_LAM + 2 * li] = lam
        c[:, C_LAM + 2 * li + 1] = 1.0 - lam
    c[:, C_DESC:C_DESC + 8] = np.arange(8, 0, -1)
    return c


class Signal:

    def __init__(self, handle, per=0):
        self.h, self.per = handle, per

    def at(self, turn, n):
        return turn * self.per + n


class Groups:

    def __init__(self, table, full, drained_a, drained_v, turns_before=0):
        self.names = [n for n, _ in table]
        self.owner = [o for _, o in table]
        assert len(set(self.names)) == len(self.names)
        self.full, self.drained = full, {"a": drained_a, "v": drained_v}

    def index(self, name):
        return self.names.index(name)

    def nth(self, g):
        return sum(o == self.owner[g] for o in self.owner[:g + 1])

    def count(self, owner):
        return sum(o == owner for o in self.owner)

    def wait_full(self, eng, turn, name):
        eng.wait_ge(self.full.h, self.full.at(turn, self.index(name) + 1))
        return self.index(name) % BANKS

    def drained_by(self, name):
        return self.drained[self.owner[self.index(name)]].h

    def wait_drained(self, eng, turn, name):
        g = self.index(name)
        s = self.drained[self.owner[g]]
        eng.wait_ge(s.h, s.at(turn, self.nth(g)))

    def wait_bank(self, eng, turn, name):
        g = self.index(name)
        if g >= BANKS:
            self.wait_drained(eng, turn, self.names[g - BANKS])
        return g % BANKS


BATCHES = [("moba", 0), ("moba", 1), ("diff", 0), ("diff", 1), ("mla", 0), ("mla", 1)]

ORDER1 = [
    ("aq0", "a"), ("aq1", "a"), ("ak0", "v"), ("ak1", "v"), ("av0", "a"), ("av1", "a"), ("A", 0),
    ("dq0", "a"), ("dq1", "a"), ("B", 0), ("dk0", "v"), ("dk1", "v"), ("V", 0), ("A", 1),
    ("dv0", "a"), ("dv1", "a"), ("B", 1), ("mc0", "a"), ("mc1", "a"), ("V", 1), ("A", 2),
    ("mc2", "a"), ("ms", "v"), ("B", 2), ("pt", "a"), ("pl0", "a"), ("pl1", "a"), ("pl2", "a"),
    ("pl3", "a"), ("V", 2), ("A", 3), ("uq0", "a"), ("uq1", "a"), ("uq2", "a"), ("uq3", "a"),
    ("rk", "v"), ("rq0", "v"), ("rq1", "v"), ("kn0", "a"), ("kn1", "a"), ("kn2", "a"),
    ("kn3", "a"), ("rq2", "v"), ("rq3", "v"), ("mv0", "v"), ("mv1", "v"), ("B", 3),
    ("az0", "v"), ("az1", "v"), ("V", 3), ("A", 4), ("bz0", "v"), ("bz1", "v"), ("B", 4),
    ("cz0", "v"), ("cz1", "v"), ("V", 4), ("A", 5), ("dn0", "v"), ("dn1", "v"),
    ("mg0", "a"), ("mg1", "a"), ("B", 5), ("mg2", "a"), ("mg3", "a"), ("V", 5),
] + [(f"mg{j}", "a") for j in range(4, 12)] + [
    (f"b{c}{j}", "v") for c in "abc" for j in range(4)] + [
    (f"ou{j}", "a") for j in range(4)] + [(f"pg{j}", "a") for j in range(4)] + [
    ("lm", "v"), ("lv", "v")]
STEPS = ("A", "B", "V")

UNITS1 = (
    [("w_in", c, 256, 8) for c in range(0, 1536, 256)]
    + [("w_in", c, 256, 8) for c in range(3232, 3232 + 1536, 256)]
    + [("w_in", 2048, 256, 8), ("w_in", 2304, 256, 8), ("w_in", 2560, 160, 8)]
    + [("p", 0, 256, 2), ("w_ple", 0, 1024, 2)]
    + [("w_uq", c, 192, 3) for c in range(0, 768, 192)] + [("w_ukv", 0, 1024, 2)]
    + [("w_in", c, 256, 8) for c in (1536, 1792, 2720, 2976, 4768, 5024)]
    + [("w_merge", c, 256, 8) for c in range(0, 3072, 256)]
    + [(w, c, 512, 4) for w in ("w_a", "w_b", "w_c") for c in (0, 512)]
    + [("w_out", c, 256, 8) for c in range(0, 1024, 256)]
    + [("w_pg", c, 256, 8) for c in range(0, 1024, 256)])
assert len(UNITS1) % RING == 0

ORDER2 = ([("ms", "v"), ("gg", "a"), ("gv", "v"), ("ac", "a"), ("ax", "v")]
          + [(f"xb{j}", "a") for j in range(4)]
          + [("dt", "v"), ("ab", "v"), ("z0", "v"), ("z1", "v"), ("acs", "v")]
          + [(f"acb{j}", "v") for j in range(4)]
          + [("xt0", "v"), ("xt1", "v"), ("cb0", "a"), ("cb1", "a"), ("cm", "v"), ("cv", "v"),
             ("ys0", "v"), ("ys1", "v"), ("gn", "v")]
          + [(f"wo{j}", "v") for j in range(4)])


def build_kernel(nc, a, out):
    ctx = ExitStack()
    with ctx:
        def sb(name, shape, stack=ctx):
            return stack.enter_context(nc.sbuf_tensor(name, shape, F32))

        def sem(name):
            return ctx.enter_context(nc.semaphore(name))

        def signal(name, per=0):
            return Signal(sem(name), per)

        bank = [ctx.enter_context(nc.psum_tensor(f"bank{i}", [P, 512], F32)) for i in range(8)]
        ring = sb("ring", [P, RING, SLOT])
        cst = sb("cst", [P, C_END])
        xT = sb("xT", [P, DT, S])
        sq = sb("sq", [P, DT, S])
        ones = sb("ones", [P, 4, P])
        zeros = ctx.enter_context(nc.sbuf_tensor("zeros", [P, 512], mybir.dt.bfloat16))
        ident = cst[:, C_IDENT:C_IDENT + P]
        ONES = {D: ones[:, 0], Q_LORA: ones[:, 1], KV_LORA: ones[:, 2], P: ones[:, 3]}

        m1 = ExitStack()
        aqk = sb("aqk", [P, 8, S], m1)
        dqk = sb("dqk", [P, 8, S], m1)
        av = sb("av", [P, TT, 512], m1)
        dv = sb("dv", [P, TT, 512], m1)
        cq = sb("cq", [P, 5, S], m1)
        cn = sb("cn", [P, 5, S], m1)
        kr = sb("kr", [P, S], m1)
        qb = sb("qb", [P, HEADS, S], m1)
        kb = sb("kb", [P, HEADS, S], m1)
        mv = sb("mv", [P, TT, 512], m1)
        rot = sb("rot", [P, 2, 512], m1)
        zs = sb("zs", [P, 12, S], m1)
        gates = sb("gates", [P, 24, S], m1)
        y = sb("y", [P, 12, S], m1)
        sc = sb("sc", [P, 4, 384], m1)
        pT = sb("pT", [P, 4, 384], m1)
        peT = sb("peT", [P, 2, S], m1)
        tmp = sb("tmp", [P, 2, 512], m1)
        rstd = sb("rstd", [P, 4, S], m1)
        nmax = sb("nmax", [P, 8], m1)
        psum_ = sb("sums", [P, 8], m1)
        pinv = sb("pinv", [P, 8], m1)
        lam_p = sb("lam_p", [P, 2, HD], m1)
        lam = sb("lam", [P, 4], m1)
        par = sb("par", [P, P1_END], m1)
        par2 = sb("par2", [P, 32], m1)
        pleT, merged = aqk, dqk
        r1, ou = qb, kb
        m1.close()

        m2 = ExitStack()
        h = sb("h", [P, DT, S], m2)
        gp = sb("gp", [P, 2, CONF_TAPS - 1 + S], m2)
        gc = sb("gc", [P, 2, S], m2)
        ap_ = sb("ap_", [P, 2, A_TAPS - 1 + S], m2)
        acs_b = sb("ac_sb", [P, 2, S], m2)
        cat = sb("cat", [P, DT, S], m2)
        ac_y = sb("ac_y", [P, 2, S], m2)
        xp = sb("xp", [P, 8, SSD_TAPS - 1 + S], m2)
        xc = sb("xc", [P, 8, S], m2)
        sz = sb("sz", [P, 4, S], m2)
        dtt = sb("dtt", [P, 8, TT * 8], m2)
        dtb = sb("dtb", [P, TT, 8, P], m2)
        acs = sb("acs", [P, TT, 8], m2)
        em = sb("em", [P, 8, 384], m2)
        cbm = sb("cbm", [P, 2, 384], m2)
        xdt = sb("xdt", [P, TT, 512], m2)
        rs2 = sb("rs2", [P, 4, S], m2)
        xth = sb("xth", [P, 8, S], m2)
        yt = sb("yt", [P, 2, S], m2)
        t2 = sb("t2", [P, 2, 512], m2)
        q2 = sb("q2", [P, P2_END], m2)
        bc = q2[:, Q_BC:Q_BC + 16]
        hf = sb("hf", [P, 2, 2, S], m2)
        ta = sb("ta", [P, 2, 2, S], m2)
        tb = sb("tb", [P, 2, 2, S], m2)
        lg = sb("lg", [P, TT, 8, 8], m2)
        gmat = sb("gmat", [P, TT, 8], m2)
        gmb = sb("gmb", [P, TT, 8, P], m2)
        gbc = sb("gbc", [P, 8, S], m2)
        m2.close()
        landed = [signal(f"w_landed{i}", 16 * len(UNITS1) // RING) for i in range(RING)]
        w_free = signal("w_slot_free", len(UNITS1))
        first_units = len(UNITS1) * LAYERS

        def unit_wait(eng, n):
            eng.wait_ge(landed[n % RING].h, 16 * (n // RING + 1))

        cst_in, x_in = sem("constants_landed"), sem("x_landed")
        ones_set = sem("ones_set")
        x0_full, x0_taken = sem("x_transposed"), sem("x_taken")
        x_ready = signal("x_ready", DT)
        par_in = signal("params_landed", 16)
        full = signal("group_full", sum(n not in STEPS for n, _ in ORDER1))
        dr_a = signal("drained_by_scalar", sum(o == "a" for _, o in ORDER1))
        dr_v = signal("drained_by_vector", sum(o == "v" for _, o in ORDER1))
        G1 = Groups([x for x in ORDER1 if x[0] not in STEPS], full, dr_a, dr_v)
        nb = len(BATCHES)
        sc_full, sc_max, p_exp, p_ready, p_turned, pT_ready, pv_full, y_ready = (
            signal(n, nb) for n in ("scores_full", "scores_max", "probs_exp", "probs_ready",
                                    "probs_turned", "probsT_ready", "pv_full", "y_ready"))
        z_tanh = signal("z_tanh", 6)
        ms_std, ms_done = (signal(n, 1) for n in ("latent_std", "latent_normed"))
        dn_sq, dn_std = (signal(n, 1) for n in ("diff_squares", "diff_std"))
        gated = signal("branch_gated", 3)
        dt_neg, dt_w = signal("dt_neg_abs", 1), signal("dt_exp_plus_1", 1)
        lamp, lame = signal("lambda_sums", 1), signal("lambda_exp", 1)
        halfb = signal("half_bias", 1)
        rope_q, kroped, kall = signal("q_roped", 4), signal("k_roped", 1), signal("k_rope_spread", 1)
        mgd = signal("merged", 8)
        r_ready = signal("r_ready", 4)
        r2_ready = signal("r_gated", 4)
        ln_sq, ln_std, normed = (signal(n, k) for n, k in (
            ("ln_squares", 1), ("ln_std", 1), ("ln_scaled", DT)))
        vlink = signal("vector_step", 34)

        def unit_view(slot, cols, k):
            return ring[:, slot, 0:k * cols].rearrange("p (k n) -> p k n", n=cols)

        def views(b, n=2):
            return bank[b][:, :].rearrange("p (t s) -> p t s", t=n)

        units2 = []
        FD, FJ = FF // S, FFE // S
        for i in range(LAYERS):
            units2 += [("w_in_2", i, c, 256, 8) for c in (2568, 2312, 256, 512)]
            units2 += [("w_in_2", i, c, 256, 8) for c in range(1280, 2304, 256)]
            units2 += [("w_in_2", i, 2304, 8, 8), ("w_in_2", i, 0, 256, 8)]
            units2 += [("w_in_2", i, c, 256, 8) for c in (768, 1024)]
            units2 += [("w_out_2", i, c, 256, 8) for c in range(0, 1024, 256)]
            if i == 0:
                for steps in [(j, j + 1) for j in range(0, FD - 1, 2)] + [(FD - 1,)]:
                    for j in steps:
                        units2 += [("ffn_w_gate_2", 0, j * S, 256, 8), ("ffn_w_up_2", 0, j * S, 256, 8)]
                    units2 += [("ffn_w_down_2", 0, j * S, 1024, 2) for j in steps]
            else:
                units2 += [("moe_router_2", 0, 0, 8, 8)]
        assert len(units2) % RING == 0
        moe_base = first_units + len(units2)
        U_MOE = 3 * FJ
        ffn_at = 16

        STEP_UNITS = [("moe_w_gate_2", 0), ("moe_w_up_2", 0), ("moe_w_gate_2", 1), ("moe_w_up_2", 1),
                      ("moe_w_down_2", 0), ("moe_w_down_2", 1)]

        def source(name, layer, c0, cols, k):
            if name in ("ffn_w_down_2",):
                return a[name][layer, c0:c0 + k * P, :].rearrange("(k p) n -> p k n", p=P)
            return a[name][layer, 0:k * P, c0:c0 + cols].rearrange("(k p) n -> p k n", p=P)

        block = ctx.enter_context(nc.Block())

        out_full, out_done = signal("out_rows_ready"), sem("out_written")

        @block.sync
        def _(sp):
            sp.dma_start(cst[:, :], a["cst"]).then_inc(cst_in, 16)
            sp.dma_start(sq[:, :, :].rearrange("p (t a) s -> p t (a s)", t=TT),
                         a["x"][0].rearrange("(t p) d -> p t d", p=P)).then_inc(x_in, 16)
            with sp.Fori(0, LAYERS) as layer:
                for u, (name, c0, cols, k) in enumerate(UNITS1):
                    sp.wait_ge(w_free.h, w_free.at(layer, u + 1))
                    src = {"p": "p", "w_a": "w_branch_a", "w_b": "w_branch_b", "w_c": "w_branch_c",
                           "w_pg": "w_ple_gate", "w_uq": "mla_w_uq", "w_ukv": "mla_w_ukv"}.get(name, name)
                    dram = a[src][bass.ds(layer, 1), 0:k * P, c0:c0 + cols] if name != "p" else \
                        a["p"][bass.ds(layer, 1), 0, :, :]
                    dram = dram.rearrange("o (k p) n -> p (o k) n", p=P)
                    sp.dma_start(unit_view(u % RING, cols, k), dram).then_inc(landed[u % RING].h, 16)
            for u, unit in enumerate(units2):
                sp.wait_ge(w_free.h, first_units + u + 1)
                sp.dma_start(unit_view(u % RING, unit[3], unit[4]), source(*unit)).then_inc(
                    landed[u % RING].h, 16)
            with sp.Fori(0, EXPERTS) as e, sp.Fori(0, FJ // 2) as jj:
                for u in range(RING):
                    name, half = STEP_UNITS[u]
                    sp.wait_ge(w_free.h, e * U_MOE + jj * RING + (moe_base + u + 1))
                    rows, j = a[name][0], jj * (2 * S) + half * S
                    if u >= 4:
                        dram = rows[bass.ds(e, 1), bass.ds(j, S), :]
                    else:
                        dram = rows[bass.ds(e, 1), :, bass.ds(j, S)]
                    sp.dma_start(unit_view(u, *((1024, 2) if u >= 4 else (256, 8))),
                                 dram.rearrange("o (k p) n -> p (o k) n", p=P)).then_inc(landed[u].h, 16)
            for t in range(TT):
                sp.wait_ge(out_full.h, 2 * (t + 1))
                sp.dma_start(out[0, t * P:(t + 1) * P, :],
                             h[:, :, :].rearrange("p (t a) s -> p t (a s)", t=TT)[:, t, :]).then_inc(out_done, 16)
            sp.wait_ge(out_done, 16 * TT)

        full2 = signal("group2_full", len(ORDER2))
        d2a = signal("drained2_by_scalar", sum(o == "a" for _, o in ORDER2))
        d2v = signal("drained2_by_vector", sum(o == "v" for _, o in ORDER2))
        G2 = Groups(ORDER2, full2, d2a, d2v)
        par2_in = signal("mixer_params_landed", 16)
        sq_ready, std_ready = signal("norm_squares", 1), signal("norm_std", 1)
        h_ready = signal("h_ready", 1)
        xc_half, xc_t, xc_done = signal("xbc_conv", 4), signal("xbc_tanh", 4), signal("xbc_done", 4)
        z_t = signal("gate_z_tanh", 2)
        dte, dtl, dta = signal("dt_exp", 1), signal("dt_ln", 1), signal("dt_done", 1)
        dtb_r = signal("dt_spread", 1)
        em_exp, em_r = signal("decay_exp", 4), signal("decay_cb", 4)
        cf_sum, cf_sq, cf_std, cf_half, cf_t, cf_done = (signal(n, 1) for n in (
            "conf_conv", "conf_squares", "conf_std", "conf_scaled", "conf_tanh", "conf_done"))
        yz_r, yz_sq, yz_std, yn_done = (signal(n, 1) for n in (
            "yz_ready", "yz_squares", "yz_std", "yn_done"))
        x_up = signal("x_updated")
        pad0 = sem("pads_cleared")
        b1_end = (LAYERS + 1) * DT
        ff_full, ff_t, ff_g, ff_h, ff_down = (signal(n) for n in (
            "ffn_full", "ffn_tanh", "ffn_gate_done", "ffn_h_ready", "ffn_down_done"))
        mo_full, mo_t, mo_g, mo_p, mo_h, mo_down = (signal(n) for n in (
            "expert_full", "expert_tanh", "expert_gated", "expert_product", "expert_h_ready", "expert_down_done"))
        rt_full, rt_top, rt_exp, rt_g, rt_b, rt_bfull, rt_bc = (signal(n) for n in (
            "router_full", "router_top", "router_exp", "router_gates", "gates_spread",
            "gates_full", "gates_ready"))
        nrm = {n: signal("final_" + n) for n in ("sq", "full", "eps", "std", "rstd", "h")}
        fin_full = signal("result_full")

        @block.tensor
        def _(pe):
            owed = [0]

            def mm(dst, w, x, start, stop, share=False):
                ins = pe.matmul(dst, w, x, start=start, stop=stop, skip_group_check=share)
                if owed[0]:
                    ins.then_inc(w_free.h, 1)
                    owed[0] = 0
                return ins

            pe.wait_ge(cst_in, 16)
            pe.wait_ge(x_in, 16)
            xtok = sq[:, :, :].rearrange("p (t a) s -> p t (a s)", t=TT)
            for b in range(4):
                for t in range(2):
                    for tt in range(TT):
                        ins = pe.transpose(views(b)[:, t, tt * P:(tt + 1) * P],
                                           xtok[:, tt, (2 * b + t) * P:(2 * b + t + 1) * P], ident)
                ins.then_inc(x0_full, 1)
            pe.wait_ge(ones_set, 6)

            def layer_body(layer):
                unit = [0]

                def take(cols, k):
                    u = unit[0]
                    unit[0] += 1
                    owed[0] = int(u > 0)
                    s = landed[u % RING]
                    pe.wait_ge(s.h, s.at(layer, 16 * (u // RING + 1)))
                    return unit_view(u % RING, cols, k)

                def begin(name):
                    return G1.wait_bank(pe, layer, name)

                def project(name, w, x, k, m=P):
                    b = begin(name)
                    for t in range(2):
                        for kk in range(k):
                            ins = mm(views(b)[0:m, t, :], w[:, kk, t * m:(t + 1) * m], x[:, kk, :],
                                     kk == 0, kk == k - 1)
                    ins.then_inc(full.h, 1)

                def values(name, w, x, k):
                    b = begin(name)
                    for t in range(TT):
                        for kk in range(k):
                            ins = mm(views(b)[:, t, :], x[:, kk, t * P:(t + 1) * P], w[:, kk, :],
                                     kk == 0, kk == k - 1)
                    ins.then_inc(full.h, 1)

                def scores(n):
                    kind, b = BATCHES[n]
                    if kind == "moba":
                        G1.wait_drained(pe, layer, "aq1")
                        G1.wait_drained(pe, layer, "ak1")
                    elif kind == "diff":
                        G1.wait_drained(pe, layer, "dq1")
                        G1.wait_drained(pe, layer, "dk1")
                    else:
                        pe.wait_ge(rope_q.h, rope_q.at(layer, 4))
                        pe.wait_ge(kall.h, kall.at(layer, 1))
                        G1.wait_drained(pe, layer, "kn3")
                    if n >= 1:
                        pe.wait_ge(pT_ready.h, pT_ready.at(layer, n))

                    def qk(m):
                        if kind == "mla":
                            return qb[0:MLA_D, 4 * b + m, :], kb[0:MLA_D, 4 * b + m, :]
                        q = aqk if kind == "moba" else dqk
                        part = slice(HD * (m % 2), HD * (m % 2) + HD)
                        return q[part, 2 * b + m // 2, :], q[part, 4 + 2 * b + m // 2, :]

                    for m in range(4):
                        q, k = qk(m)
                        mm(bank[4 + m % 2][:, (m // 2) * S:(m // 2) * S + S], q[:, P:S], k, True, True)
                    for m in (0, 2, 1, 3):
                        q, k = qk(m)
                        if m == 1 and n >= 1:
                            pe.wait_ge(y_ready.h, y_ready.at(layer, n))
                        ins = mm(bank[6 + m % 2][:, (m // 2) * P:(m // 2) * P + P], q[:, 0:P], k[:, 0:P],
                                 True, True)
                    ins.then_inc(sc_full.h, 1)

                def turn(n):
                    pe.wait_ge(p_ready.h, p_ready.at(layer, n + 1))
                    maps = 2 if BATCHES[n][0] == "diff" else 4
                    for b, c0 in ((4, 256), (5, 0), (6, 128)):
                        for m in range(maps):
                            ins = pe.transpose(bank[b][:, m * P:(m + 1) * P], sc[:, m, c0:c0 + P], ident)
                    ins.then_inc(p_turned.h, 1)

                def pv(n):
                    kind, b = BATCHES[n]
                    pe.wait_ge(pT_ready.h, pT_ready.at(layer, n + 1))
                    if kind == "mla":
                        G1.wait_drained(pe, layer, "mv1")
                    else:
                        G1.wait_drained(pe, layer, "av1" if kind == "moba" else "dv1")
                    maps = 2 if kind == "diff" else 4
                    for m in range(maps):
                        if kind == "diff":
                            v = dv[:, :, (2 * b + m) * P:(2 * b + m + 1) * P]
                            dst = views(7)[:, m, :]
                        else:
                            v = (av if kind == "moba" else mv)[:, :, (4 * b + m) * HD:(4 * b + m + 1) * HD]
                            dst = views(7)[HD * (m % 2):HD * (m % 2) + HD, m // 2, :]
                        mm(dst, v[:, 0, :], pT[:, m, 0:S], True, False)
                        ins = mm(dst[:, P:S], v[:, 1, :], pT[:, m, S:S + P], False, True)
                    ins.then_inc(pv_full.h, 1)

                pe.wait_ge(x_ready.h, x_ready.at(layer, DT))
                for name, who in ORDER1:
                    if name == "A":
                        scores(who)
                    elif name == "B":
                        turn(who)
                    elif name == "V":
                        pv(who)
                    elif name in ("av0", "av1", "dv0", "dv1"):
                        values(name, take(256, 8), xT, 8)
                    elif name == "mc2":
                        w = take(160, 8)
                        b = begin(name)
                        for kk in range(8):
                            mm(views(b)[:, 0, :], w[:, kk, 0:P], xT[:, kk, :], kk == 0, kk == 7)
                        for kk in range(8):
                            ins = mm(views(b)[HD:MLA_D, 1, :], w[:, kk, P:P + ROPE], xT[:, kk, :],
                                     kk == 0, kk == 7)
                        ins.then_inc(full.h, 1)
                    elif name == "ms":
                        G1.wait_drained(pe, layer, "mc2")
                        b = begin(name)
                        for kk in range(3):
                            mm(views(b)[:, 0, :], ONES[Q_LORA], sq[:, kk, :], kk == 0, kk == 2)
                        for kk in range(2):
                            ins = mm(views(b)[:, 1, :], ONES[KV_LORA], sq[:, 3 + kk, :], kk == 0, kk == 1)
                        ins.then_inc(full.h, 1)
                    elif name == "pt":
                        w = take(256, 2)
                        b = begin(name)
                        for kk in range(2):
                            for t in range(TT):
                                ins = pe.transpose(views(b)[:, kk, t * P:(t + 1) * P],
                                                   w[:, t, kk * P:(kk + 1) * P], ident)
                        ins.then_inc(full.h, 1)
                    elif name[:2] == "pl":
                        j = int(name[2])
                        if j == 0:
                            w = take(1024, 2)
                            G1.wait_drained(pe, layer, "pt")
                        project(name, w[:, :, 256 * j:256 * j + 256], peT, 2)
                    elif name[:2] == "uq":
                        if name == "uq0":
                            pe.wait_ge(ms_done.h, ms_done.at(layer, 1))
                        project(name, take(192, 3), cn, 3, m=MLA_D)
                    elif name[:1] == "r":
                        if name == "rk":
                            G1.wait_drained(pe, layer, "mc2")
                            src, width = kr[0:MLA_D, :], S
                        else:
                            j = int(name[2])
                            G1.wait_drained(pe, layer, f"uq{j}")
                            src, width = qb[0:MLA_D, 2 * j:2 * j + 2, :], 2 * S
                        b = begin(name)
                        mm(bank[b][0:MLA_D, 0:width], cst[0:MLA_D, C_ROT:C_ROT + MLA_D], src,
                           True, True).then_inc(full.h, 1)
                    elif name[:2] == "kn":
                        j = int(name[2])
                        if j == 0:
                            w = take(1024, 2)
                        b = begin(name)
                        for t in range(2):
                            for kk in range(2):
                                c0 = (2 * j + t) * 2 * HD
                                ins = mm(views(b)[0:HD, t, :], w[:, kk, c0:c0 + HD], cn[:, 3 + kk, :],
                                         kk == 0, kk == 1)
                        ins.then_inc(full.h, 1)
                    elif name[:2] == "mv":
                        t = int(name[2])
                        b = begin(name)
                        for kk in range(2):
                            wv = w[:, kk, :].rearrange("p (h d) -> p h d", d=2 * HD)[:, :, HD:2 * HD]
                            ins = mm(bank[b][:, :].rearrange("p (h d) -> p h d", d=HD),
                                     cn[:, 3 + kk, t * P:(t + 1) * P], wv, kk == 0, kk == 1)
                        ins.then_inc(full.h, 1)
                    elif name[:2] == "dn":
                        j = int(name[2])
                        if j == 0:
                            pe.wait_ge(dn_sq.h, dn_sq.at(layer, 1))
                        b = begin(name)
                        mm(bank[b][:, :], ONES[P], sq[:, 2 * j:2 * j + 2, :], True, True).then_inc(full.h, 1)
                    elif name[:2] in ("ba", "bb", "bc"):
                        j, c = int(name[2]), "abc".index(name[1])
                        if j % 2 == 0:
                            w = take(512, 4)
                        if j == 0:
                            pe.wait_ge(gated.h, gated.at(layer, {"a": 1, "c": 2, "b": 3}[name[1]]))
                        project(name, w[:, :, 256 * (j % 2):256 * (j % 2) + 256], y[:, 4 * c:4 * c + 4, :], 4)
                    elif name[:2] == "ou":
                        if name == "ou0":
                            pe.wait_ge(mgd.h, mgd.at(layer, 8))
                        project(name, take(256, 8), merged, 8)
                    elif name[:2] == "pg":
                        if name == "pg0":
                            pe.wait_ge(r_ready.h, r_ready.at(layer, 4))
                        project(name, take(256, 8), r1, 8)
                    elif name in ("lm", "lv"):
                        if name == "lm":
                            pe.wait_ge(r2_ready.h, r2_ready.at(layer, 4))
                        else:
                            pe.wait_ge(ln_sq.h, ln_sq.at(layer, 1))
                        b = begin(name)
                        owed[0] = int(name == "lm")
                        src = merged if name == "lm" else sq
                        for kk in range(DT):
                            ins = mm(views(b)[:, 0, :], ONES[D], src[:, kk, :], kk == 0, kk == DT - 1)
                        ins.then_inc(full.h, 1)
                    else:
                        project(name, take(256, 8), xT, 8)
                assert unit[0] == len(UNITS1)

            with pe.Fori(0, LAYERS) as layer:
                layer_body(layer)

            unit = [0]

            def take(cols, k):
                u = unit[0]
                unit[0] += 1
                owed[0] = int(u > 0)
                unit_wait(pe, first_units + u)
                return unit_view(u % RING, cols, k)

            def mixer(m):
                def begin(name):
                    return G2.wait_bank(pe, m, name)

                def project(name, w, x, k=DT):
                    b = begin(name)
                    for t in range(2):
                        for kk in range(k):
                            ins = mm(views(b)[:, t, :], w[:, kk, t * P:(t + 1) * P], x[:, kk, :],
                                     kk == 0, kk == k - 1)
                    ins.then_inc(full2.h, 1)

                def mean(name, src, tiles, t=0, width=D):
                    b = G2.index(name) % BANKS
                    for n, kk in enumerate(tiles):
                        ins = mm(views(b)[:, t, :], ONES[width], src[:, kk, :], n == 0, n == len(tiles) - 1)
                    return ins

                for name, _ in ORDER2:
                    if name == "ms":
                        pe.wait_ge(sq_ready.h, sq_ready.at(m, 1))
                        begin(name)
                        mean(name, sq, range(DT)).then_inc(full2.h, 1)
                        pe.wait_ge(h_ready.h, h_ready.at(m, 1))
                    elif name == "dt":
                        w = take(8, 8)
                        b = begin(name)
                        for t in range(TT):
                            for kk in range(DT):
                                ins = mm(bank[b][:, 8 * t:8 * t + 8], h[:, kk, t * P:(t + 1) * P],
                                         w[:, kk, :], kk == 0, kk == DT - 1)
                        ins.then_inc(full2.h, 1)
                    elif name == "acs":
                        pe.wait_ge(dta.h, dta.at(m, 1))
                        b = begin(name)
                        x = dtt[:, 7, :].rearrange("p (t e) -> p t e", t=TT)
                        mm(bank[b][:, 0:8], cst[:, C_TRI:C_TRI + P], x[:, 0, :], True, True)
                        mm(bank[b][:, 8:16], cst[:, C_TRI + P:C_TRI + S], x[:, 0, :], True, False)
                        mm(bank[b][:, 8:16], cst[:, C_TRI:C_TRI + P], x[:, 1, :], False, True).then_inc(
                            full2.h, 1)
                    elif name[:3] == "acb":
                        j = int(name[3])
                        if j == 0:
                            pe.wait_ge(dtb_r.h, dtb_r.at(m, 1))
                        b = begin(name)
                        for t in range(2):
                            mm(views(b)[:, t, :], dtb[:, 0, 2 * j + t, :], cst[:, C_TRI:C_TRI + S], True, False)
                            ins = mm(views(b)[:, t, P:S], dtb[:, 1, 2 * j + t, :], cst[:, C_TRI:C_TRI + P],
                                     False, True)
                        ins.then_inc(full2.h, 1)
                    elif name[:2] == "xt":
                        t = int(name[2])
                        if t == 0:
                            pe.wait_ge(xc_done.h, xc_done.at(m, 2))
                        b = begin(name)
                        for kk in range(4):
                            ins = pe.transpose(bank[b][:, kk * P:(kk + 1) * P], xc[:, kk, t * P:(t + 1) * P], ident)
                        ins.then_inc(full2.h, 1)
                    elif name[:2] == "cb":
                        g = int(name[2])
                        if g == 0:
                            pe.wait_ge(xc_done.h, xc_done.at(m, 4))
                        b = begin(name)
                        mm(bank[b][:, 0:S], xc[:, 4 + g, 0:P], xc[:, 6 + g, :], True, True)
                        mm(bank[b][:, S:S + P], xc[:, 4 + g, P:S], xc[:, 6 + g, P:S], True, True).then_inc(full2.h, 1)
                    elif name in ("cm", "cv"):
                        s = cf_sum if name == "cm" else cf_sq
                        pe.wait_ge(s.h, s.at(m, 1))
                        begin(name)
                        mean(name, gc if name == "cm" else sq, (0, 1) if name == "cm" else (4, 5), 0, KV_LORA).then_inc(full2.h, 1)
                    elif name[:2] == "ys":
                        j = int(name[2])
                        if j == 0:
                            G2.wait_drained(pe, m, "xt1")
                        pe.wait_ge(em_r.h, em_r.at(m, 2 * j + 2))
                        b = begin(name)
                        for hh in range(4 * j, 4 * j + 4):
                            dst = views(b)[HD * (hh % 2):HD * (hh % 2) + HD, (hh % 4) // 2, :]
                            mm(dst, xdt[:, 0, hh * HD:(hh + 1) * HD], em[:, hh, 0:S], True, False)
                            ins = mm(dst[:, P:S], xdt[:, 1, hh * HD:(hh + 1) * HD], em[:, hh, S:S + P], False, True)
                        ins.then_inc(full2.h, 1)
                    elif name == "gn":
                        pe.wait_ge(yz_sq.h, yz_sq.at(m, 1))
                        begin(name)
                        mean(name, sq, (0, 1), 0, KV_LORA)
                        mean(name, sq, (2, 3), 1, KV_LORA).then_inc(full2.h, 1)
                    elif name[:2] == "wo":
                        if name == "wo0":
                            G2.wait_drained(pe, m, "ab")
                            pe.wait_ge(yn_done.h, yn_done.at(m, 1))
                            pe.wait_ge(cf_done.h, cf_done.at(m, 1))
                        project(name, take(256, 8), cat)
                    else:
                        project(name, take(256, 8), h)

            def norm(n):
                pe.wait_ge(nrm["sq"].h, n)
                for kk in range(DT):
                    ins = mm(views(0)[:, 0, :], ONES[D], sq[:, kk, :], kk == 0, kk == DT - 1)
                ins.then_inc(nrm["full"].h, 1)
                pe.wait_ge(nrm["h"].h, n)

            def up(w, b, count):
                for t in range(2):
                    for kk in range(DT):
                        ins = mm(views(b)[:, t, :], w[:, kk, t * P:(t + 1) * P], h[:, kk, :],
                                 kk == 0, kk == DT - 1)
                ins.then_inc(count.h, 1)

            def down(w, x):
                for kk in range(2):
                    for t in range(DT):
                        ins = mm(views(4 + t // 2)[:, t % 2, :], w[:, kk, t * P:(t + 1) * P], x[:, kk, :],
                                 False, False, share=True)
                return ins

            def clear_sums():
                for b in range(4, 8):
                    pe.matmul(bank[b][:, :], zeros[:, 0:P], zeros[:, :], start=True, stop=True)

            mixer(0)
            norm(1)
            clear_sums()
            n0 = first_units + ffn_at
            with pe.Fori(0, FD // 2) as jj:
                for u in range(RING):
                    s = landed[(n0 + u) % RING]
                    owed[0] = 1
                    pe.wait_ge(s.h, jj * 16 + 16 * ((n0 + u) // RING + 1))
                    w = unit_view((n0 + u) % RING, *((1024, 2) if u >= 4 else (256, 8)))
                    if u < 4:
                        up(w, u, ff_full)
                    else:
                        pe.wait_ge(ff_h.h, jj * 2 + (u - 3))
                        down(w, hf[:, u - 4]).then_inc(ff_down.h, 1)
            unit[0] = ffn_at + 3 * (FD - 1)
            up(take(256, 8), 0, ff_full)
            up(take(256, 8), 1, ff_full)
            pe.wait_ge(ff_h.h, FD)
            down(take(1024, 2), hf[:, 0]).then_inc(ff_down.h, 1)
            mixer(1)
            norm(2)
            w = take(8, 8)
            for t in range(TT):
                for kk in range(DT):
                    ins = mm(bank[1][:, 8 * t:8 * t + 8], h[:, kk, t * P:(t + 1) * P], w[:, kk, :],
                             kk == 0, kk == DT - 1)
            ins.then_inc(rt_full.h, 1)
            pe.wait_ge(rt_b.h, 1)
            for b in range(4):
                for t in range(2):
                    for tt in range(TT):
                        ins = mm(views(b)[:, t, tt * P:(tt + 1) * P], gmb[:, tt, 2 * b + t, :], ident, True, True)
                ins.then_inc(rt_bfull.h, 1)
            assert unit[0] == len(units2)
            pe.wait_ge(rt_bc.h, 4)
            clear_sums()
            with pe.Fori(0, EXPERTS) as e, pe.Fori(0, FJ // 2) as jj:
                for u in range(RING):
                    owed[0] = 1
                    pe.wait_ge(landed[u].h, e * (16 * U_MOE // RING) + jj * 16 + 16 * (moe_base // RING + 1))
                    w = unit_view(u, *((1024, 2) if u >= 4 else (256, 8)))
                    if u < 4:
                        up(w, u, mo_full)
                    else:
                        pe.wait_ge(mo_h.h, e * FJ + jj * 2 + (u - 3))
                        down(w, hf[:, u - 4]).then_inc(mo_down.h, 1)
            norm(3)
            for t in range(TT):
                for half in range(2):
                    for kk in range(4):
                        ins = pe.transpose(bank[2 * t + half][:, kk * P:(kk + 1) * P],
                                           cat[:, 4 * half + kk, t * P:(t + 1) * P], ident)
                    ins.then_inc(fin_full.h, 1)


        @block.scalar
        def _(act):
            def fn(dst, src, func, **kw):
                return nc.scalar.activation(dst, src, func, **kw)

            def copy(dst, src, scale=1.0):
                return nc.scalar.activation(dst, src, ACT.Copy, scale=scale)

            for b in range(4):
                act.wait_ge(x0_full, b + 1)
                copy(xT[:, 2 * b:2 * b + 2, :], views(b)).then_inc(x_ready.h, 2)

            def layer_body(layer):
                def drain(name, dst, scale=1.0, rows=slice(0, P)):
                    b = G1.wait_full(act, layer, name)
                    copy(dst, views(b)[rows], scale).then_inc(dr_a.h, 1)

                def exps(n):
                    act.wait_ge(sc_max.h, sc_max.at(layer, n + 1))
                    for m in range(4):
                        fn(sc[:, m, 0:S], sc[:, m, 0:S], ACT.Exp, bias=nmax[:, m:m + 1],
                           accum_out=psum_[:, m:m + 1])
                        ins = fn(sc[:, m, S:384], sc[:, m, S:384], ACT.Exp, bias=nmax[:, 4 + m:5 + m],
                                 accum_out=psum_[:, 4 + m:5 + m])
                    ins.then_inc(p_exp.h, 1)

                def take_turned(n):
                    act.wait_ge(p_turned.h, p_turned.at(layer, n + 1))
                    maps = 2 if BATCHES[n][0] == "diff" else 4
                    for i, b in enumerate((4, 5, 6)):
                        ins = copy(pT[:, 0:maps, i * P:(i + 1) * P],
                                   bank[b][:, 0:maps * P].rearrange("p (m q) -> p m q", m=maps))
                    ins.then_inc(pT_ready.h, 1)

                def take_y(n):
                    kind, b = BATCHES[n]
                    act.wait_ge(pv_full.h, pv_full.at(layer, n + 1))
                    t0 = {"moba": 0, "mla": 4, "diff": 8}[kind] + 2 * b
                    copy(y[:, t0:t0 + 2, :], views(7)).then_inc(y_ready.h, 1)

                def gate_tanh(names, first):
                    for i, name in enumerate(names):
                        b = G1.wait_full(act, layer, name)
                        if first + i >= 2:
                            G1.wait_drained(act, layer, ["az0", "az1", "bz0", "bz1", "cz0", "cz1"][first + i - 2])
                        fn(tmp[:, i, :], bank[b][:, :], ACT.Tanh, scale=0.5).then_inc(z_tanh.h, 1)

                def merge_gate(j):
                    b = G1.wait_full(act, layer, f"mg{j}")
                    for t in range(2):
                        ins = fn(gates[:, 2 * j + t, :], views(b)[:, t, :], ACT.Tanh, scale=0.5,
                                 bias=par2[:, 2 * j + t:2 * j + t + 1])
                    ins.then_inc(dr_a.h, 1)

                scale = HD ** -0.5
                drain("aq0", aqk[:, 0:2, :], scale)
                drain("aq1", aqk[:, 2:4, :], scale)
                drain("av0", av[:, :, 0:S])
                drain("av1", av[:, :, S:512])
                act.wait_ge(lamp.h, lamp.at(layer, 1))
                fn(lam[:, 0:2], lam[:, 0:2], ACT.Exp).then_inc(lame.h, 1)
                exps(0)
                drain("dq0", dqk[:, 0:2, :], scale)
                drain("dq1", dqk[:, 2:4, :], scale)
                take_turned(0)
                take_y(0)
                exps(1)
                drain("dv0", dv[:, :, 0:S])
                drain("dv1", dv[:, :, S:512])
                take_turned(1)
                for i, name in enumerate(("mc0", "mc1")):
                    b = G1.wait_full(act, layer, name)
                    copy(cq[:, 2 * i:2 * i + 2, :], views(b))
                    fn(sq[:, 2 * i:2 * i + 2, :], views(b), ACT.Square).then_inc(dr_a.h, 1)
                take_y(1)
                exps(2)
                b = G1.wait_full(act, layer, "mc2")
                copy(cq[:, 4, :], views(b)[:, 0, :])
                fn(sq[:, 4, :], views(b)[:, 0, :], ACT.Square)
                copy(kr[HD:MLA_D, :], views(b)[HD:MLA_D, 1, :]).then_inc(dr_a.h, 1)
                G1.wait_drained(act, layer, "ms")
                fn(rstd[:, 0:2, :], rstd[:, 0:2, :], ACT.Sqrt).then_inc(ms_std.h, 1)
                take_turned(2)
                drain("pt", peT[:, :, :])
                for j in range(4):
                    drain(f"pl{j}", pleT[:, 2 * j:2 * j + 2, :])
                take_y(2)
                exps(3)
                for j in range(4):
                    drain(f"uq{j}", qb[0:MLA_D, 2 * j:2 * j + 2, :], MLA_D ** -0.5, slice(0, MLA_D))
                for j in range(4):
                    drain(f"kn{j}", kb[0:HD, 2 * j:2 * j + 2, :], 1.0, slice(0, HD))
                act.wait_ge(kroped.h, kroped.at(layer, 1))
                copy(kb[HD:MLA_D, :, :], kr[HD:MLA_D, :].unsqueeze(1).broadcast_to([ROPE, HEADS, S])).then_inc(
                    kall.h, 1)
                take_turned(3)
                gate_tanh(("az0", "az1"), 0)
                take_y(3)
                act.wait_ge(y_ready.h, y_ready.at(layer, 4))
                fn(sq[:, 0:4, :], y[:, 8:12, :], ACT.Square).then_inc(dn_sq.h, 1)
                exps(4)
                gate_tanh(("bz0", "bz1"), 2)
                take_turned(4)
                gate_tanh(("cz0", "cz1"), 4)
                take_y(4)
                exps(5)
                G1.wait_drained(act, layer, "dn1")
                fn(rstd[:, :, :], rstd[:, :, :], ACT.Sqrt).then_inc(dn_std.h, 1)
                act.wait_ge(halfb.h, halfb.at(layer, 1))
                merge_gate(0)
                merge_gate(1)
                take_turned(5)
                merge_gate(2)
                merge_gate(3)
                take_y(5)
                for j in range(4, 12):
                    merge_gate(j)
                for j in range(4):
                    drain(f"ou{j}", ou[:, 2 * j:2 * j + 2, :], 0.5)
                for j in range(4):
                    b = G1.wait_full(act, layer, f"pg{j}")
                    if j >= 2:
                        act.wait_ge(r2_ready.h, r2_ready.at(layer, j - 1))
                    fn(tmp[:, j % 2, :], bank[b][:, :], ACT.Tanh, scale=0.5).then_inc(dr_a.h, 1)
                G1.wait_drained(act, layer, "lm")
                fn(sq[:, :, :], r1[:, :, :], ACT.Square).then_inc(ln_sq.h, 1)
                G1.wait_drained(act, layer, "lv")
                fn(rstd[:, 0, :], rstd[:, 0, :], ACT.Sqrt).then_inc(ln_std.h, 1)
                for t in range(DT):
                    act.wait_ge(normed.h, normed.at(layer, t + 1))
                    fn(xT[:, t, :], r1[:, t, :], ACT.Identity, bias=par[:, P_LB + t:P_LB + t + 1]).then_inc(
                        x_ready.h, 1)

            with act.Fori(0, LAYERS) as layer:
                layer_body(layer)

            def mixer(m):
                if m:
                    act.wait_ge(x_up.h, 4)
                else:
                    act.wait_ge(x_ready.h, b1_end)
                fn(sq[:, :, :], xT[:, :, :], ACT.Square).then_inc(sq_ready.h, 1)
                G2.wait_drained(act, m, "ms")
                fn(rs2[:, 0, :], rs2[:, 0, :], ACT.Sqrt).then_inc(std_ready.h, 1)
                b = G2.wait_full(act, m, "gg")
                fn(ta[:, 0], views(b), ACT.Tanh, scale=0.5).then_inc(d2a.h, 1)
                b = G2.wait_full(act, m, "ac")
                copy(acs_b[:, :, :], views(b)).then_inc(d2a.h, 1)
                act.wait_ge(pad0, 3)
                for j in range(4):
                    b = G2.wait_full(act, m, f"xb{j}")
                    copy(xp[:, 2 * j:2 * j + 2, SSD_TAPS - 1:], views(b)).then_inc(d2a.h, 1)
                    if j:
                        act.wait_ge(xc_half.h, xc_half.at(m, j))
                        fn(xth[:, 2 * j - 2:2 * j, :], xc[:, 2 * j - 2:2 * j, :], ACT.Tanh).then_inc(xc_t.h, 1)
                act.wait_ge(xc_half.h, xc_half.at(m, 4))
                fn(xth[:, 6:8, :], xc[:, 6:8, :], ACT.Tanh).then_inc(xc_t.h, 1)
                act.wait_ge(dt_neg.h, dt_neg.at(m, 1))
                act.wait_ge(par2_in.h, par2_in.at(m, par2_in.per))
                fn(bc[:, 8:16], bc[:, 8:16], ACT.Exp)
                fn(dtt[:, 2, :], dtt[:, 1, :], ACT.Exp).then_inc(dte.h, 1)
                act.wait_ge(dt_w.h, dt_w.at(m, 1))
                fn(dtt[:, 4, :], dtt[:, 3, :], ACT.Ln).then_inc(dtl.h, 1)
                for j in range(2):
                    b = G2.wait_full(act, m, f"z{j}")
                    if j == 0:
                        G2.wait_drained(act, m, "gv")
                    fn(ta[:, j], views(b), ACT.Tanh, scale=0.5).then_inc(z_t.h, 1)
                for j in range(4):
                    G2.wait_drained(act, m, f"acb{j}")
                    fn(em[:, 2 * j:2 * j + 2, :], em[:, 2 * j:2 * j + 2, :], ACT.Exp).then_inc(em_exp.h, 1)
                for g in range(2):
                    b = G2.wait_full(act, m, f"cb{g}")
                    copy(cbm[:, g, :], bank[b][:, 0:384]).then_inc(d2a.h, 1)
                G2.wait_drained(act, m, "cm")
                fn(sq[:, 4:6, :], gc[:, :, :], ACT.Square).then_inc(cf_sq.h, 1)
                G2.wait_drained(act, m, "cv")
                fn(rs2[:, 1, :], rs2[:, 1, :], ACT.Sqrt).then_inc(cf_std.h, 1)
                act.wait_ge(yz_r.h, yz_r.at(m, 1))
                fn(sq[:, 0:4, :], cat[:, 2:6, :], ACT.Square).then_inc(yz_sq.h, 1)
                G2.wait_drained(act, m, "gn")
                fn(rs2[:, 2:4, :], rs2[:, 2:4, :], ACT.Sqrt).then_inc(yz_std.h, 1)
                act.wait_ge(cf_half.h, cf_half.at(m, 1))
                fn(yt[:, :, :], gc[:, :, :], ACT.Tanh).then_inc(cf_t.h, 1)

            def norm(n):
                fn(sq[:, :, :], xT[:, :, :], ACT.Square).then_inc(nrm["sq"].h, 1)
                act.wait_ge(nrm["eps"].h, n)
                fn(rs2[:, 0, :], rs2[:, 0, :], ACT.Sqrt).then_inc(nrm["std"].h, 1)

            mixer(0)
            G2.wait_drained(act, 0, "wo3")
            norm(1)
            with act.Fori(0, FD // 2) as jj:
                for half in range(2):
                    act.wait_ge(ff_full.h, jj * 4 + (2 * half + 1))
                    fn(ta[:, half], views(2 * half), ACT.Tanh, scale=0.5).then_inc(ff_t.h, 1)
            act.wait_ge(ff_full.h, 2 * FD - 1)
            fn(ta[:, 0], views(0), ACT.Tanh, scale=0.5).then_inc(ff_t.h, 1)
            mixer(1)
            G2.wait_drained(act, 1, "wo3")
            norm(2)
            act.wait_ge(rt_top.h, 1)
            fn(lg[:, :, 6, 0:1], lg[:, :, 5, 0:1], ACT.Exp).then_inc(rt_exp.h, 1)
            for b in range(4):
                act.wait_ge(rt_bfull.h, b + 1)
                copy(gbc[:, 2 * b:2 * b + 2, :], views(b)).then_inc(rt_bc.h, 1)
            with act.Fori(0, EXPERTS) as e, act.Fori(0, FJ // 2) as jj:
                for half in range(2):
                    act.wait_ge(mo_full.h, e * (2 * FJ) + jj * 4 + (2 * half + 1))
                    fn(ta[:, half], views(2 * half), ACT.Tanh, scale=0.5).then_inc(mo_t.h, 1)
            act.wait_ge(x_up.h, 8)
            norm(3)

        @block.vector
        def _(dve):
            link_at = [0, 0]

            def tt_(dst, x, z, op):
                return nc.vector.tensor_tensor(dst, x, z, op)

            def ts(dst, x, s1, s2=None, op0=ALU.mult, op1=None):
                if op1 is None:
                    return nc.vector.tensor_scalar(dst, x, s1, None, op0)
                return nc.vector.tensor_scalar(dst, x, s1, s2, op0, op1)

            def stt(dst, x, s1, z, op0, op1):
                return nc.vector.scalar_tensor_tensor(out=dst, in0=x, scalar=s1, in1=z, op0=op0, op1=op1)

            turn = [0]

            def link(ins):
                link_at[0] += 1
                ins.then_inc(vlink.h, 1)
                dve.wait_ge(vlink.h, vlink.at(turn[0], link_at[0]))

            def layer_body(layer):
                turn[0] = layer

                def drain(name, dst):
                    b = G1.wait_full(dve, layer, name)
                    nc.vector.tensor_copy(dst, views(b)).then_inc(dr_v.h, 1)

                def softmax(n):
                    kind, bb = BATCHES[n]
                    dve.wait_ge(sc_full.h, sc_full.at(layer, n + 1))
                    dist = cst[:, C_DIST:C_DIST + S] if kind != "mla" else cst[:, C_MASK:C_MASK + S]
                    for m in range(4):
                        slope = {"moba": MOBA_SLOPES[(4 * bb + m) % 8], "mla": 1.0,
                                 "diff": DIFF_SLOPES[(2 * bb + m // 2) % 4]}[kind]
                        stt(sc[:, m, 0:S], dist, slope, bank[4 + m % 2][:, (m // 2) * S:(m // 2) * S + S],
                            ALU.mult, ALU.add)
                        ins = stt(sc[:, m, S:384], dist[:, P:S], slope,
                                  bank[6 + m % 2][:, (m // 2) * P:(m // 2) * P + P], ALU.mult, ALU.add)
                    link(ins)
                    nc.vector.tensor_reduce(nmax[:, 0:4], sc[:, :, 0:S], AX.X, ALU.max, negate=True)
                    nc.vector.tensor_reduce(nmax[:, 4:8], sc[:, :, S:384], AX.X, ALU.max, negate=True).then_inc(
                        sc_max.h, 1)
                    dve.wait_ge(p_exp.h, p_exp.at(layer, n + 1))
                    link(nc.vector.reciprocal(pinv[:, :], psum_[:, :]))
                    if kind == "diff":
                        second = pinv[:, :].rearrange("p (m c) -> p m c", c=2)[:, :, 1]
                        link(ts(second, second, lam[:, 2:3]))
                    tt_(sc[:, :, 0:S], sc[:, :, 0:S], pinv[:, 0:4].unsqueeze(2).broadcast_to([P, 4, S]), ALU.mult)
                    ins = tt_(sc[:, :, S:384], sc[:, :, S:384],
                              pinv[:, 4:8].unsqueeze(2).broadcast_to([P, 4, P]), ALU.mult)
                    if kind == "diff":
                        link(ins)
                        link(tt_(sc[:, 0, :], sc[:, 0, :], sc[:, 1, :], ALU.add))
                        ins = tt_(sc[:, 1, :], sc[:, 2, :], sc[:, 3, :], ALU.add)
                    ins.then_inc(p_ready.h, 1)

                def silu2(name, i, k):
                    b = G1.wait_full(dve, layer, name)
                    dve.wait_ge(z_tanh.h, z_tanh.at(layer, k + 1))
                    stt(zs[:, 2 * k:2 * k + 2, :], tmp[:, i, :].rearrange("p (t s) -> p t s", t=2), 1.0,
                        views(b), ALU.add, ALU.mult).then_inc(dr_v.h, 1)

                def gate(c):
                    stt(y[:, 4 * c:4 * c + 4, :], zs[:, 4 * c:4 * c + 4, :], 0.5, y[:, 4 * c:4 * c + 4, :],
                        ALU.mult, ALU.mult).then_inc(gated.h, 1)

                drain("ak0", aqk[:, 4:6, :])
                drain("ak1", aqk[:, 6:8, :])
                dve.wait_ge(par_in.h, par_in.at(layer, par_in.per))
                ts(par2[:, 0:24], par[:, P_BM:P_BM + 24], 0.5).then_inc(halfb.h, 1)
                ts(par2[:, 24:25], par[:, P_SUB:P_SUB + 1], par[:, P_LAM + 1:P_LAM + 2])
                lv = par[:, P_LQK:P1_END].rearrange("p (a b d) -> p a b d", b=2, d=HD)
                link(tt_(lam_p[:, :, :], lv[:, :, 0, :], lv[:, :, 1, :], ALU.mult))
                nc.vector.tensor_reduce(lam[:, 0:2], lam_p[:, :, :], AX.X, ALU.add).then_inc(lamp.h, 1)
                dve.wait_ge(lame.h, lame.at(layer, 1))
                link(tt_(lam[:, 3:4], lam[:, 1:2], lam[:, 0:1], ALU.subtract))
                link(tt_(lam[:, 2:3], lam[:, 3:4], par[:, P_LAM:P_LAM + 1], ALU.subtract))
                softmax(0)
                drain("dk0", dqk[:, 4:6, :])
                drain("dk1", dqk[:, 6:8, :])
                softmax(1)
                softmax(2)
                b = G1.wait_full(dve, layer, "ms")
                ts(rstd[:, 0:2, :], views(b), 1e-6, None, ALU.add).then_inc(dr_v.h, 1)
                dve.wait_ge(ms_std.h, ms_std.at(layer, 1))
                link(nc.vector.reciprocal(rstd[:, 0:2, :], rstd[:, 0:2, :]))
                for t in range(5):
                    ins = stt(cn[:, t, :], cq[:, t, :], par[:, P_GQ + t:P_GQ + t + 1], rstd[:, int(t >= 3), :],
                              ALU.mult, ALU.mult)
                ins.then_inc(ms_done.h, 1)
                softmax(3)

                def rope(name, dst, j):
                    b = G1.wait_full(dve, layer, name)
                    n = 1 if name == "rk" else 2
                    r = slice(HD, MLA_D)

                    def table(c):
                        return cst[r, c:c + S].unsqueeze(1).broadcast_to([ROPE, n, S])
                    got = bank[b][r, 0:n * S].rearrange("p (t s) -> p t s", t=n)
                    turned = rot[r, j % 2, 0:n * S].rearrange("p (t s) -> p t s", t=n)
                    tt_(turned, got, table(C_SIN), ALU.mult).then_inc(dr_v.h, 1)
                    link(tt_(dst, dst, table(C_COS), ALU.mult))
                    G1.wait_drained(dve, layer, name)
                    return tt_(dst, dst, turned, ALU.add)

                rope("rk", kr[HD:MLA_D, :].unsqueeze(1), 0).then_inc(kroped.h, 1)
                for j in range(4):
                    rope(f"rq{j}", qb[HD:MLA_D, 2 * j:2 * j + 2, :], j + 1).then_inc(rope_q.h, 1)
                for t in range(TT):
                    b = G1.wait_full(dve, layer, f"mv{t}")
                    nc.vector.tensor_copy(mv[:, t, :], bank[b][:, :]).then_inc(dr_v.h, 1)
                silu2("az0", 0, 0)
                silu2("az1", 1, 1)
                dve.wait_ge(y_ready.h, y_ready.at(layer, 2))
                G1.wait_drained(dve, layer, "az1")
                gate(0)
                softmax(4)
                silu2("bz0", 0, 2)
                silu2("bz1", 1, 3)
                silu2("cz0", 0, 4)
                silu2("cz1", 1, 5)
                softmax(5)
                for j in range(2):
                    b = G1.wait_full(dve, layer, f"dn{j}")
                    ts(rstd[:, 2 * j:2 * j + 2, :], views(b), 1e-5, None, ALU.add).then_inc(dr_v.h, 1)
                dve.wait_ge(dn_std.h, dn_std.at(layer, 1))
                link(nc.vector.reciprocal(rstd[:, :, :], rstd[:, :, :]))
                link(stt(y[:, 8:12, :], y[:, 8:12, :], par2[:, 24:25], rstd[:, :, :], ALU.mult, ALU.mult))
                G1.wait_drained(dve, layer, "cz1")
                gate(2)
                dve.wait_ge(y_ready.h, y_ready.at(layer, 6))
                gate(1)
                for c, br in enumerate("abc"):
                    for j in range(4):
                        b = G1.wait_full(dve, layer, f"b{br}{j}")
                        g = gates[:, 8 * c + 2 * j:8 * c + 2 * j + 2, :]
                        dst = merged[:, 2 * j:2 * j + 2, :]
                        if c == 0:
                            if j == 0:
                                G1.wait_drained(dve, layer, "mg11")
                            stt(dst, g, 1.0, views(b), ALU.add, ALU.mult).then_inc(dr_v.h, 1)
                            continue
                        u = tmp[:, j % 2, :].rearrange("p (t s) -> p t s", t=2)
                        stt(u, g, 1.0, views(b), ALU.add, ALU.mult).then_inc(dr_v.h, 1)
                        G1.wait_drained(dve, layer, f"b{br}{j}")
                        if c == 2:
                            dve.wait_ge(mgd.h, mgd.at(layer, j + 1))
                        tt_(dst, dst, u, ALU.add).then_inc(mgd.h, 1)
                for j in range(4):
                    G1.wait_drained(dve, layer, f"ou{j}")
                    stt(r1[:, 2 * j:2 * j + 2, :], xT[:, 2 * j:2 * j + 2, :], ALPHA, ou[:, 2 * j:2 * j + 2, :],
                        ALU.mult, ALU.add).then_inc(r_ready.h, 1)
                for j in range(4):
                    G1.wait_drained(dve, layer, f"pg{j}")
                    u = tmp[:, j % 2, :].rearrange("p (t s) -> p t s", t=2)
                    link(stt(u, u, 1.0, pleT[:, 2 * j:2 * j + 2, :], ALU.add, ALU.mult))
                    stt(merged[:, 2 * j:2 * j + 2, :], u, 0.5, r1[:, 2 * j:2 * j + 2, :], ALU.mult, ALU.add).then_inc(
                        r2_ready.h, 1)
                b = G1.wait_full(dve, layer, "lm")
                tt_(r1[:, :, :], merged[:, :, :], views(b)[:, 0:1, :].broadcast_to([P, DT, S]),
                    ALU.subtract).then_inc(dr_v.h, 1)
                b = G1.wait_full(dve, layer, "lv")
                ts(rstd[:, 0, :], views(b)[:, 0, :], 1e-5, None, ALU.add).then_inc(dr_v.h, 1)
                dve.wait_ge(ln_std.h, ln_std.at(layer, 1))
                link(nc.vector.reciprocal(rstd[:, 0, :], rstd[:, 0, :]))
                for t in range(DT):
                    stt(r1[:, t, :], r1[:, t, :], par[:, P_LG + t:P_LG + t + 1], rstd[:, 0, :],
                        ALU.mult, ALU.mult).then_inc(normed.h, 1)

            with dve.Fori(0, LAYERS) as layer:
                layer_body(layer)
            assert link_at[0] == vlink.per, f"vector steps of a layer: {link_at[0]}"
            turn[0], link_at[0] = LAYERS, 0

            def mixer(m):
                def drain(name):
                    return G2.wait_full(dve, m, name)

                dve.wait_ge(par2_in.h, par2_in.at(m, par2_in.per))
                for c0, c1 in ((Q_CS, Q_DS), (Q_CC, Q_CCB), (Q_CG, Q_CB + 2)):
                    ins = ts(q2[:, c0:c1], q2[:, c0:c1], 0.5)
                link(ins)
                b = drain("ms")
                ts(rs2[:, 0, :], views(b)[:, 0, :], 1e-5, None, ALU.add).then_inc(d2v.h, 1)
                dve.wait_ge(std_ready.h, std_ready.at(m, 1))
                link(nc.vector.reciprocal(rs2[:, 0, :], rs2[:, 0, :]))
                for t in range(DT):
                    ins = stt(h[:, t, :], xT[:, t, :], q2[:, Q_NM + t:Q_NM + t + 1], rs2[:, 0, :],
                              ALU.mult, ALU.mult)
                ins.then_inc(h_ready.h, 1)
                dve.wait_ge(pad0, 3)
                b = drain("gv")
                G2.wait_drained(dve, m, "gg")
                stt(gp[:, :, CONF_TAPS - 1:], ta[:, 0], 1.0, views(b), ALU.add, ALU.mult).then_inc(d2v.h, 1)
                G2.wait_drained(dve, m, "gv")

                def conv(dsts, srcs, cols, bias, k0, k1):
                    for k in range(k0, k1):
                        for dst, src, c, bb in zip(dsts, srcs, cols, bias):
                            x = src[:, k:k + S]
                            if k == 0 and bb is not None:
                                ins = ts(dst, x, q2[:, c:c + 1], q2[:, bb:bb + 1], ALU.mult, ALU.add)
                            elif k == 0:
                                ins = ts(dst, x, q2[:, c:c + 1])
                            else:
                                ins = stt(dst, x, q2[:, c + k:c + k + 1], dst, ALU.mult, ALU.add)
                        if k < k1 - 1:
                            link(ins)
                    return ins

                def conf(k0, k1):
                    return conv([gc[:, t, :] for t in range(2)], [gp[:, t, :] for t in range(2)],
                                [Q_CC + CONF_TAPS * t for t in range(2)], [Q_CCB, Q_CCB + 1], k0, k1)

                link(conf(0, 16))
                b = drain("ax")
                G2.wait_drained(dve, m, "ac")
                tt_(ap_[:, :, A_TAPS - 1:], acs_b[:, :, :], views(b), ALU.mult).then_inc(d2v.h, 1)
                G2.wait_drained(dve, m, "ax")
                conv([ac_y[:, t, :] for t in range(2)], [ap_[:, t, :] for t in range(2)],
                     [Q_CA + A_TAPS * t for t in range(2)], [None, None], 0, A_TAPS).then_inc(vlink.h, 1)
                link_at[0] += 1
                conf(16, CONF_TAPS).then_inc(cf_sum.h, 1)
                for j in range(4):
                    G2.wait_drained(dve, m, f"xb{j}")
                    conv([xc[:, t, :] for t in (2 * j, 2 * j + 1)], [xp[:, t, :] for t in (2 * j, 2 * j + 1)],
                         [Q_CS + SSD_TAPS * t for t in (2 * j, 2 * j + 1)],
                         [Q_CSB + t for t in (2 * j, 2 * j + 1)], 0, SSD_TAPS).then_inc(xc_half.h, 1)
                    if j:
                        silu_x(m, j - 1)
                b = drain("dt")
                v2 = dtt[:, 0, :].rearrange("p (t e) -> p t e", t=TT)
                tt_(v2, bank[b][:, 0:16].rearrange("p (t e) -> p t e", t=TT),
                    bc[:, 0:8].unsqueeze(1).broadcast_to([P, TT, 8]), ALU.add).then_inc(d2v.h, 1)
                G2.wait_drained(dve, m, "dt")
                stt(dtt[:, 1, :], dtt[:, 0, :], -1.0, dtt[:, 0, :], ALU.mult, ALU.min).then_inc(dt_neg.h, 1)
                dve.wait_ge(dte.h, dte.at(m, 1))
                ts(dtt[:, 3, :], dtt[:, 2, :], 1.0, None, ALU.add).then_inc(dt_w.h, 1)
                silu_x(m, 3)
                dve.wait_ge(dt_w.h, dt_w.at(m, 1))
                link(ts(dtt[:, 5, :], dtt[:, 3, :], 1.0, None, ALU.is_equal))
                dve.wait_ge(dtl.h, dtl.at(m, 1))
                tt_(dtt[:, 4, :], dtt[:, 4, :], dtt[:, 5, :], ALU.add)
                link(stt(dtt[:, 3, :], dtt[:, 3, :], -1.0, dtt[:, 5, :], ALU.add, ALU.add))
                link(nc.vector.reciprocal(dtt[:, 3, :], dtt[:, 3, :]))
                link(tt_(dtt[:, 4, :], dtt[:, 4, :], dtt[:, 3, :], ALU.mult))
                link(tt_(dtt[:, 4, :], dtt[:, 4, :], dtt[:, 2, :], ALU.mult))
                link(stt(dtt[:, 6, :], dtt[:, 0, :], 0.0, dtt[:, 4, :], ALU.max, ALU.add))
                stt(dtt[:, 7, :].rearrange("p (t e) -> p t e", t=TT),
                    dtt[:, 6, :].rearrange("p (t e) -> p t e", t=TT), -1.0,
                    bc[:, 8:16].unsqueeze(1).broadcast_to([P, TT, 8]), ALU.mult, ALU.mult).then_inc(dta.h, 1)
                dve.wait_ge(dta.h, dta.at(m, 1))
                nc.vector.tensor_copy(dtb[:, :, :, :].rearrange("p t e k -> p (t e) k"),
                                      dtt[:, 7, :].unsqueeze(2).broadcast_to([P, TT * 8, P])).then_inc(dtb_r.h, 1)
                b = drain("ab")
                dve.wait_ge(vlink.h, vlink.at(LAYERS, link_at[0]))
                tt_(cat[:, 0:2, :], views(b), ac_y[:, :, :], ALU.mult).then_inc(d2v.h, 1)
                for j in range(2):
                    b = drain(f"z{j}")
                    dve.wait_ge(z_t.h, z_t.at(m, j + 1))
                    stt(sz[:, 2 * j:2 * j + 2, :], ta[:, j], 1.0, views(b), ALU.add, ALU.mult).then_inc(d2v.h, 1)
                b = drain("acs")
                nc.vector.tensor_copy(acs[:, :, :], bank[b][:, 0:16].rearrange("p (t e) -> p t e", t=TT)).then_inc(
                    d2v.h, 1)
                G2.wait_drained(dve, m, "acs")
                for j in range(4):
                    b = drain(f"acb{j}")
                    mask = cst[:, C_MASKT:C_MASKT + S]
                    for t in range(2):
                        e = 2 * j + t
                        stt(em[:, e, 0:S], views(b)[:, t, :], acs[:, 0, e:e + 1], mask, ALU.subtract, ALU.add)
                        ins = stt(em[:, e, S:384], views(b)[:, t, P:S], acs[:, 1, e:e + 1], mask[:, 0:P],
                                  ALU.subtract, ALU.add)
                    ins.then_inc(d2v.h, 1)
                for t in range(TT):
                    b = drain(f"xt{t}")
                    tt_(xdt[:, t, :].rearrange("p (e d) -> p e d", d=HD),
                        bank[b][:, :].rearrange("p (e d) -> p e d", d=HD),
                        dtt[:, 6, 8 * t:8 * t + 8].unsqueeze(2).broadcast_to([P, 8, HD]), ALU.mult).then_inc(d2v.h, 1)
                for j in range(4):
                    dve.wait_ge(em_exp.h, em_exp.at(m, j + 1))
                    G2.wait_drained(dve, m, f"cb{j // 2}")
                    tt_(em[:, 2 * j:2 * j + 2, :], em[:, 2 * j:2 * j + 2, :],
                        cbm[:, j // 2:j // 2 + 1, :].broadcast_to([P, 2, 384]), ALU.mult).then_inc(em_r.h, 1)
                b = drain("cm")
                tt_(gc[:, :, :], gc[:, :, :], views(b)[:, 0:1, :].broadcast_to([P, 2, S]), ALU.subtract).then_inc(d2v.h, 1)
                b = drain("cv")
                ts(rs2[:, 1, :], views(b)[:, 0, :], 1e-5, None, ALU.add).then_inc(d2v.h, 1)
                for j in range(2):
                    b = drain(f"ys{j}")
                    for t in range(2):
                        k = 2 * j + t
                        ins = stt(cat[:, 2 + k, :], xc[:, k, :], q2[:, Q_DS + k:Q_DS + k + 1], views(b)[:, t, :],
                                  ALU.mult, ALU.add)
                    ins.then_inc(d2v.h, 1)
                G2.wait_drained(dve, m, "ys1")
                stt(cat[:, 2:6, :], sz[:, :, :], 0.5, cat[:, 2:6, :], ALU.mult, ALU.mult).then_inc(yz_r.h, 1)
                dve.wait_ge(cf_std.h, cf_std.at(m, 1))
                link(nc.vector.reciprocal(rs2[:, 1, :], rs2[:, 1, :]))
                for t in range(2):
                    ins = stt(gc[:, t, :], gc[:, t, :], q2[:, Q_CG + t:Q_CG + t + 1], rs2[:, 1, :], ALU.mult, ALU.mult)
                link(ins)
                for t in range(2):
                    ins = ts(gc[:, t, :], gc[:, t, :], q2[:, Q_CB + t:Q_CB + t + 1], None, ALU.add)
                ins.then_inc(cf_half.h, 1)
                b = drain("gn")
                ts(rs2[:, 2:4, :], views(b), 1e-5, None, ALU.add).then_inc(d2v.h, 1)
                dve.wait_ge(yz_std.h, yz_std.at(m, 1))
                link(nc.vector.reciprocal(rs2[:, 2:4, :], rs2[:, 2:4, :]))
                for t in range(4):
                    ins = stt(cat[:, 2 + t, :], cat[:, 2 + t, :], q2[:, Q_NW + t:Q_NW + t + 1], rs2[:, 2 + t // 2, :],
                              ALU.mult, ALU.mult)
                ins.then_inc(yn_done.h, 1)
                dve.wait_ge(cf_t.h, cf_t.at(m, 1))
                stt(cat[:, 6:8, :], yt[:, :, :], 1.0, gc[:, :, :], ALU.add, ALU.mult).then_inc(cf_done.h, 1)
                for j in range(4):
                    b = drain(f"wo{j}")
                    tt_(xT[:, 2 * j:2 * j + 2, :], xT[:, 2 * j:2 * j + 2, :], views(b), ALU.add).then_inc(d2v.h, 1)
                G2.wait_drained(dve, m, "wo3")

            def silu_x(m, j):
                dve.wait_ge(xc_t.h, xc_t.at(m, j + 1))
                stt(xc[:, 2 * j:2 * j + 2, :], xth[:, 2 * j:2 * j + 2, :], 1.0, xc[:, 2 * j:2 * j + 2, :],
                    ALU.add, ALU.mult).then_inc(xc_done.h, 1)

            def norm(n, dst, w):
                dve.wait_ge(nrm["full"].h, n)
                ts(rs2[:, 0, :], views(0)[:, 0, :], 1e-5, None, ALU.add).then_inc(nrm["eps"].h, 1)
                dve.wait_ge(nrm["std"].h, n)
                link(nc.vector.reciprocal(rs2[:, 0, :], rs2[:, 0, :]))
                for t in range(DT):
                    ins = stt(dst[:, t, :], xT[:, t, :], q2[:, w + t:w + t + 1], rs2[:, 0, :], ALU.mult, ALU.mult)
                ins.then_inc(nrm["h"].h, 1)

            def add_sums():
                for j in range(4):
                    tt_(xT[:, 2 * j:2 * j + 2, :], xT[:, 2 * j:2 * j + 2, :], views(4 + j), ALU.add).then_inc(x_up.h, 1)

            mixer(0)
            norm(1, h, Q_NF)
            with dve.Fori(0, FD // 2) as jj:
                for half in range(2):
                    dve.wait_ge(ff_t.h, jj * 2 + (half + 1))
                    stt(tb[:, half], ta[:, half], 1.0, views(2 * half), ALU.add, ALU.mult).then_inc(ff_g.h, 1)
                    dve.wait_ge(ff_g.h, jj * 2 + (half + 1))
                    dve.wait_ge(ff_full.h, jj * 4 + (2 * half + 2))
                    stt(hf[:, half], tb[:, half], 0.5, views(2 * half + 1), ALU.mult, ALU.mult).then_inc(ff_h.h, 1)
            dve.wait_ge(ff_t.h, FD)
            stt(tb[:, 0], ta[:, 0], 1.0, views(0), ALU.add, ALU.mult).then_inc(ff_g.h, 1)
            dve.wait_ge(ff_g.h, FD)
            dve.wait_ge(ff_full.h, 2 * FD)
            stt(hf[:, 0], tb[:, 0], 0.5, views(1), ALU.mult, ALU.mult).then_inc(ff_h.h, 1)
            dve.wait_ge(ff_down.h, FD)
            add_sums()
            dve.wait_ge(x_up.h, 4)
            mixer(1)
            norm(2, h, Q_NF)

            def spread(x):
                return x.broadcast_to([P, TT, 8])

            desc = cst[:, C_DESC:C_DESC + 8].unsqueeze(1).broadcast_to([P, TT, 8])
            dve.wait_ge(rt_full.h, 1)
            link(nc.vector.tensor_copy(lg[:, :, 0, :], bank[1][:, 0:16].rearrange("p (t e) -> p t e", t=TT)))

            def choose(src, to, top):
                link(nc.vector.tensor_reduce(lg[:, :, 4, top:top + 1], lg[:, :, src, :], AX.X, ALU.max))
                link(tt_(lg[:, :, to, :], lg[:, :, src, :], spread(lg[:, :, 4, top:top + 1]), ALU.is_equal))
                link(tt_(lg[:, :, to, :], lg[:, :, to, :], desc, ALU.mult))
                link(nc.vector.tensor_reduce(lg[:, :, 4, 2:3], lg[:, :, to, :], AX.X, ALU.max))
                link(tt_(lg[:, :, to, :], lg[:, :, to, :], spread(lg[:, :, 4, 2:3]), ALU.is_equal))

            choose(0, 1, 0)
            link(stt(lg[:, :, 2, :], lg[:, :, 1, :], -3e38, lg[:, :, 0, :], ALU.mult, ALU.add))
            choose(2, 3, 1)
            tt_(lg[:, :, 5, 0:1], lg[:, :, 4, 1:2], lg[:, :, 4, 0:1], ALU.subtract).then_inc(rt_top.h, 1)
            dve.wait_ge(rt_exp.h, 1)
            link(ts(lg[:, :, 7, 2:3], lg[:, :, 6, 0:1], 1.0, None, ALU.add))
            link(nc.vector.reciprocal(lg[:, :, 7, 0:1], lg[:, :, 7, 2:3]))
            link(tt_(lg[:, :, 7, 1:2], lg[:, :, 6, 0:1], lg[:, :, 7, 0:1], ALU.mult))
            tt_(lg[:, :, 1, :], lg[:, :, 1, :], spread(lg[:, :, 7, 0:1]), ALU.mult)
            link(tt_(lg[:, :, 3, :], lg[:, :, 3, :], spread(lg[:, :, 7, 1:2]), ALU.mult))
            link(tt_(gmat[:, :, :], lg[:, :, 1, :], lg[:, :, 3, :], ALU.add))
            link(ts(gmat[:, :, :], gmat[:, :, :], 0.5))
            nc.vector.tensor_copy(gmb[:, :, :, :].rearrange("p t e k -> p (t e) k"),
                                  gmat[:, :, :].rearrange("p t e -> p (t e)").unsqueeze(2).broadcast_to(
                                      [P, TT * 8, P])).then_inc(rt_b.h, 1)
            dve.wait_ge(rt_bc.h, 4)

            with dve.Fori(0, EXPERTS) as e, dve.Fori(0, FJ // 2) as jj:
                for half in range(2):
                    dve.wait_ge(mo_t.h, e * FJ + jj * 2 + (half + 1))
                    stt(tb[:, half], ta[:, half], 1.0, views(2 * half), ALU.add, ALU.mult).then_inc(mo_g.h, 1)
                    dve.wait_ge(mo_g.h, e * FJ + jj * 2 + (half + 1))
                    dve.wait_ge(mo_full.h, e * (2 * FJ) + jj * 4 + (2 * half + 2))
                    tt_(tb[:, half], tb[:, half], views(2 * half + 1), ALU.mult).then_inc(mo_p.h, 1)
                    dve.wait_ge(mo_p.h, e * FJ + jj * 2 + (half + 1))
                    tt_(hf[:, half], tb[:, half], gbc[:, bass.ds(e, 1), :].broadcast_to([P, 2, S]),
                        ALU.mult).then_inc(mo_h.h, 1)
            dve.wait_ge(mo_down.h, EXPERTS * FJ)
            add_sums()
            dve.wait_ge(x_up.h, 8)
            norm(3, cat, Q_NL)
            for n in range(4):
                dve.wait_ge(fin_full.h, n + 1)
                nc.vector.tensor_copy(h[:, 2 * n:2 * n + 2, :], views(n)).then_inc(out_full.h, 1)

        @block.gpsimd
        def _(pool):
            nc.gpsimd.memset(ones[:, 0], 1.0 / D).then_inc(ones_set, 1)
            nc.gpsimd.memset(ones[:, 1], 1.0 / Q_LORA).then_inc(ones_set, 1)
            nc.gpsimd.memset(ones[:, 2], 1.0 / KV_LORA).then_inc(ones_set, 1)
            nc.gpsimd.memset(ones[:, 3], 1.0 / P).then_inc(ones_set, 1)
            nc.gpsimd.memset(zeros[:, 0:256], 0.0).then_inc(w_free.h, RING)
            nc.gpsimd.memset(kr[0:HD, :], 0.0).then_inc(ones_set, 1)
            nc.gpsimd.memset(zeros[:, 256:512], 0.0).then_inc(ones_set, 1)

            with pool.Fori(0, LAYERS) as layer:
                pool.wait_ge(x_ready.h, x_ready.at(layer, DT))
                pool.dma_start(par[:, :], a["params1"][bass.ds(layer, 1), :, :].rearrange("o p c -> (o p) c")).then_inc(
                    par_in.h, 16)

            for m in range(LAYERS):
                if m == 0:
                    pool.wait_ge(x_ready.h, b1_end)
                    nc.gpsimd.memset(gp[:, :, 0:CONF_TAPS - 1], 0.0).then_inc(pad0, 1)
                    nc.gpsimd.memset(ap_[:, :, 0:A_TAPS - 1], 0.0).then_inc(pad0, 1)
                    nc.gpsimd.memset(xp[:, :, 0:SSD_TAPS - 1], 0.0).then_inc(pad0, 1)
                else:
                    pool.wait_ge(x_up.h, 4)

                pool.dma_start(q2[:, :], a["params2"][m, :, :]).then_inc(par2_in.h, 16)


_LARGE = ['x', 'p', 'w_in', 'mla_w_uq', 'mla_w_ukv', 'w_branch_a', 'w_branch_b', 'w_branch_c', 'w_merge', 'w_out',
          'w_ple_gate', 'w_ple', 'w_in_2', 'w_out_2', 'ffn_w_gate_2', 'ffn_w_up_2', 'ffn_w_down_2', 'moe_router_2',
          'moe_w_gate_2', 'moe_w_up_2', 'moe_w_down_2']
_SMALL = ['mla_q_norm_g', 'mla_kv_norm_g', 'diff_lambda', 'diff_subln_g', 'b_merge', 'ln_g', 'ln_b', 'norm_mix_2',
          'conv_a_w_2', 'conv_ssd_w_2', 'conv_ssd_b_2', 'dt_bias_2', 'a_log_2', 'd_skip_2', 'ssd_norm_w_2',
          'conv_conf_w_2', 'conv_conf_b_2', 'conf_ln_g_2', 'conf_ln_b_2', 'norm_ffn_2', 'norm_final_2']


def kernel(**inputs):
    import concourse.bacc as _bacc
    from concourse.bass_utils import run_bass_kernel_spmd as _run

    nc = _bacc.Bacc("TRN2", target_bir_lowering=False, num_devices=1)
    table = constants()
    v = {name: np.asarray(inputs[name]) for name in _SMALL}
    given = {name: np.ascontiguousarray(inputs[name]) for name in _LARGE}
    given["cst"] = table
    lam = np.broadcast_to(table[0, C_LAM:C_LAM + 4].reshape(LAYERS, 1, 2), (LAYERS, P, 2))
    given["params1"] = np.ascontiguousarray(np.concatenate(
        [by_feature(v[n]) for n in ("mla_q_norm_g", "mla_kv_norm_g", "diff_subln_g", "b_merge", "ln_g", "ln_b")]
        + [lam, on_all(v["diff_lambda"].reshape(LAYERS, -1))], axis=2))
    last = np.broadcast_to(v["norm_final_2"][None], (LAYERS, D))
    given["params2"] = np.ascontiguousarray(np.concatenate(
        [by_feature(v[n]) for n in ("norm_mix_2", "conv_a_w_2", "conv_ssd_w_2", "conv_ssd_b_2")]
        + [by_feature(np.repeat(v["d_skip_2"], HD, axis=1))]
        + [by_feature(v[n]) for n in ("ssd_norm_w_2", "conv_conf_w_2", "conv_conf_b_2", "conf_ln_g_2",
                                      "conf_ln_b_2", "norm_ffn_2")]
        + [by_feature(last), on_all(v["dt_bias_2"]), on_all(v["a_log_2"])], axis=2))
    arrays, args = {}, {}
    for name, v in given.items():
        arrays[f"in_{name}_dram"] = v
        args[name] = nc.dram_tensor(f"in_{name}_dram", v.shape, mybir.dt.from_np(v.dtype), kind="ExternalInput").ap()
    out = nc.dram_tensor("out_0_dram", (1, S, D), F32, kind="ExternalOutput").ap()
    build_kernel(nc, args, out)
    r = _run(nc, [arrays], core_ids=[0])
    return r.results[0]["out_0_dram"]
```

```python
from contextlib import ExitStack

import numpy as np

import concourse.bass as bass
from concourse import mybir

F32 = mybir.dt.float32
ACT = mybir.ActivationFunctionType
ALU = mybir.AluOpType
AX = mybir.AxisListType

P = 128
S = 256
TT = S // P
D = 1024
DT = D // P
LAYERS = 2
HEADS = 8
HD = 64
ROPE = 32
MLA_D = HD + ROPE
DIFF_HEADS = 4
ALPHA = (2 * LAYERS) ** 0.25
Q_LORA, KV_LORA, PLE = 384, 256, 256
FF = 2816
EXPERTS = 8
TOP = 2
FFE = 3584
CONF_TAPS, SSD_TAPS, A_TAPS = 31, 4, 3
RING = 6
SLOT = 2048
BANKS = 4
NEG = -1e30

_n = HEADS + DIFF_HEADS
_slopes = [2.0 ** (-8.0 * (i + 1) / _n) for i in range(_n)]
_diff_at = [i * (_n // DIFF_HEADS) for i in range(DIFF_HEADS)]
DIFF_SLOPES = [_slopes[i] for i in _diff_at]
MOBA_SLOPES = [s for i, s in enumerate(_slopes) if i not in _diff_at]

C_IDENT, C_DIST, C_MASK, C_TRI, C_MASKT, C_ROT, C_COS, C_SIN, C_LAM, C_DESC, C_IOTA, C_END = (
    int(v) for v in np.cumsum([0, P, S, S, S, S, MLA_D, S, S, 4, 8, P]))


P_GQ, P_GKV, P_SUB, P_BM, P_LG, P_LB, P_LAM, P_LQK, P1_END = (
    int(v) for v in np.cumsum([0, 3, 2, 1, 24, 8, 8, 2, 4 * HD]))
Q_NM, Q_CA, Q_CS, Q_CSB, Q_DS, Q_NW, Q_CC, Q_CCB, Q_CG, Q_CB, Q_NF, Q_NL, Q_BC, P2_END = (
    int(v) for v in np.cumsum([0, 8, 2 * A_TAPS, 8 * SSD_TAPS, 8, 4, 4, 2 * CONF_TAPS, 2, 2, 2, 8, 8, 16]))


def by_feature(v):
    if v.ndim == 2:
        v = v[:, None, :]
    layers, taps, n = v.shape
    return v.reshape(layers, taps, n // P, P).transpose(0, 3, 2, 1).reshape(layers, P, -1)


def on_all(v):
    return np.broadcast_to(v[:, None, :], (v.shape[0], P, v.shape[1]))


def constants():
    c = np.zeros((P, C_END), np.float32)
    p, k = np.arange(P)[:, None], np.arange(P)[None, :]
    c[:, C_IDENT:C_IDENT + P] = p == k
    c[:, C_DIST:C_DIST + P] = k - P - p
    c[:, C_DIST + P:C_DIST + S] = np.where(k <= p, k - p, NEG)
    c[:, C_MASK + P:C_MASK + S] = np.where(k <= p, 0.0, NEG)
    c[:, C_TRI:C_TRI + P] = p <= k
    c[:, C_TRI + P:C_TRI + S] = 1.0
    c[:, C_MASKT:C_MASKT + P] = np.where(k >= p, 0.0, NEG)
    half = ROPE // 2
    for m in range(ROPE):
        if m < half:
            c[HD + m + half, C_ROT + HD + m] = -1.0
        else:
            c[HD + m - half, C_ROT + HD + m] = 1.0
    freqs = np.float32(10000.0) ** (-np.arange(0, ROPE, 2, dtype=np.float32) / np.float32(ROPE))
    ang = np.arange(S, dtype=np.float32)[None, :] * freqs[:, None].astype(np.float32)
    c[HD:MLA_D, C_COS:C_COS + S] = np.tile(np.cos(ang), (2, 1))
    c[HD:MLA_D, C_SIN:C_SIN + S] = np.tile(np.sin(ang), (2, 1))
    for li in range(LAYERS):
        lam = 0.8 - 0.6 * np.exp(-0.3 * li)
        c[:, C_LAM + 2 * li] = lam
        c[:, C_LAM + 2 * li + 1] = 1.0 - lam
    c[:, C_DESC:C_DESC + 8] = np.arange(8, 0, -1)
    c[:, C_IOTA:C_IOTA + P] = k
    return c


class Signal:

    def __init__(self, handle, per=0):
        self.h, self.per = handle, per

    def at(self, turn, n):
        return turn * self.per + n


class Groups:

    def __init__(self, table, full, drained_a, drained_v, turns_before=0):
        self.names = [n for n, _ in table]
        self.owner = [o for _, o in table]
        assert len(set(self.names)) == len(self.names)
        self.full, self.drained = full, {"a": drained_a, "v": drained_v}

    def index(self, name):
        return self.names.index(name)

    def nth(self, g):
        return sum(o == self.owner[g] for o in self.owner[:g + 1])

    def count(self, owner):
        return sum(o == owner for o in self.owner)

    def wait_full(self, eng, turn, name):
        eng.wait_ge(self.full.h, self.full.at(turn, self.index(name) + 1))
        return self.index(name) % BANKS

    def drained_by(self, name):
        return self.drained[self.owner[self.index(name)]].h

    def wait_drained(self, eng, turn, name):
        g = self.index(name)
        s = self.drained[self.owner[g]]
        eng.wait_ge(s.h, s.at(turn, self.nth(g)))

    def wait_bank(self, eng, turn, name):
        g = self.index(name)
        if g >= BANKS:
            self.wait_drained(eng, turn, self.names[g - BANKS])
        return g % BANKS


BATCHES = [("moba", 0), ("moba", 1), ("diff", 0), ("diff", 1), ("mla", 0), ("mla", 1)]

ORDER1 = [
    ("aq0", "a"), ("aq1", "a"), ("ak0", "v"), ("ak1", "v"), ("av0", "a"), ("av1", "a"), ("A", 0),
    ("dq0", "a"), ("dq1", "a"), ("B", 0), ("dk0", "v"), ("dk1", "v"), ("V", 0), ("A", 1),
    ("dv0", "a"), ("dv1", "a"), ("B", 1), ("mc0", "a"), ("mc1", "a"), ("V", 1), ("A", 2),
    ("mc2", "a"), ("ms", "v"), ("B", 2), ("pt", "a"), ("pl0", "a"), ("pl1", "a"), ("pl2", "a"),
    ("pl3", "a"), ("V", 2), ("A", 3), ("uq0", "a"), ("uq1", "a"), ("uq2", "a"), ("uq3", "a"),
    ("rk", "v"), ("rq0", "v"), ("rq1", "v"), ("kn0", "a"), ("kn1", "a"), ("kn2", "a"),
    ("kn3", "a"), ("rq2", "v"), ("rq3", "v"), ("mv0", "v"), ("mv1", "v"), ("B", 3),
    ("az0", "v"), ("az1", "v"), ("V", 3), ("A", 4), ("bz0", "v"), ("bz1", "v"), ("B", 4),
    ("cz0", "v"), ("cz1", "v"), ("V", 4), ("A", 5), ("dn0", "v"), ("dn1", "v"),
    ("mg0", "a"), ("mg1", "a"), ("B", 5), ("mg2", "a"), ("mg3", "a"), ("V", 5),
] + [(f"mg{j}", "a") for j in range(4, 12)] + [
    (f"b{c}{j}", "v") for c in "abc" for j in range(4)] + [
    (f"ou{j}", "a") for j in range(4)] + [(f"pg{j}", "a") for j in range(4)] + [
    ("lm", "v"), ("lv", "v")]
STEPS = ("A", "B", "V")

UNITS1 = (
    [("w_in", c, 256, 8) for c in range(0, 1536, 256)]
    + [("w_in", c, 256, 8) for c in range(3232, 3232 + 1536, 256)]
    + [("w_in", 2048, 256, 8), ("w_in", 2304, 256, 8), ("w_in", 2560, 160, 8)]
    + [("p", 0, 256, 2), ("w_ple", 0, 1024, 2)]
    + [("w_uq", c, 192, 3) for c in range(0, 768, 192)] + [("w_ukv", 0, 1024, 2)]
    + [("w_in", c, 256, 8) for c in (1536, 1792, 2720, 2976, 4768, 5024)]
    + [("w_merge", c, 256, 8) for c in range(0, 3072, 256)]
    + [(w, c, 512, 4) for w in ("w_a", "w_b", "w_c") for c in (0, 512)]
    + [("w_out", c, 256, 8) for c in range(0, 1024, 256)]
    + [("w_pg", c, 256, 8) for c in range(0, 1024, 256)])
assert len(UNITS1) % RING == 0

ORDER2 = ([("ms", "v"), ("gg", "a"), ("gv", "v"), ("ac", "a"), ("ax", "v")]
          + [(f"xb{j}", "a") for j in range(4)]
          + [("dt", "v"), ("ab", "v"), ("z0", "v"), ("z1", "v"), ("acs", "v")]
          + [(f"acb{j}", "v") for j in range(4)]
          + [("xt0", "v"), ("xt1", "v"), ("cb0", "a"), ("cb1", "a"), ("cm", "v"), ("cv", "v"),
             ("ys0", "v"), ("ys1", "v"), ("gn", "v")]
          + [(f"wo{j}", "v") for j in range(4)])


def build_kernel(nc, a, out):
    ctx = ExitStack()
    with ctx:
        def sb(name, shape, stack=ctx):
            return stack.enter_context(nc.sbuf_tensor(name, shape, F32))

        def sem(name):
            return ctx.enter_context(nc.semaphore(name))

        def signal(name, per=0):
            return Signal(sem(name), per)

        bank = [ctx.enter_context(nc.psum_tensor(f"bank{i}", [P, 512], F32)) for i in range(8)]
        ring = sb("ring", [P, RING, SLOT])
        cst = sb("cst", [P, C_END])
        xT = sb("xT", [P, DT, S])
        sq = sb("sq", [P, DT, S])
        ones = sb("ones", [P, 4, P])
        zeros = ctx.enter_context(nc.sbuf_tensor("zeros", [P, 512], mybir.dt.bfloat16))
        ident = cst[:, C_IDENT:C_IDENT + P]
        ONES = {D: ones[:, 0], Q_LORA: ones[:, 1], KV_LORA: ones[:, 2], P: ones[:, 3]}

        m1 = ExitStack()
        aqk = sb("aqk", [P, 8, S], m1)
        dqk = sb("dqk", [P, 8, S], m1)
        av = sb("av", [P, TT, 512], m1)
        dv = sb("dv", [P, TT, 512], m1)
        cq = sb("cq", [P, 5, S], m1)
        cn = sb("cn", [P, 5, S], m1)
        kr = sb("kr", [P, S], m1)
        qb = sb("qb", [P, HEADS, S], m1)
        kb = sb("kb", [P, HEADS, S], m1)
        mv = sb("mv", [P, TT, 512], m1)
        rot = sb("rot", [P, 2, 512], m1)
        zs = sb("zs", [P, 12, S], m1)
        gates = sb("gates", [P, 24, S], m1)
        y = sb("y", [P, 12, S], m1)
        sc = sb("sc", [P, 4, 384], m1)
        pT = sb("pT", [P, 4, 384], m1)
        peT = sb("peT", [P, 2, S], m1)
        tmp = sb("tmp", [P, 2, 512], m1)
        rstd = sb("rstd", [P, 4, S], m1)
        nmax = sb("nmax", [P, 8], m1)
        psum_ = sb("sums", [P, 8], m1)
        pinv = sb("pinv", [P, 8], m1)
        lam_p = sb("lam_p", [P, 2, HD], m1)
        lam = sb("lam", [P, 4], m1)
        par = sb("par", [P, P1_END], m1)
        par2 = sb("par2", [P, 32], m1)
        pleT, merged = aqk, dqk
        r1, ou = qb, kb
        m1.close()

        m2 = ExitStack()
        h = sb("h", [P, DT, S], m2)
        gp = sb("gp", [P, 2, CONF_TAPS - 1 + S], m2)
        gc = sb("gc", [P, 2, S], m2)
        ap_ = sb("ap_", [P, 2, A_TAPS - 1 + S], m2)
        acs_b = sb("ac_sb", [P, 2, S], m2)
        cat = sb("cat", [P, DT, S], m2)
        ac_y = sb("ac_y", [P, 2, S], m2)
        xp = sb("xp", [P, 8, SSD_TAPS - 1 + S], m2)
        xc = sb("xc", [P, 8, S], m2)
        sz = sb("sz", [P, 4, S], m2)
        dtt = sb("dtt", [P, 8, TT * 8], m2)
        dtb = sb("dtb", [P, TT, 8, P], m2)
        acs = sb("acs", [P, TT, 8], m2)
        em = sb("em", [P, 8, 384], m2)
        cbm = sb("cbm", [P, 2, 384], m2)
        xdt = sb("xdt", [P, TT, 512], m2)
        rs2 = sb("rs2", [P, 4, S], m2)
        xth = sb("xth", [P, 8, S], m2)
        yt = sb("yt", [P, 2, S], m2)
        t2 = sb("t2", [P, 2, 512], m2)
        q2 = sb("q2", [P, P2_END], m2)
        bc = q2[:, Q_BC:Q_BC + 16]
        hf = sb("hf", [P, 2, 2, S], m2)
        ta = sb("ta", [P, 2, 2, S], m2)
        tb = sb("tb", [P, 2, 2, S], m2)
        lg = sb("lg", [P, TT, 8, 8], m2)
        gmat = sb("gmat", [P, TT, 8], m2)
        chosen = sb("chosen", [P, TT, 8], m2)
        place = sb("place", [P, TT, 8], m2)
        place2 = sb("place2", [P, TT, 8], m2)
        over = sb("over", [P, 4, 8], m2)
        over_n = m2.enter_context(nc.sbuf_tensor("over_n", [P, 4], mybir.dt.int32))
        htok = sb("htok", [P, TT, D], m2)
        pick = sb("pick", [P, TT, P], m2)
        pickg = sb("pickg", [P, TT, P], m2)
        put = sb("put", [P, S], m2)
        xg = sb("xg", [P, DT, P], m2)
        hd = sb("hd", [P, 512], m2)
        hdT = sb("hdT", [P, 4, P], m2)
        ye = sb("ye", [P, D], m2)
        m2.close()
        landed = [signal(f"w_landed{i}", 16 * len(UNITS1) // RING) for i in range(RING)]
        w_free = signal("w_slot_free", len(UNITS1))
        first_units = len(UNITS1) * LAYERS

        def unit_wait(eng, n):
            eng.wait_ge(landed[n % RING].h, 16 * (n // RING + 1))

        cst_in, x_in = sem("constants_landed"), sem("x_landed")
        ones_set = sem("ones_set")
        x0_full, x0_taken = sem("x_transposed"), sem("x_taken")
        x_ready = signal("x_ready", DT)
        par_in = signal("params_landed", 16)
        full = signal("group_full", sum(n not in STEPS for n, _ in ORDER1))
        dr_a = signal("drained_by_scalar", sum(o == "a" for _, o in ORDER1))
        dr_v = signal("drained_by_vector", sum(o == "v" for _, o in ORDER1))
        G1 = Groups([x for x in ORDER1 if x[0] not in STEPS], full, dr_a, dr_v)
        nb = len(BATCHES)
        sc_full, sc_max, p_exp, p_ready, p_turned, pT_ready, pv_full, y_ready = (
            signal(n, nb) for n in ("scores_full", "scores_max", "probs_exp", "probs_ready",
                                    "probs_turned", "probsT_ready", "pv_full", "y_ready"))
        z_tanh = signal("z_tanh", 6)
        ms_std, ms_done = (signal(n, 1) for n in ("latent_std", "latent_normed"))
        dn_sq, dn_std = (signal(n, 1) for n in ("diff_squares", "diff_std"))
        gated = signal("branch_gated", 3)
        dt_neg, dt_w = signal("dt_neg_abs", 1), signal("dt_exp_plus_1", 1)
        lamp, lame = signal("lambda_sums", 1), signal("lambda_exp", 1)
        halfb = signal("half_bias", 1)
        rope_q, kroped, kall = signal("q_roped", 4), signal("k_roped", 1), signal("k_rope_spread", 1)
        mgd = signal("merged", 8)
        r_ready = signal("r_ready", 4)
        r2_ready = signal("r_gated", 4)
        ln_sq, ln_std, normed = (signal(n, k) for n, k in (
            ("ln_squares", 1), ("ln_std", 1), ("ln_scaled", DT)))
        vlink = signal("vector_step", 34)

        def unit_view(slot, cols, k):
            return ring[:, slot, 0:k * cols].rearrange("p (k n) -> p k n", n=cols)

        def views(b, n=2):
            return bank[b][:, :].rearrange("p (t s) -> p t s", t=n)

        units2 = []
        FD, FJ = FF // S, FFE // S
        for i in range(LAYERS):
            units2 += [("w_in_2", i, c, 256, 8) for c in (2568, 2312, 256, 512)]
            units2 += [("w_in_2", i, c, 256, 8) for c in range(1280, 2304, 256)]
            units2 += [("w_in_2", i, 2304, 8, 8), ("w_in_2", i, 0, 256, 8)]
            units2 += [("w_in_2", i, c, 256, 8) for c in (768, 1024)]
            units2 += [("w_out_2", i, c, 256, 8) for c in range(0, 1024, 256)]
            if i == 0:
                for steps in [(j, j + 1) for j in range(0, FD - 1, 2)] + [(FD - 1,)]:
                    for j in steps:
                        units2 += [("ffn_w_gate_2", 0, j * S, 256, 8), ("ffn_w_up_2", 0, j * S, 256, 8)]
                    units2 += [("ffn_w_down_2", 0, j * S, 1024, 2) for j in steps]
            else:
                units2 += [("moe_router_2", 0, 0, 8, 8)]
        assert len(units2) % RING == 0
        moe_base = first_units + len(units2)
        U_MOE = 3 * FJ
        HS = FFE // 512
        OVER = TOP * S // (P + 1)
        ffn_at = 16

        def source(name, layer, c0, cols, k):
            if name in ("ffn_w_down_2",):
                return a[name][layer, c0:c0 + k * P, :].rearrange("(k p) n -> p k n", p=P)
            return a[name][layer, 0:k * P, c0:c0 + cols].rearrange("(k p) n -> p k n", p=P)

        block = ctx.enter_context(nc.Block())

        out_full, out_done = signal("out_rows_ready"), sem("out_written")
        over_ready = signal("over_list_ready")

        @block.sync
        def _(sp):
            sp.dma_start(cst[:, :], a["cst"]).then_inc(cst_in, 16)
            sp.dma_start(sq[:, :, :].rearrange("p (t a) s -> p t (a s)", t=TT),
                         a["x"][0].rearrange("(t p) d -> p t d", p=P)).then_inc(x_in, 16)
            with sp.Fori(0, LAYERS) as layer:
                for u, (name, c0, cols, k) in enumerate(UNITS1):
                    sp.wait_ge(w_free.h, w_free.at(layer, u + 1))
                    src = {"p": "p", "w_a": "w_branch_a", "w_b": "w_branch_b", "w_c": "w_branch_c",
                           "w_pg": "w_ple_gate", "w_uq": "mla_w_uq", "w_ukv": "mla_w_ukv"}.get(name, name)
                    dram = a[src][bass.ds(layer, 1), 0:k * P, c0:c0 + cols] if name != "p" else \
                        a["p"][bass.ds(layer, 1), 0, :, :]
                    dram = dram.rearrange("o (k p) n -> p (o k) n", p=P)
                    sp.dma_start(unit_view(u % RING, cols, k), dram).then_inc(landed[u % RING].h, 16)
            for u, unit in enumerate(units2):
                sp.wait_ge(w_free.h, first_units + u + 1)
                sp.dma_start(unit_view(u % RING, unit[3], unit[4]), source(*unit)).then_inc(
                    landed[u % RING].h, 16)
            def expert(turn, e):
                def unit(u, name, half, step, at):
                    sp.wait_ge(w_free.h, turn * U_MOE + at + (moe_base + u + 1))
                    rows = a[name][0]
                    if name == "moe_w_down_2":
                        dram = rows[bass.ds(e, 1), bass.ds(step * 512 + half * S, S), :]
                        view = unit_view(u % RING, 1024, 2)
                    else:
                        dram = rows[bass.ds(e, 1), half * 512:half * 512 + 512, bass.ds(step * 512, 512)]
                        view = unit_view(u % RING, 512, 4)
                    sp.dma_start(view, dram.rearrange("o (k p) n -> p (o k) n", p=P)).then_inc(
                        landed[u % RING].h, 16)

                for u in range(4):
                    unit(u, ("moe_w_gate_2", "moe_w_up_2")[u // 2], u % 2, 0, 0)
                with sp.Fori(0, HS - 1) as s:
                    for u in range(RING):
                        unit(4 + u, ("moe_w_gate_2", "moe_w_down_2", "moe_w_up_2")[u // 2], u % 2,
                             s if u // 2 == 1 else s + 1, s * RING)
                for u in range(2):
                    unit(U_MOE - 2 + u, "moe_w_down_2", u, HS - 1, 0)

            with sp.Fori(0, EXPERTS) as e:
                expert(e, e)
            sp.wait_ge(over_ready.h, 1)
            n_over = sp.value_load(over_n[0:1, 0:1], min_val=0, max_val=OVER)
            with sp.Fori(0, OVER) as k:
                with sp.If(n_over > k):
                    e = sp.value_load(over_n[0:1, bass.ds(k + 1, 1)], min_val=0, max_val=EXPERTS - 1)
                    expert(k + EXPERTS, e)
            for t in range(TT):
                sp.wait_ge(out_full.h, 2 * (t + 1))
                sp.dma_start(out[0, t * P:(t + 1) * P, :],
                             h[:, :, :].rearrange("p (t a) s -> p t (a s)", t=TT)[:, t, :]).then_inc(out_done, 16)
            sp.wait_ge(out_done, 16 * TT)

        full2 = signal("group2_full", len(ORDER2))
        d2a = signal("drained2_by_scalar", sum(o == "a" for _, o in ORDER2))
        d2v = signal("drained2_by_vector", sum(o == "v" for _, o in ORDER2))
        G2 = Groups(ORDER2, full2, d2a, d2v)
        par2_in = signal("mixer_params_landed", 16)
        sq_ready, std_ready = signal("norm_squares", 1), signal("norm_std", 1)
        h_ready = signal("h_ready", 1)
        xc_half, xc_t, xc_done = signal("xbc_conv", 4), signal("xbc_tanh", 4), signal("xbc_done", 4)
        z_t = signal("gate_z_tanh", 2)
        dte, dtl, dta = signal("dt_exp", 1), signal("dt_ln", 1), signal("dt_done", 1)
        dtb_r = signal("dt_spread", 1)
        em_exp, em_r = signal("decay_exp", 4), signal("decay_cb", 4)
        cf_sum, cf_sq, cf_std, cf_half, cf_t, cf_done = (signal(n, 1) for n in (
            "conf_conv", "conf_squares", "conf_std", "conf_scaled", "conf_tanh", "conf_done"))
        yz_r, yz_sq, yz_std, yn_done = (signal(n, 1) for n in (
            "yz_ready", "yz_squares", "yz_std", "yn_done"))
        x_up = signal("x_updated")
        pad0 = sem("pads_cleared")
        b1_end = (LAYERS + 1) * DT
        ff_full, ff_t, ff_g, ff_h, ff_down = (signal(n) for n in (
            "ffn_full", "ffn_tanh", "ffn_gate_done", "ffn_h_ready", "ffn_down_done"))
        g_full, u_full, mo_t, mo_g, mo_h, hT_full, hT_ready = (signal(n, HS) for n in (
            "expert_gate_full", "expert_up_full", "expert_tanh", "expert_silu", "expert_hidden",
            "hidden_turned", "hiddenT_ready"))
        picked = signal("tokens_picked", 2)
        xg_full, xg_ready = signal("gather_full", 2), signal("gathered", 2)
        put_full, put_ready = signal("gates_turned", 1), signal("gatesT_ready", 1)
        ye_full, ye_a, ye_v = (signal(n, 1) for n in ("result_e_full", "result_e_scalar", "result_e_vector"))
        comb_full = signal("combine_full", 4)
        comb = signal("combined", 4)
        rt_full, rt_top, rt_exp, rt_mask, rt_place, htok_full, htok_ready, x_done = (
            signal(n) for n in ("router_full", "router_top", "router_exp", "router_chosen", "places_full",
                                "h_turned", "h_tokens_ready", "experts_added"))
        nrm = {n: signal("final_" + n) for n in ("sq", "full", "eps", "std", "rstd", "h")}
        fin_full = signal("result_full")

        @block.tensor
        def _(pe):
            owed = [0]

            def mm(dst, w, x, start, stop, share=False):
                ins = pe.matmul(dst, w, x, start=start, stop=stop, skip_group_check=share)
                if owed[0]:
                    ins.then_inc(w_free.h, 1)
                    owed[0] = 0
                return ins

            pe.wait_ge(cst_in, 16)
            pe.wait_ge(x_in, 16)
            xtok = sq[:, :, :].rearrange("p (t a) s -> p t (a s)", t=TT)
            for b in range(4):
                for t in range(2):
                    for tt in range(TT):
                        ins = pe.transpose(views(b)[:, t, tt * P:(tt + 1) * P],
                                           xtok[:, tt, (2 * b + t) * P:(2 * b + t + 1) * P], ident)
                ins.then_inc(x0_full, 1)
            pe.wait_ge(ones_set, 6)

            def layer_body(layer):
                unit = [0]

                def take(cols, k):
                    u = unit[0]
                    unit[0] += 1
                    owed[0] = int(u > 0)
                    s = landed[u % RING]
                    pe.wait_ge(s.h, s.at(layer, 16 * (u // RING + 1)))
                    return unit_view(u % RING, cols, k)

                def begin(name):
                    return G1.wait_bank(pe, layer, name)

                def project(name, w, x, k, m=P):
                    b = begin(name)
                    for t in range(2):
                        for kk in range(k):
                            ins = mm(views(b)[0:m, t, :], w[:, kk, t * m:(t + 1) * m], x[:, kk, :],
                                     kk == 0, kk == k - 1)
                    ins.then_inc(full.h, 1)

                def values(name, w, x, k):
                    b = begin(name)
                    for t in range(TT):
                        for kk in range(k):
                            ins = mm(views(b)[:, t, :], x[:, kk, t * P:(t + 1) * P], w[:, kk, :],
                                     kk == 0, kk == k - 1)
                    ins.then_inc(full.h, 1)

                def scores(n):
                    kind, b = BATCHES[n]
                    if kind == "moba":
                        G1.wait_drained(pe, layer, "aq1")
                        G1.wait_drained(pe, layer, "ak1")
                    elif kind == "diff":
                        G1.wait_drained(pe, layer, "dq1")
                        G1.wait_drained(pe, layer, "dk1")
                    else:
                        pe.wait_ge(rope_q.h, rope_q.at(layer, 4))
                        pe.wait_ge(kall.h, kall.at(layer, 1))
                        G1.wait_drained(pe, layer, "kn3")
                    if n >= 1:
                        pe.wait_ge(pT_ready.h, pT_ready.at(layer, n))

                    def qk(m):
                        if kind == "mla":
                            return qb[0:MLA_D, 4 * b + m, :], kb[0:MLA_D, 4 * b + m, :]
                        q = aqk if kind == "moba" else dqk
                        part = slice(HD * (m % 2), HD * (m % 2) + HD)
                        return q[part, 2 * b + m // 2, :], q[part, 4 + 2 * b + m // 2, :]

                    for m in range(4):
                        q, k = qk(m)
                        mm(bank[4 + m % 2][:, (m // 2) * S:(m // 2) * S + S], q[:, P:S], k, True, True)
                    for m in (0, 2, 1, 3):
                        q, k = qk(m)
                        if m == 1 and n >= 1:
                            pe.wait_ge(y_ready.h, y_ready.at(layer, n))
                        ins = mm(bank[6 + m % 2][:, (m // 2) * P:(m // 2) * P + P], q[:, 0:P], k[:, 0:P],
                                 True, True)
                    ins.then_inc(sc_full.h, 1)

                def turn(n):
                    pe.wait_ge(p_ready.h, p_ready.at(layer, n + 1))
                    maps = 2 if BATCHES[n][0] == "diff" else 4
                    for b, c0 in ((4, 256), (5, 0), (6, 128)):
                        for m in range(maps):
                            ins = pe.transpose(bank[b][:, m * P:(m + 1) * P], sc[:, m, c0:c0 + P], ident)
                    ins.then_inc(p_turned.h, 1)

                def pv(n):
                    kind, b = BATCHES[n]
                    pe.wait_ge(pT_ready.h, pT_ready.at(layer, n + 1))
                    if kind == "mla":
                        G1.wait_drained(pe, layer, "mv1")
                    else:
                        G1.wait_drained(pe, layer, "av1" if kind == "moba" else "dv1")
                    maps = 2 if kind == "diff" else 4
                    for m in range(maps):
                        if kind == "diff":
                            v = dv[:, :, (2 * b + m) * P:(2 * b + m + 1) * P]
                            dst = views(7)[:, m, :]
                        else:
                            v = (av if kind == "moba" else mv)[:, :, (4 * b + m) * HD:(4 * b + m + 1) * HD]
                            dst = views(7)[HD * (m % 2):HD * (m % 2) + HD, m // 2, :]
                        mm(dst, v[:, 0, :], pT[:, m, 0:S], True, False)
                        ins = mm(dst[:, P:S], v[:, 1, :], pT[:, m, S:S + P], False, True)
                    ins.then_inc(pv_full.h, 1)

                pe.wait_ge(x_ready.h, x_ready.at(layer, DT))
                for name, who in ORDER1:
                    if name == "A":
                        scores(who)
                    elif name == "B":
                        turn(who)
                    elif name == "V":
                        pv(who)
                    elif name in ("av0", "av1", "dv0", "dv1"):
                        values(name, take(256, 8), xT, 8)
                    elif name == "mc2":
                        w = take(160, 8)
                        b = begin(name)
                        for kk in range(8):
                            mm(views(b)[:, 0, :], w[:, kk, 0:P], xT[:, kk, :], kk == 0, kk == 7)
                        for kk in range(8):
                            ins = mm(views(b)[HD:MLA_D, 1, :], w[:, kk, P:P + ROPE], xT[:, kk, :],
                                     kk == 0, kk == 7)
                        ins.then_inc(full.h, 1)
                    elif name == "ms":
                        G1.wait_drained(pe, layer, "mc2")
                        b = begin(name)
                        for kk in range(3):
                            mm(views(b)[:, 0, :], ONES[Q_LORA], sq[:, kk, :], kk == 0, kk == 2)
                        for kk in range(2):
                            ins = mm(views(b)[:, 1, :], ONES[KV_LORA], sq[:, 3 + kk, :], kk == 0, kk == 1)
                        ins.then_inc(full.h, 1)
                    elif name == "pt":
                        w = take(256, 2)
                        b = begin(name)
                        for kk in range(2):
                            for t in range(TT):
                                ins = pe.transpose(views(b)[:, kk, t * P:(t + 1) * P],
                                                   w[:, t, kk * P:(kk + 1) * P], ident)
                        ins.then_inc(full.h, 1)
                    elif name[:2] == "pl":
                        j = int(name[2])
                        if j == 0:
                            w = take(1024, 2)
                            G1.wait_drained(pe, layer, "pt")
                        project(name, w[:, :, 256 * j:256 * j + 256], peT, 2)
                    elif name[:2] == "uq":
                        if name == "uq0":
                            pe.wait_ge(ms_done.h, ms_done.at(layer, 1))
                        project(name, take(192, 3), cn, 3, m=MLA_D)
                    elif name[:1] == "r":
                        if name == "rk":
                            G1.wait_drained(pe, layer, "mc2")
                            src, width = kr[0:MLA_D, :], S
                        else:
                            j = int(name[2])
                            G1.wait_drained(pe, layer, f"uq{j}")
                            src, width = qb[0:MLA_D, 2 * j:2 * j + 2, :], 2 * S
                        b = begin(name)
                        mm(bank[b][0:MLA_D, 0:width], cst[0:MLA_D, C_ROT:C_ROT + MLA_D], src,
                           True, True).then_inc(full.h, 1)
                    elif name[:2] == "kn":
                        j = int(name[2])
                        if j == 0:
                            w = take(1024, 2)
                        b = begin(name)
                        for t in range(2):
                            for kk in range(2):
                                c0 = (2 * j + t) * 2 * HD
                                ins = mm(views(b)[0:HD, t, :], w[:, kk, c0:c0 + HD], cn[:, 3 + kk, :],
                                         kk == 0, kk == 1)
                        ins.then_inc(full.h, 1)
                    elif name[:2] == "mv":
                        t = int(name[2])
                        b = begin(name)
                        for kk in range(2):
                            wv = w[:, kk, :].rearrange("p (h d) -> p h d", d=2 * HD)[:, :, HD:2 * HD]
                            ins = mm(bank[b][:, :].rearrange("p (h d) -> p h d", d=HD),
                                     cn[:, 3 + kk, t * P:(t + 1) * P], wv, kk == 0, kk == 1)
                        ins.then_inc(full.h, 1)
                    elif name[:2] == "dn":
                        j = int(name[2])
                        if j == 0:
                            pe.wait_ge(dn_sq.h, dn_sq.at(layer, 1))
                        b = begin(name)
                        mm(bank[b][:, :], ONES[P], sq[:, 2 * j:2 * j + 2, :], True, True).then_inc(full.h, 1)
                    elif name[:2] in ("ba", "bb", "bc"):
                        j, c = int(name[2]), "abc".index(name[1])
                        if j % 2 == 0:
                            w = take(512, 4)
                        if j == 0:
                            pe.wait_ge(gated.h, gated.at(layer, {"a": 1, "c": 2, "b": 3}[name[1]]))
                        project(name, w[:, :, 256 * (j % 2):256 * (j % 2) + 256], y[:, 4 * c:4 * c + 4, :], 4)
                    elif name[:2] == "ou":
                        if name == "ou0":
                            pe.wait_ge(mgd.h, mgd.at(layer, 8))
                        project(name, take(256, 8), merged, 8)
                    elif name[:2] == "pg":
                        if name == "pg0":
                            pe.wait_ge(r_ready.h, r_ready.at(layer, 4))
                        project(name, take(256, 8), r1, 8)
                    elif name in ("lm", "lv"):
                        if name == "lm":
                            pe.wait_ge(r2_ready.h, r2_ready.at(layer, 4))
                        else:
                            pe.wait_ge(ln_sq.h, ln_sq.at(layer, 1))
                        b = begin(name)
                        owed[0] = int(name == "lm")
                        src = merged if name == "lm" else sq
                        for kk in range(DT):
                            ins = mm(views(b)[:, 0, :], ONES[D], src[:, kk, :], kk == 0, kk == DT - 1)
                        ins.then_inc(full.h, 1)
                    else:
                        project(name, take(256, 8), xT, 8)
                assert unit[0] == len(UNITS1)

            with pe.Fori(0, LAYERS) as layer:
                layer_body(layer)

            unit = [0]

            def take(cols, k):
                u = unit[0]
                unit[0] += 1
                owed[0] = int(u > 0)
                unit_wait(pe, first_units + u)
                return unit_view(u % RING, cols, k)

            def mixer(m):
                def begin(name):
                    return G2.wait_bank(pe, m, name)

                def project(name, w, x, k=DT):
                    b = begin(name)
                    for t in range(2):
                        for kk in range(k):
                            ins = mm(views(b)[:, t, :], w[:, kk, t * P:(t + 1) * P], x[:, kk, :],
                                     kk == 0, kk == k - 1)
                    ins.then_inc(full2.h, 1)

                def mean(name, src, tiles, t=0, width=D):
                    b = G2.index(name) % BANKS
                    for n, kk in enumerate(tiles):
                        ins = mm(views(b)[:, t, :], ONES[width], src[:, kk, :], n == 0, n == len(tiles) - 1)
                    return ins

                for name, _ in ORDER2:
                    if name == "ms":
                        pe.wait_ge(sq_ready.h, sq_ready.at(m, 1))
                        begin(name)
                        mean(name, sq, range(DT)).then_inc(full2.h, 1)
                        pe.wait_ge(h_ready.h, h_ready.at(m, 1))
                    elif name == "dt":
                        w = take(8, 8)
                        b = begin(name)
                        for t in range(TT):
                            for kk in range(DT):
                                ins = mm(bank[b][:, 8 * t:8 * t + 8], h[:, kk, t * P:(t + 1) * P],
                                         w[:, kk, :], kk == 0, kk == DT - 1)
                        ins.then_inc(full2.h, 1)
                    elif name == "acs":
                        pe.wait_ge(dta.h, dta.at(m, 1))
                        b = begin(name)
                        x = dtt[:, 7, :].rearrange("p (t e) -> p t e", t=TT)
                        mm(bank[b][:, 0:8], cst[:, C_TRI:C_TRI + P], x[:, 0, :], True, True)
                        mm(bank[b][:, 8:16], cst[:, C_TRI + P:C_TRI + S], x[:, 0, :], True, False)
                        mm(bank[b][:, 8:16], cst[:, C_TRI:C_TRI + P], x[:, 1, :], False, True).then_inc(
                            full2.h, 1)
                    elif name[:3] == "acb":
                        j = int(name[3])
                        if j == 0:
                            pe.wait_ge(dtb_r.h, dtb_r.at(m, 1))
                        b = begin(name)
                        for t in range(2):
                            mm(views(b)[:, t, :], dtb[:, 0, 2 * j + t, :], cst[:, C_TRI:C_TRI + S], True, False)
                            ins = mm(views(b)[:, t, P:S], dtb[:, 1, 2 * j + t, :], cst[:, C_TRI:C_TRI + P],
                                     False, True)
                        ins.then_inc(full2.h, 1)
                    elif name[:2] == "xt":
                        t = int(name[2])
                        if t == 0:
                            pe.wait_ge(xc_done.h, xc_done.at(m, 2))
                        b = begin(name)
                        for kk in range(4):
                            ins = pe.transpose(bank[b][:, kk * P:(kk + 1) * P], xc[:, kk, t * P:(t + 1) * P], ident)
                        ins.then_inc(full2.h, 1)
                    elif name[:2] == "cb":
                        g = int(name[2])
                        if g == 0:
                            pe.wait_ge(xc_done.h, xc_done.at(m, 4))
                        b = begin(name)
                        mm(bank[b][:, 0:S], xc[:, 4 + g, 0:P], xc[:, 6 + g, :], True, True)
                        mm(bank[b][:, S:S + P], xc[:, 4 + g, P:S], xc[:, 6 + g, P:S], True, True).then_inc(full2.h, 1)
                    elif name in ("cm", "cv"):
                        s = cf_sum if name == "cm" else cf_sq
                        pe.wait_ge(s.h, s.at(m, 1))
                        begin(name)
                        mean(name, gc if name == "cm" else sq, (0, 1) if name == "cm" else (4, 5), 0, KV_LORA).then_inc(full2.h, 1)
                    elif name[:2] == "ys":
                        j = int(name[2])
                        if j == 0:
                            G2.wait_drained(pe, m, "xt1")
                        pe.wait_ge(em_r.h, em_r.at(m, 2 * j + 2))
                        b = begin(name)
                        for hh in range(4 * j, 4 * j + 4):
                            dst = views(b)[HD * (hh % 2):HD * (hh % 2) + HD, (hh % 4) // 2, :]
                            mm(dst, xdt[:, 0, hh * HD:(hh + 1) * HD], em[:, hh, 0:S], True, False)
                            ins = mm(dst[:, P:S], xdt[:, 1, hh * HD:(hh + 1) * HD], em[:, hh, S:S + P], False, True)
                        ins.then_inc(full2.h, 1)
                    elif name == "gn":
                        pe.wait_ge(yz_sq.h, yz_sq.at(m, 1))
                        begin(name)
                        mean(name, sq, (0, 1), 0, KV_LORA)
                        mean(name, sq, (2, 3), 1, KV_LORA).then_inc(full2.h, 1)
                    elif name[:2] == "wo":
                        if name == "wo0":
                            G2.wait_drained(pe, m, "ab")
                            pe.wait_ge(yn_done.h, yn_done.at(m, 1))
                            pe.wait_ge(cf_done.h, cf_done.at(m, 1))
                        project(name, take(256, 8), cat)
                    else:
                        project(name, take(256, 8), h)

            def norm(n):
                pe.wait_ge(nrm["sq"].h, n)
                for kk in range(DT):
                    ins = mm(views(0)[:, 0, :], ONES[D], sq[:, kk, :], kk == 0, kk == DT - 1)
                ins.then_inc(nrm["full"].h, 1)
                pe.wait_ge(nrm["h"].h, n)

            def up(w, b, count):
                for t in range(2):
                    for kk in range(DT):
                        ins = mm(views(b)[:, t, :], w[:, kk, t * P:(t + 1) * P], h[:, kk, :],
                                 kk == 0, kk == DT - 1)
                ins.then_inc(count.h, 1)

            def down(w, x):
                for kk in range(2):
                    for t in range(DT):
                        ins = mm(views(4 + t // 2)[:, t % 2, :], w[:, kk, t * P:(t + 1) * P], x[:, kk, :],
                                 False, False, share=True)
                return ins

            def clear_sums():
                for b in range(4, 8):
                    pe.matmul(bank[b][:, :], zeros[:, 0:P], zeros[:, :], start=True, stop=True)

            mixer(0)
            norm(1)
            clear_sums()
            n0 = first_units + ffn_at
            with pe.Fori(0, FD // 2) as jj:
                for u in range(RING):
                    s = landed[(n0 + u) % RING]
                    owed[0] = 1
                    pe.wait_ge(s.h, jj * 16 + 16 * ((n0 + u) // RING + 1))
                    w = unit_view((n0 + u) % RING, *((1024, 2) if u >= 4 else (256, 8)))
                    if u < 4:
                        up(w, u, ff_full)
                    else:
                        pe.wait_ge(ff_h.h, jj * 2 + (u - 3))
                        down(w, hf[:, u - 4]).then_inc(ff_down.h, 1)
            unit[0] = ffn_at + 3 * (FD - 1)
            up(take(256, 8), 0, ff_full)
            up(take(256, 8), 1, ff_full)
            pe.wait_ge(ff_h.h, FD)
            down(take(1024, 2), hf[:, 0]).then_inc(ff_down.h, 1)
            mixer(1)
            norm(2)
            w = take(8, 8)
            for t in range(TT):
                for kk in range(DT):
                    ins = mm(bank[1][:, 8 * t:8 * t + 8], h[:, kk, t * P:(t + 1) * P], w[:, kk, :],
                             kk == 0, kk == DT - 1)
            ins.then_inc(rt_full.h, 1)
            assert unit[0] == len(units2)
            for t in range(TT):
                for half in range(2):
                    for kk in range(4):
                        ins = pe.transpose(bank[4 + 2 * t + half][:, kk * P:(kk + 1) * P],
                                           h[:, 4 * half + kk, t * P:(t + 1) * P], ident)
                        if owed[0]:
                            ins.then_inc(w_free.h, 1)
                            owed[0] = 0
                            ins = None
                    ins.then_inc(htok_full.h, 1)
            pe.wait_ge(rt_mask.h, 1)
            tri, all_ = cst[:, C_TRI:C_TRI + P], cst[:, C_TRI + P:C_TRI + S]
            mm(bank[2][:, 0:8], tri, chosen[:, 0, :], True, True)
            mm(bank[2][:, 8:16], all_, chosen[:, 0, :], True, False)
            mm(bank[2][:, 8:16], tri, chosen[:, 1, :], False, True)
            mm(bank[2][:, 16:24], all_, chosen[:, 0, :], True, False)
            mm(bank[2][:, 16:24], all_, chosen[:, 1, :], False, True).then_inc(rt_place.h, 1)
            pe.wait_ge(htok_ready.h, 4)

            def gather(turn, half):
                if half == 0:
                    pe.wait_ge(picked.h, picked.at(turn, 1))
                for kk in range(4):
                    for t in range(TT):
                        ins = mm(bank[5 + half][:, kk * P:(kk + 1) * P],
                                 htok[:, t, (4 * half + kk) * P:(4 * half + kk + 1) * P], pick[:, t, :],
                                 t == 0, t == TT - 1)
                ins.then_inc(xg_full.h, 1)

            def expert(turn, ahead=None):
                def landed_unit(u, at):
                    owed[0] = int(u > 0)
                    pe.wait_ge(landed[u % RING].h, turn * (16 * U_MOE // RING) + at + 16 * ((moe_base + u) // RING + 1))

                def product(u, b, count, at=0, between=None):
                    for half in range(2):
                        landed_unit(u + half, at)
                        w = unit_view((u + half) % RING, 512, 4)
                        for kk in range(4):
                            ins = mm(bank[b][:, :], xg[:, 4 * half + kk, :], w[:, kk, :],
                                     half == 0 and kk == 0, half == 1 and kk == 3)
                        if half == 0 and between:
                            between()
                    ins.then_inc(count.h, 1)

                def turn_hidden(s):
                    pe.wait_ge(mo_h.h, turn * HS + s + 1)
                    for c in range(4):
                        ins = pe.transpose(bank[2][:, c * P:(c + 1) * P], hd[:, c * P:(c + 1) * P], ident)
                    ins.then_inc(hT_full.h, 1)

                def down_(u, s, at=0):
                    pe.wait_ge(hT_ready.h, turn * HS + s + 1)
                    for half in range(2):
                        landed_unit(u + half, at)
                        w = unit_view((u + half) % RING, 1024, 2)
                        for kk in range(2):
                            for n in range(2):
                                ins = mm(bank[3 + n][:, :], hdT[:, 2 * half + kk, :],
                                         w[:, kk, n * 512:n * 512 + 512], False, False, share=True)
                    return ins

                pe.wait_ge(xg_ready.h, xg_ready.at(turn, 2))
                pe.wait_ge(comb.h, comb.at(turn, 1))
                product(0, 0, g_full)
                pe.wait_ge(comb.h, comb.at(turn, 2))
                product(2, 1, u_full)
                pe.wait_ge(comb.h, comb.at(turn, 4))
                for b in (3, 4):
                    pe.matmul(bank[b][:, :], zeros[:, 0:P], zeros[:, :], start=True, stop=True)
                with pe.Fori(0, HS - 1) as s:
                    pe.wait_ge(mo_g.h, turn * HS + s + 1)
                    product(4, 0, g_full, s * 16, lambda: turn_hidden(s))
                    down_(6, s, s * 16)
                    product(8, 1, u_full, s * 16)
                if ahead is not None:
                    gather(ahead, 0)
                turn_hidden(HS - 1)
                pe.wait_ge(picked.h, picked.at(turn, 2))
                for t in range(TT):
                    ins = pe.transpose(bank[7][:, t * P:(t + 1) * P], pickg[:, t, :], ident)
                ins.then_inc(put_full.h, 1)
                down_(U_MOE - 2, HS - 1).then_inc(ye_full.h, 1)
                owed[0] = 1
                if ahead is not None:
                    gather(ahead, 1)
                pe.wait_ge(ye_a.h, ye_a.at(turn, 1))
                pe.wait_ge(ye_v.h, ye_v.at(turn, 1))
                pe.wait_ge(put_ready.h, put_ready.at(turn, 1))
                for j, b in enumerate((0, 1, 2, 7)):
                    for t in range(2):
                        ins = mm(views(b)[:, t, :], ye[:, (2 * j + t) * P:(2 * j + t + 1) * P], put[:, :], True, True)
                    ins.then_inc(comb_full.h, 1)

            gather(0, 0)
            gather(0, 1)
            with pe.Fori(0, EXPERTS - 1) as e:
                expert(e, e + 1)
            expert(EXPERTS - 1)
            pe.wait_ge(over_ready.h, 1)
            n_over = pe.value_load(over_n[0:1, 0:1], min_val=0, max_val=OVER)
            with pe.Fori(0, OVER) as k:
                with pe.If(n_over > k):
                    gather(k + EXPERTS, 0)
                    gather(k + EXPERTS, 1)
                    expert(k + EXPERTS)
            norm(3)
            for t in range(TT):
                for half in range(2):
                    for kk in range(4):
                        ins = pe.transpose(bank[2 * t + half][:, kk * P:(kk + 1) * P],
                                           cat[:, 4 * half + kk, t * P:(t + 1) * P], ident)
                    ins.then_inc(fin_full.h, 1)


        @block.scalar
        def _(act):
            def fn(dst, src, func, **kw):
                return nc.scalar.activation(dst, src, func, **kw)

            def copy(dst, src, scale=1.0):
                return nc.scalar.activation(dst, src, ACT.Copy, scale=scale)

            for b in range(4):
                act.wait_ge(x0_full, b + 1)
                copy(xT[:, 2 * b:2 * b + 2, :], views(b)).then_inc(x_ready.h, 2)

            def layer_body(layer):
                def drain(name, dst, scale=1.0, rows=slice(0, P)):
                    b = G1.wait_full(act, layer, name)
                    copy(dst, views(b)[rows], scale).then_inc(dr_a.h, 1)

                def exps(n):
                    act.wait_ge(sc_max.h, sc_max.at(layer, n + 1))
                    for m in range(4):
                        fn(sc[:, m, 0:S], sc[:, m, 0:S], ACT.Exp, bias=nmax[:, m:m + 1],
                           accum_out=psum_[:, m:m + 1])
                        ins = fn(sc[:, m, S:384], sc[:, m, S:384], ACT.Exp, bias=nmax[:, 4 + m:5 + m],
                                 accum_out=psum_[:, 4 + m:5 + m])
                    ins.then_inc(p_exp.h, 1)

                def take_turned(n):
                    act.wait_ge(p_turned.h, p_turned.at(layer, n + 1))
                    maps = 2 if BATCHES[n][0] == "diff" else 4
                    for i, b in enumerate((4, 5, 6)):
                        ins = copy(pT[:, 0:maps, i * P:(i + 1) * P],
                                   bank[b][:, 0:maps * P].rearrange("p (m q) -> p m q", m=maps))
                    ins.then_inc(pT_ready.h, 1)

                def take_y(n):
                    kind, b = BATCHES[n]
                    act.wait_ge(pv_full.h, pv_full.at(layer, n + 1))
                    t0 = {"moba": 0, "mla": 4, "diff": 8}[kind] + 2 * b
                    copy(y[:, t0:t0 + 2, :], views(7)).then_inc(y_ready.h, 1)

                def gate_tanh(names, first):
                    for i, name in enumerate(names):
                        b = G1.wait_full(act, layer, name)
                        if first + i >= 2:
                            G1.wait_drained(act, layer, ["az0", "az1", "bz0", "bz1", "cz0", "cz1"][first + i - 2])
                        fn(tmp[:, i, :], bank[b][:, :], ACT.Tanh, scale=0.5).then_inc(z_tanh.h, 1)

                def merge_gate(j):
                    b = G1.wait_full(act, layer, f"mg{j}")
                    for t in range(2):
                        ins = fn(gates[:, 2 * j + t, :], views(b)[:, t, :], ACT.Tanh, scale=0.5,
                                 bias=par2[:, 2 * j + t:2 * j + t + 1])
                    ins.then_inc(dr_a.h, 1)

                scale = HD ** -0.5
                drain("aq0", aqk[:, 0:2, :], scale)
                drain("aq1", aqk[:, 2:4, :], scale)
                drain("av0", av[:, :, 0:S])
                drain("av1", av[:, :, S:512])
                act.wait_ge(lamp.h, lamp.at(layer, 1))
                fn(lam[:, 0:2], lam[:, 0:2], ACT.Exp).then_inc(lame.h, 1)
                exps(0)
                drain("dq0", dqk[:, 0:2, :], scale)
                drain("dq1", dqk[:, 2:4, :], scale)
                take_turned(0)
                take_y(0)
                exps(1)
                drain("dv0", dv[:, :, 0:S])
                drain("dv1", dv[:, :, S:512])
                take_turned(1)
                for i, name in enumerate(("mc0", "mc1")):
                    b = G1.wait_full(act, layer, name)
                    copy(cq[:, 2 * i:2 * i + 2, :], views(b))
                    fn(sq[:, 2 * i:2 * i + 2, :], views(b), ACT.Square).then_inc(dr_a.h, 1)
                take_y(1)
                exps(2)
                b = G1.wait_full(act, layer, "mc2")
                copy(cq[:, 4, :], views(b)[:, 0, :])
                fn(sq[:, 4, :], views(b)[:, 0, :], ACT.Square)
                copy(kr[HD:MLA_D, :], views(b)[HD:MLA_D, 1, :]).then_inc(dr_a.h, 1)
                G1.wait_drained(act, layer, "ms")
                fn(rstd[:, 0:2, :], rstd[:, 0:2, :], ACT.Sqrt).then_inc(ms_std.h, 1)
                take_turned(2)
                drain("pt", peT[:, :, :])
                for j in range(4):
                    drain(f"pl{j}", pleT[:, 2 * j:2 * j + 2, :])
                take_y(2)
                exps(3)
                for j in range(4):
                    drain(f"uq{j}", qb[0:MLA_D, 2 * j:2 * j + 2, :], MLA_D ** -0.5, slice(0, MLA_D))
                for j in range(4):
                    drain(f"kn{j}", kb[0:HD, 2 * j:2 * j + 2, :], 1.0, slice(0, HD))
                act.wait_ge(kroped.h, kroped.at(layer, 1))
                copy(kb[HD:MLA_D, :, :], kr[HD:MLA_D, :].unsqueeze(1).broadcast_to([ROPE, HEADS, S])).then_inc(
                    kall.h, 1)
                take_turned(3)
                gate_tanh(("az0", "az1"), 0)
                take_y(3)
                act.wait_ge(y_ready.h, y_ready.at(layer, 4))
                fn(sq[:, 0:4, :], y[:, 8:12, :], ACT.Square).then_inc(dn_sq.h, 1)
                exps(4)
                gate_tanh(("bz0", "bz1"), 2)
                take_turned(4)
                gate_tanh(("cz0", "cz1"), 4)
                take_y(4)
                exps(5)
                G1.wait_drained(act, layer, "dn1")
                fn(rstd[:, :, :], rstd[:, :, :], ACT.Sqrt).then_inc(dn_std.h, 1)
                act.wait_ge(halfb.h, halfb.at(layer, 1))
                merge_gate(0)
                merge_gate(1)
                take_turned(5)
                merge_gate(2)
                merge_gate(3)
                take_y(5)
                for j in range(4, 12):
                    merge_gate(j)
                for j in range(4):
                    drain(f"ou{j}", ou[:, 2 * j:2 * j + 2, :], 0.5)
                for j in range(4):
                    b = G1.wait_full(act, layer, f"pg{j}")
                    if j >= 2:
                        act.wait_ge(r2_ready.h, r2_ready.at(layer, j - 1))
                    fn(tmp[:, j % 2, :], bank[b][:, :], ACT.Tanh, scale=0.5).then_inc(dr_a.h, 1)
                G1.wait_drained(act, layer, "lm")
                fn(sq[:, :, :], r1[:, :, :], ACT.Square).then_inc(ln_sq.h, 1)
                G1.wait_drained(act, layer, "lv")
                fn(rstd[:, 0, :], rstd[:, 0, :], ACT.Sqrt).then_inc(ln_std.h, 1)
                for t in range(DT):
                    act.wait_ge(normed.h, normed.at(layer, t + 1))
                    fn(xT[:, t, :], r1[:, t, :], ACT.Identity, bias=par[:, P_LB + t:P_LB + t + 1]).then_inc(
                        x_ready.h, 1)

            with act.Fori(0, LAYERS) as layer:
                layer_body(layer)

            def mixer(m):
                if m:
                    act.wait_ge(x_up.h, 4)
                else:
                    act.wait_ge(x_ready.h, b1_end)
                fn(sq[:, :, :], xT[:, :, :], ACT.Square).then_inc(sq_ready.h, 1)
                G2.wait_drained(act, m, "ms")
                fn(rs2[:, 0, :], rs2[:, 0, :], ACT.Sqrt).then_inc(std_ready.h, 1)
                b = G2.wait_full(act, m, "gg")
                fn(ta[:, 0], views(b), ACT.Tanh, scale=0.5).then_inc(d2a.h, 1)
                b = G2.wait_full(act, m, "ac")
                copy(acs_b[:, :, :], views(b)).then_inc(d2a.h, 1)
                act.wait_ge(pad0, 3)
                for j in range(4):
                    b = G2.wait_full(act, m, f"xb{j}")
                    copy(xp[:, 2 * j:2 * j + 2, SSD_TAPS - 1:], views(b)).then_inc(d2a.h, 1)
                    if j:
                        act.wait_ge(xc_half.h, xc_half.at(m, j))
                        fn(xth[:, 2 * j - 2:2 * j, :], xc[:, 2 * j - 2:2 * j, :], ACT.Tanh).then_inc(xc_t.h, 1)
                act.wait_ge(xc_half.h, xc_half.at(m, 4))
                fn(xth[:, 6:8, :], xc[:, 6:8, :], ACT.Tanh).then_inc(xc_t.h, 1)
                act.wait_ge(dt_neg.h, dt_neg.at(m, 1))
                act.wait_ge(par2_in.h, par2_in.at(m, par2_in.per))
                fn(bc[:, 8:16], bc[:, 8:16], ACT.Exp)
                fn(dtt[:, 2, :], dtt[:, 1, :], ACT.Exp).then_inc(dte.h, 1)
                act.wait_ge(dt_w.h, dt_w.at(m, 1))
                fn(dtt[:, 4, :], dtt[:, 3, :], ACT.Ln).then_inc(dtl.h, 1)
                for j in range(2):
                    b = G2.wait_full(act, m, f"z{j}")
                    if j == 0:
                        G2.wait_drained(act, m, "gv")
                    fn(ta[:, j], views(b), ACT.Tanh, scale=0.5).then_inc(z_t.h, 1)
                for j in range(4):
                    G2.wait_drained(act, m, f"acb{j}")
                    fn(em[:, 2 * j:2 * j + 2, :], em[:, 2 * j:2 * j + 2, :], ACT.Exp).then_inc(em_exp.h, 1)
                for g in range(2):
                    b = G2.wait_full(act, m, f"cb{g}")
                    copy(cbm[:, g, :], bank[b][:, 0:384]).then_inc(d2a.h, 1)
                G2.wait_drained(act, m, "cm")
                fn(sq[:, 4:6, :], gc[:, :, :], ACT.Square).then_inc(cf_sq.h, 1)
                G2.wait_drained(act, m, "cv")
                fn(rs2[:, 1, :], rs2[:, 1, :], ACT.Sqrt).then_inc(cf_std.h, 1)
                act.wait_ge(yz_r.h, yz_r.at(m, 1))
                fn(sq[:, 0:4, :], cat[:, 2:6, :], ACT.Square).then_inc(yz_sq.h, 1)
                G2.wait_drained(act, m, "gn")
                fn(rs2[:, 2:4, :], rs2[:, 2:4, :], ACT.Sqrt).then_inc(yz_std.h, 1)
                act.wait_ge(cf_half.h, cf_half.at(m, 1))
                fn(yt[:, :, :], gc[:, :, :], ACT.Tanh).then_inc(cf_t.h, 1)

            def norm(n):
                fn(sq[:, :, :], xT[:, :, :], ACT.Square).then_inc(nrm["sq"].h, 1)
                act.wait_ge(nrm["eps"].h, n)
                fn(rs2[:, 0, :], rs2[:, 0, :], ACT.Sqrt).then_inc(nrm["std"].h, 1)

            mixer(0)
            G2.wait_drained(act, 0, "wo3")
            norm(1)
            with act.Fori(0, FD // 2) as jj:
                for half in range(2):
                    act.wait_ge(ff_full.h, jj * 4 + (2 * half + 1))
                    fn(ta[:, half], views(2 * half), ACT.Tanh, scale=0.5).then_inc(ff_t.h, 1)
            act.wait_ge(ff_full.h, 2 * FD - 1)
            fn(ta[:, 0], views(0), ACT.Tanh, scale=0.5).then_inc(ff_t.h, 1)
            mixer(1)
            G2.wait_drained(act, 1, "wo3")
            norm(2)
            act.wait_ge(rt_top.h, 1)
            fn(lg[:, :, 6, 0:1], lg[:, :, 5, 0:1], ACT.Exp).then_inc(rt_exp.h, 1)
            for n in range(4):
                act.wait_ge(htok_full.h, n + 1)
                copy(htok[:, n // 2, (n % 2) * 512:(n % 2) * 512 + 512], bank[4 + n][:, :]).then_inc(htok_ready.h, 1)

            def gathered(turn, half):
                act.wait_ge(xg_full.h, xg_full.at(turn, half + 1))
                copy(xg[:, 4 * half:4 * half + 4, :], views(5 + half, 4)).then_inc(xg_ready.h, 1)

            def tanh(turn, s):
                act.wait_ge(g_full.h, turn * HS + s + 1)
                fn(ta[:, 0], views(0), ACT.Tanh, scale=0.5).then_inc(mo_t.h, 1)

            def turned(turn, s):
                act.wait_ge(hT_full.h, turn * HS + s + 1)
                copy(hdT[:, :, :], views(2, 4)).then_inc(hT_ready.h, 1)

            def expert(turn, ahead=None):
                tanh(turn, 0)
                with act.Fori(0, HS - 1) as s:
                    turned(turn, s)
                    tanh(turn, s + 1)
                if ahead is not None:
                    gathered(ahead, 0)
                turned(turn, HS - 1)
                act.wait_ge(put_full.h, put_full.at(turn, 1))
                copy(put[:, :], bank[7][:, 0:S]).then_inc(put_ready.h, 1)
                act.wait_ge(ye_full.h, ye_full.at(turn, 1))
                copy(ye[:, 0:512], bank[3][:, :]).then_inc(ye_a.h, 1)
                if ahead is not None:
                    gathered(ahead, 1)

            gathered(0, 0)
            gathered(0, 1)
            with act.Fori(0, EXPERTS - 1) as e:
                expert(e, e + 1)
            expert(EXPERTS - 1)
            act.wait_ge(over_ready.h, 1)
            n_over = act.value_load(over_n[0:1, 0:1], min_val=0, max_val=OVER)
            with act.Fori(0, OVER) as k:
                with act.If(n_over > k):
                    gathered(k + EXPERTS, 0)
                    gathered(k + EXPERTS, 1)
                    expert(k + EXPERTS)
            act.wait_ge(x_done.h, 1)
            norm(3)

        @block.vector
        def _(dve):
            link_at = [0, 0]

            def tt_(dst, x, z, op):
                return nc.vector.tensor_tensor(dst, x, z, op)

            def ts(dst, x, s1, s2=None, op0=ALU.mult, op1=None):
                if op1 is None:
                    return nc.vector.tensor_scalar(dst, x, s1, None, op0)
                return nc.vector.tensor_scalar(dst, x, s1, s2, op0, op1)

            def stt(dst, x, s1, z, op0, op1):
                return nc.vector.scalar_tensor_tensor(out=dst, in0=x, scalar=s1, in1=z, op0=op0, op1=op1)

            turn = [0]

            def link(ins):
                link_at[0] += 1
                ins.then_inc(vlink.h, 1)
                dve.wait_ge(vlink.h, vlink.at(turn[0], link_at[0]))

            def layer_body(layer):
                turn[0] = layer

                def drain(name, dst):
                    b = G1.wait_full(dve, layer, name)
                    nc.vector.tensor_copy(dst, views(b)).then_inc(dr_v.h, 1)

                def softmax(n):
                    kind, bb = BATCHES[n]
                    dve.wait_ge(sc_full.h, sc_full.at(layer, n + 1))
                    dist = cst[:, C_DIST:C_DIST + S] if kind != "mla" else cst[:, C_MASK:C_MASK + S]
                    for m in range(4):
                        slope = {"moba": MOBA_SLOPES[(4 * bb + m) % 8], "mla": 1.0,
                                 "diff": DIFF_SLOPES[(2 * bb + m // 2) % 4]}[kind]
                        stt(sc[:, m, 0:S], dist, slope, bank[4 + m % 2][:, (m // 2) * S:(m // 2) * S + S],
                            ALU.mult, ALU.add)
                        ins = stt(sc[:, m, S:384], dist[:, P:S], slope,
                                  bank[6 + m % 2][:, (m // 2) * P:(m // 2) * P + P], ALU.mult, ALU.add)
                    link(ins)
                    nc.vector.tensor_reduce(nmax[:, 0:4], sc[:, :, 0:S], AX.X, ALU.max, negate=True)
                    nc.vector.tensor_reduce(nmax[:, 4:8], sc[:, :, S:384], AX.X, ALU.max, negate=True).then_inc(
                        sc_max.h, 1)
                    dve.wait_ge(p_exp.h, p_exp.at(layer, n + 1))
                    link(nc.vector.reciprocal(pinv[:, :], psum_[:, :]))
                    if kind == "diff":
                        second = pinv[:, :].rearrange("p (m c) -> p m c", c=2)[:, :, 1]
                        link(ts(second, second, lam[:, 2:3]))
                    tt_(sc[:, :, 0:S], sc[:, :, 0:S], pinv[:, 0:4].unsqueeze(2).broadcast_to([P, 4, S]), ALU.mult)
                    ins = tt_(sc[:, :, S:384], sc[:, :, S:384],
                              pinv[:, 4:8].unsqueeze(2).broadcast_to([P, 4, P]), ALU.mult)
                    if kind == "diff":
                        link(ins)
                        link(tt_(sc[:, 0, :], sc[:, 0, :], sc[:, 1, :], ALU.add))
                        ins = tt_(sc[:, 1, :], sc[:, 2, :], sc[:, 3, :], ALU.add)
                    ins.then_inc(p_ready.h, 1)

                def silu2(name, i, k):
                    b = G1.wait_full(dve, layer, name)
                    dve.wait_ge(z_tanh.h, z_tanh.at(layer, k + 1))
                    stt(zs[:, 2 * k:2 * k + 2, :], tmp[:, i, :].rearrange("p (t s) -> p t s", t=2), 1.0,
                        views(b), ALU.add, ALU.mult).then_inc(dr_v.h, 1)

                def gate(c):
                    stt(y[:, 4 * c:4 * c + 4, :], zs[:, 4 * c:4 * c + 4, :], 0.5, y[:, 4 * c:4 * c + 4, :],
                        ALU.mult, ALU.mult).then_inc(gated.h, 1)

                drain("ak0", aqk[:, 4:6, :])
                drain("ak1", aqk[:, 6:8, :])
                dve.wait_ge(par_in.h, par_in.at(layer, par_in.per))
                ts(par2[:, 0:24], par[:, P_BM:P_BM + 24], 0.5).then_inc(halfb.h, 1)
                ts(par2[:, 24:25], par[:, P_SUB:P_SUB + 1], par[:, P_LAM + 1:P_LAM + 2])
                lv = par[:, P_LQK:P1_END].rearrange("p (a b d) -> p a b d", b=2, d=HD)
                link(tt_(lam_p[:, :, :], lv[:, :, 0, :], lv[:, :, 1, :], ALU.mult))
                nc.vector.tensor_reduce(lam[:, 0:2], lam_p[:, :, :], AX.X, ALU.add).then_inc(lamp.h, 1)
                dve.wait_ge(lame.h, lame.at(layer, 1))
                link(tt_(lam[:, 3:4], lam[:, 1:2], lam[:, 0:1], ALU.subtract))
                link(tt_(lam[:, 2:3], lam[:, 3:4], par[:, P_LAM:P_LAM + 1], ALU.subtract))
                softmax(0)
                drain("dk0", dqk[:, 4:6, :])
                drain("dk1", dqk[:, 6:8, :])
                softmax(1)
                softmax(2)
                b = G1.wait_full(dve, layer, "ms")
                ts(rstd[:, 0:2, :], views(b), 1e-6, None, ALU.add).then_inc(dr_v.h, 1)
                dve.wait_ge(ms_std.h, ms_std.at(layer, 1))
                link(nc.vector.reciprocal(rstd[:, 0:2, :], rstd[:, 0:2, :]))
                for t in range(5):
                    ins = stt(cn[:, t, :], cq[:, t, :], par[:, P_GQ + t:P_GQ + t + 1], rstd[:, int(t >= 3), :],
                              ALU.mult, ALU.mult)
                ins.then_inc(ms_done.h, 1)
                softmax(3)

                def rope(name, dst, j):
                    b = G1.wait_full(dve, layer, name)
                    n = 1 if name == "rk" else 2
                    r = slice(HD, MLA_D)

                    def table(c):
                        return cst[r, c:c + S].unsqueeze(1).broadcast_to([ROPE, n, S])
                    got = bank[b][r, 0:n * S].rearrange("p (t s) -> p t s", t=n)
                    turned = rot[r, j % 2, 0:n * S].rearrange("p (t s) -> p t s", t=n)
                    tt_(turned, got, table(C_SIN), ALU.mult).then_inc(dr_v.h, 1)
                    link(tt_(dst, dst, table(C_COS), ALU.mult))
                    G1.wait_drained(dve, layer, name)
                    return tt_(dst, dst, turned, ALU.add)

                rope("rk", kr[HD:MLA_D, :].unsqueeze(1), 0).then_inc(kroped.h, 1)
                for j in range(4):
                    rope(f"rq{j}", qb[HD:MLA_D, 2 * j:2 * j + 2, :], j + 1).then_inc(rope_q.h, 1)
                for t in range(TT):
                    b = G1.wait_full(dve, layer, f"mv{t}")
                    nc.vector.tensor_copy(mv[:, t, :], bank[b][:, :]).then_inc(dr_v.h, 1)
                silu2("az0", 0, 0)
                silu2("az1", 1, 1)
                dve.wait_ge(y_ready.h, y_ready.at(layer, 2))
                G1.wait_drained(dve, layer, "az1")
                gate(0)
                softmax(4)
                silu2("bz0", 0, 2)
                silu2("bz1", 1, 3)
                silu2("cz0", 0, 4)
                silu2("cz1", 1, 5)
                softmax(5)
                for j in range(2):
                    b = G1.wait_full(dve, layer, f"dn{j}")
                    ts(rstd[:, 2 * j:2 * j + 2, :], views(b), 1e-5, None, ALU.add).then_inc(dr_v.h, 1)
                dve.wait_ge(dn_std.h, dn_std.at(layer, 1))
                link(nc.vector.reciprocal(rstd[:, :, :], rstd[:, :, :]))
                link(stt(y[:, 8:12, :], y[:, 8:12, :], par2[:, 24:25], rstd[:, :, :], ALU.mult, ALU.mult))
                G1.wait_drained(dve, layer, "cz1")
                gate(2)
                dve.wait_ge(y_ready.h, y_ready.at(layer, 6))
                gate(1)
                for c, br in enumerate("abc"):
                    for j in range(4):
                        b = G1.wait_full(dve, layer, f"b{br}{j}")
                        g = gates[:, 8 * c + 2 * j:8 * c + 2 * j + 2, :]
                        dst = merged[:, 2 * j:2 * j + 2, :]
                        if c == 0:
                            if j == 0:
                                G1.wait_drained(dve, layer, "mg11")
                            stt(dst, g, 1.0, views(b), ALU.add, ALU.mult).then_inc(dr_v.h, 1)
                            continue
                        u = tmp[:, j % 2, :].rearrange("p (t s) -> p t s", t=2)
                        stt(u, g, 1.0, views(b), ALU.add, ALU.mult).then_inc(dr_v.h, 1)
                        G1.wait_drained(dve, layer, f"b{br}{j}")
                        if c == 2:
                            dve.wait_ge(mgd.h, mgd.at(layer, j + 1))
                        tt_(dst, dst, u, ALU.add).then_inc(mgd.h, 1)
                for j in range(4):
                    G1.wait_drained(dve, layer, f"ou{j}")
                    stt(r1[:, 2 * j:2 * j + 2, :], xT[:, 2 * j:2 * j + 2, :], ALPHA, ou[:, 2 * j:2 * j + 2, :],
                        ALU.mult, ALU.add).then_inc(r_ready.h, 1)
                for j in range(4):
                    G1.wait_drained(dve, layer, f"pg{j}")
                    u = tmp[:, j % 2, :].rearrange("p (t s) -> p t s", t=2)
                    link(stt(u, u, 1.0, pleT[:, 2 * j:2 * j + 2, :], ALU.add, ALU.mult))
                    stt(merged[:, 2 * j:2 * j + 2, :], u, 0.5, r1[:, 2 * j:2 * j + 2, :], ALU.mult, ALU.add).then_inc(
                        r2_ready.h, 1)
                b = G1.wait_full(dve, layer, "lm")
                tt_(r1[:, :, :], merged[:, :, :], views(b)[:, 0:1, :].broadcast_to([P, DT, S]),
                    ALU.subtract).then_inc(dr_v.h, 1)
                b = G1.wait_full(dve, layer, "lv")
                ts(rstd[:, 0, :], views(b)[:, 0, :], 1e-5, None, ALU.add).then_inc(dr_v.h, 1)
                dve.wait_ge(ln_std.h, ln_std.at(layer, 1))
                link(nc.vector.reciprocal(rstd[:, 0, :], rstd[:, 0, :]))
                for t in range(DT):
                    stt(r1[:, t, :], r1[:, t, :], par[:, P_LG + t:P_LG + t + 1], rstd[:, 0, :],
                        ALU.mult, ALU.mult).then_inc(normed.h, 1)

            with dve.Fori(0, LAYERS) as layer:
                layer_body(layer)
            assert link_at[0] == vlink.per, f"vector steps of a layer: {link_at[0]}"
            turn[0], link_at[0] = LAYERS, 0

            def mixer(m):
                def drain(name):
                    return G2.wait_full(dve, m, name)

                dve.wait_ge(par2_in.h, par2_in.at(m, par2_in.per))
                for c0, c1 in ((Q_CS, Q_DS), (Q_CC, Q_CCB), (Q_CG, Q_CB + 2)):
                    ins = ts(q2[:, c0:c1], q2[:, c0:c1], 0.5)
                link(ins)
                b = drain("ms")
                ts(rs2[:, 0, :], views(b)[:, 0, :], 1e-5, None, ALU.add).then_inc(d2v.h, 1)
                dve.wait_ge(std_ready.h, std_ready.at(m, 1))
                link(nc.vector.reciprocal(rs2[:, 0, :], rs2[:, 0, :]))
                for t in range(DT):
                    ins = stt(h[:, t, :], xT[:, t, :], q2[:, Q_NM + t:Q_NM + t + 1], rs2[:, 0, :],
                              ALU.mult, ALU.mult)
                ins.then_inc(h_ready.h, 1)
                dve.wait_ge(pad0, 3)
                b = drain("gv")
                G2.wait_drained(dve, m, "gg")
                stt(gp[:, :, CONF_TAPS - 1:], ta[:, 0], 1.0, views(b), ALU.add, ALU.mult).then_inc(d2v.h, 1)
                G2.wait_drained(dve, m, "gv")

                def conv(dsts, srcs, cols, bias, k0, k1):
                    for k in range(k0, k1):
                        for dst, src, c, bb in zip(dsts, srcs, cols, bias):
                            x = src[:, k:k + S]
                            if k == 0 and bb is not None:
                                ins = ts(dst, x, q2[:, c:c + 1], q2[:, bb:bb + 1], ALU.mult, ALU.add)
                            elif k == 0:
                                ins = ts(dst, x, q2[:, c:c + 1])
                            else:
                                ins = stt(dst, x, q2[:, c + k:c + k + 1], dst, ALU.mult, ALU.add)
                        if k < k1 - 1:
                            link(ins)
                    return ins

                def conf(k0, k1):
                    return conv([gc[:, t, :] for t in range(2)], [gp[:, t, :] for t in range(2)],
                                [Q_CC + CONF_TAPS * t for t in range(2)], [Q_CCB, Q_CCB + 1], k0, k1)

                link(conf(0, 16))
                b = drain("ax")
                G2.wait_drained(dve, m, "ac")
                tt_(ap_[:, :, A_TAPS - 1:], acs_b[:, :, :], views(b), ALU.mult).then_inc(d2v.h, 1)
                G2.wait_drained(dve, m, "ax")
                conv([ac_y[:, t, :] for t in range(2)], [ap_[:, t, :] for t in range(2)],
                     [Q_CA + A_TAPS * t for t in range(2)], [None, None], 0, A_TAPS).then_inc(vlink.h, 1)
                link_at[0] += 1
                conf(16, CONF_TAPS).then_inc(cf_sum.h, 1)
                for j in range(4):
                    G2.wait_drained(dve, m, f"xb{j}")
                    conv([xc[:, t, :] for t in (2 * j, 2 * j + 1)], [xp[:, t, :] for t in (2 * j, 2 * j + 1)],
                         [Q_CS + SSD_TAPS * t for t in (2 * j, 2 * j + 1)],
                         [Q_CSB + t for t in (2 * j, 2 * j + 1)], 0, SSD_TAPS).then_inc(xc_half.h, 1)
                    if j:
                        silu_x(m, j - 1)
                b = drain("dt")
                v2 = dtt[:, 0, :].rearrange("p (t e) -> p t e", t=TT)
                tt_(v2, bank[b][:, 0:16].rearrange("p (t e) -> p t e", t=TT),
                    bc[:, 0:8].unsqueeze(1).broadcast_to([P, TT, 8]), ALU.add).then_inc(d2v.h, 1)
                G2.wait_drained(dve, m, "dt")
                stt(dtt[:, 1, :], dtt[:, 0, :], -1.0, dtt[:, 0, :], ALU.mult, ALU.min).then_inc(dt_neg.h, 1)
                dve.wait_ge(dte.h, dte.at(m, 1))
                ts(dtt[:, 3, :], dtt[:, 2, :], 1.0, None, ALU.add).then_inc(dt_w.h, 1)
                silu_x(m, 3)
                dve.wait_ge(dt_w.h, dt_w.at(m, 1))
                link(ts(dtt[:, 5, :], dtt[:, 3, :], 1.0, None, ALU.is_equal))
                dve.wait_ge(dtl.h, dtl.at(m, 1))
                tt_(dtt[:, 4, :], dtt[:, 4, :], dtt[:, 5, :], ALU.add)
                link(stt(dtt[:, 3, :], dtt[:, 3, :], -1.0, dtt[:, 5, :], ALU.add, ALU.add))
                link(nc.vector.reciprocal(dtt[:, 3, :], dtt[:, 3, :]))
                link(tt_(dtt[:, 4, :], dtt[:, 4, :], dtt[:, 3, :], ALU.mult))
                link(tt_(dtt[:, 4, :], dtt[:, 4, :], dtt[:, 2, :], ALU.mult))
                link(stt(dtt[:, 6, :], dtt[:, 0, :], 0.0, dtt[:, 4, :], ALU.max, ALU.add))
                stt(dtt[:, 7, :].rearrange("p (t e) -> p t e", t=TT),
                    dtt[:, 6, :].rearrange("p (t e) -> p t e", t=TT), -1.0,
                    bc[:, 8:16].unsqueeze(1).broadcast_to([P, TT, 8]), ALU.mult, ALU.mult).then_inc(dta.h, 1)
                dve.wait_ge(dta.h, dta.at(m, 1))
                nc.vector.tensor_copy(dtb[:, :, :, :].rearrange("p t e k -> p (t e) k"),
                                      dtt[:, 7, :].unsqueeze(2).broadcast_to([P, TT * 8, P])).then_inc(dtb_r.h, 1)
                b = drain("ab")
                dve.wait_ge(vlink.h, vlink.at(LAYERS, link_at[0]))
                tt_(cat[:, 0:2, :], views(b), ac_y[:, :, :], ALU.mult).then_inc(d2v.h, 1)
                for j in range(2):
                    b = drain(f"z{j}")
                    dve.wait_ge(z_t.h, z_t.at(m, j + 1))
                    stt(sz[:, 2 * j:2 * j + 2, :], ta[:, j], 1.0, views(b), ALU.add, ALU.mult).then_inc(d2v.h, 1)
                b = drain("acs")
                nc.vector.tensor_copy(acs[:, :, :], bank[b][:, 0:16].rearrange("p (t e) -> p t e", t=TT)).then_inc(
                    d2v.h, 1)
                G2.wait_drained(dve, m, "acs")
                for j in range(4):
                    b = drain(f"acb{j}")
                    mask = cst[:, C_MASKT:C_MASKT + S]
                    for t in range(2):
                        e = 2 * j + t
                        stt(em[:, e, 0:S], views(b)[:, t, :], acs[:, 0, e:e + 1], mask, ALU.subtract, ALU.add)
                        ins = stt(em[:, e, S:384], views(b)[:, t, P:S], acs[:, 1, e:e + 1], mask[:, 0:P],
                                  ALU.subtract, ALU.add)
                    ins.then_inc(d2v.h, 1)
                for t in range(TT):
                    b = drain(f"xt{t}")
                    tt_(xdt[:, t, :].rearrange("p (e d) -> p e d", d=HD),
                        bank[b][:, :].rearrange("p (e d) -> p e d", d=HD),
                        dtt[:, 6, 8 * t:8 * t + 8].unsqueeze(2).broadcast_to([P, 8, HD]), ALU.mult).then_inc(d2v.h, 1)
                for j in range(4):
                    dve.wait_ge(em_exp.h, em_exp.at(m, j + 1))
                    G2.wait_drained(dve, m, f"cb{j // 2}")
                    tt_(em[:, 2 * j:2 * j + 2, :], em[:, 2 * j:2 * j + 2, :],
                        cbm[:, j // 2:j // 2 + 1, :].broadcast_to([P, 2, 384]), ALU.mult).then_inc(em_r.h, 1)
                b = drain("cm")
                tt_(gc[:, :, :], gc[:, :, :], views(b)[:, 0:1, :].broadcast_to([P, 2, S]), ALU.subtract).then_inc(d2v.h, 1)
                b = drain("cv")
                ts(rs2[:, 1, :], views(b)[:, 0, :], 1e-5, None, ALU.add).then_inc(d2v.h, 1)
                for j in range(2):
                    b = drain(f"ys{j}")
                    for t in range(2):
                        k = 2 * j + t
                        ins = stt(cat[:, 2 + k, :], xc[:, k, :], q2[:, Q_DS + k:Q_DS + k + 1], views(b)[:, t, :],
                                  ALU.mult, ALU.add)
                    ins.then_inc(d2v.h, 1)
                G2.wait_drained(dve, m, "ys1")
                stt(cat[:, 2:6, :], sz[:, :, :], 0.5, cat[:, 2:6, :], ALU.mult, ALU.mult).then_inc(yz_r.h, 1)
                dve.wait_ge(cf_std.h, cf_std.at(m, 1))
                link(nc.vector.reciprocal(rs2[:, 1, :], rs2[:, 1, :]))
                for t in range(2):
                    ins = stt(gc[:, t, :], gc[:, t, :], q2[:, Q_CG + t:Q_CG + t + 1], rs2[:, 1, :], ALU.mult, ALU.mult)
                link(ins)
                for t in range(2):
                    ins = ts(gc[:, t, :], gc[:, t, :], q2[:, Q_CB + t:Q_CB + t + 1], None, ALU.add)
                ins.then_inc(cf_half.h, 1)
                b = drain("gn")
                ts(rs2[:, 2:4, :], views(b), 1e-5, None, ALU.add).then_inc(d2v.h, 1)
                dve.wait_ge(yz_std.h, yz_std.at(m, 1))
                link(nc.vector.reciprocal(rs2[:, 2:4, :], rs2[:, 2:4, :]))
                for t in range(4):
                    ins = stt(cat[:, 2 + t, :], cat[:, 2 + t, :], q2[:, Q_NW + t:Q_NW + t + 1], rs2[:, 2 + t // 2, :],
                              ALU.mult, ALU.mult)
                ins.then_inc(yn_done.h, 1)
                dve.wait_ge(cf_t.h, cf_t.at(m, 1))
                stt(cat[:, 6:8, :], yt[:, :, :], 1.0, gc[:, :, :], ALU.add, ALU.mult).then_inc(cf_done.h, 1)
                for j in range(4):
                    b = drain(f"wo{j}")
                    tt_(xT[:, 2 * j:2 * j + 2, :], xT[:, 2 * j:2 * j + 2, :], views(b), ALU.add).then_inc(d2v.h, 1)
                G2.wait_drained(dve, m, "wo3")

            def silu_x(m, j):
                dve.wait_ge(xc_t.h, xc_t.at(m, j + 1))
                stt(xc[:, 2 * j:2 * j + 2, :], xth[:, 2 * j:2 * j + 2, :], 1.0, xc[:, 2 * j:2 * j + 2, :],
                    ALU.add, ALU.mult).then_inc(xc_done.h, 1)

            def norm(n, dst, w):
                dve.wait_ge(nrm["full"].h, n)
                ts(rs2[:, 0, :], views(0)[:, 0, :], 1e-5, None, ALU.add).then_inc(nrm["eps"].h, 1)
                dve.wait_ge(nrm["std"].h, n)
                link(nc.vector.reciprocal(rs2[:, 0, :], rs2[:, 0, :]))
                for t in range(DT):
                    ins = stt(dst[:, t, :], xT[:, t, :], q2[:, w + t:w + t + 1], rs2[:, 0, :], ALU.mult, ALU.mult)
                ins.then_inc(nrm["h"].h, 1)

            def add_sums():
                for j in range(4):
                    tt_(xT[:, 2 * j:2 * j + 2, :], xT[:, 2 * j:2 * j + 2, :], views(4 + j), ALU.add).then_inc(x_up.h, 1)

            mixer(0)
            norm(1, h, Q_NF)
            with dve.Fori(0, FD // 2) as jj:
                for half in range(2):
                    dve.wait_ge(ff_t.h, jj * 2 + (half + 1))
                    stt(tb[:, half], ta[:, half], 1.0, views(2 * half), ALU.add, ALU.mult).then_inc(ff_g.h, 1)
                    dve.wait_ge(ff_g.h, jj * 2 + (half + 1))
                    dve.wait_ge(ff_full.h, jj * 4 + (2 * half + 2))
                    stt(hf[:, half], tb[:, half], 0.5, views(2 * half + 1), ALU.mult, ALU.mult).then_inc(ff_h.h, 1)
            dve.wait_ge(ff_t.h, FD)
            stt(tb[:, 0], ta[:, 0], 1.0, views(0), ALU.add, ALU.mult).then_inc(ff_g.h, 1)
            dve.wait_ge(ff_g.h, FD)
            dve.wait_ge(ff_full.h, 2 * FD)
            stt(hf[:, 0], tb[:, 0], 0.5, views(1), ALU.mult, ALU.mult).then_inc(ff_h.h, 1)
            dve.wait_ge(ff_down.h, FD)
            add_sums()
            dve.wait_ge(x_up.h, 4)
            mixer(1)
            norm(2, h, Q_NF)

            def spread(x):
                return x.broadcast_to([P, TT, 8])

            desc = cst[:, C_DESC:C_DESC + 8].unsqueeze(1).broadcast_to([P, TT, 8])
            dve.wait_ge(rt_full.h, 1)
            link(nc.vector.tensor_copy(lg[:, :, 0, :], bank[1][:, 0:16].rearrange("p (t e) -> p t e", t=TT)))

            def choose(src, to, top):
                link(nc.vector.tensor_reduce(lg[:, :, 4, top:top + 1], lg[:, :, src, :], AX.X, ALU.max))
                link(tt_(lg[:, :, to, :], lg[:, :, src, :], spread(lg[:, :, 4, top:top + 1]), ALU.is_equal))
                link(tt_(lg[:, :, to, :], lg[:, :, to, :], desc, ALU.mult))
                link(nc.vector.tensor_reduce(lg[:, :, 4, 2:3], lg[:, :, to, :], AX.X, ALU.max))
                link(tt_(lg[:, :, to, :], lg[:, :, to, :], spread(lg[:, :, 4, 2:3]), ALU.is_equal))

            choose(0, 1, 0)
            link(stt(lg[:, :, 2, :], lg[:, :, 1, :], -3e38, lg[:, :, 0, :], ALU.mult, ALU.add))
            choose(2, 3, 1)
            tt_(lg[:, :, 5, 0:1], lg[:, :, 4, 1:2], lg[:, :, 4, 0:1], ALU.subtract).then_inc(rt_top.h, 1)
            tt_(chosen[:, :, :], lg[:, :, 1, :], lg[:, :, 3, :], ALU.add).then_inc(rt_mask.h, 1)
            dve.wait_ge(rt_exp.h, 1)
            link(ts(lg[:, :, 7, 2:3], lg[:, :, 6, 0:1], 1.0, None, ALU.add))
            link(nc.vector.reciprocal(lg[:, :, 7, 0:1], lg[:, :, 7, 2:3]))
            link(tt_(lg[:, :, 7, 1:2], lg[:, :, 6, 0:1], lg[:, :, 7, 0:1], ALU.mult))
            tt_(lg[:, :, 1, :], lg[:, :, 1, :], spread(lg[:, :, 7, 0:1]), ALU.mult)
            link(tt_(lg[:, :, 3, :], lg[:, :, 3, :], spread(lg[:, :, 7, 1:2]), ALU.mult))
            link(tt_(gmat[:, :, :], lg[:, :, 1, :], lg[:, :, 3, :], ALU.add))
            link(ts(gmat[:, :, :], gmat[:, :, :], 0.5))
            dve.wait_ge(rt_place.h, 1)
            link(tt_(place[:, :, :], bank[2][:, 0:16].rearrange("p (t e) -> p t e", t=TT), chosen[:, :, :], ALU.mult))
            link(ts(place[:, :, :], place[:, :, :], -1.0, None, ALU.add))

            slots = cst[:, C_IOTA:C_IOTA + P].unsqueeze(1).broadcast_to([P, TT, P])

            def pick_slots(turn, where, e):
                tt_(pick[:, :, :], slots, where[:, :, bass.ds(e, 1)].broadcast_to([P, TT, P]),
                    ALU.is_equal).then_inc(picked.h, 1)
                dve.wait_ge(picked.h, picked.at(turn, 1))

            def pick_gates(e):
                tt_(pickg[:, :, :], pick[:, :, :], gmat[:, :, bass.ds(e, 1)].broadcast_to([P, TT, P]),
                    ALU.mult).then_inc(picked.h, 1)

            pick_slots(0, place, 0)
            pick_gates(0)
            ts(place2[:, :, :], place[:, :, :], -float(P), None, ALU.add)
            link(ts(over[:, 0, :], bank[2][:, 16:24], P + 0.5, None, ALU.is_gt))
            link(nc.vector.tensor_reduce(over[:, 2, 0:1], over[:, 0, :], AX.X, ALU.add))
            link(tt_(over[:, 0, :], over[:, 0, :], cst[:, C_DESC:C_DESC + 8], ALU.mult))
            for k in range(OVER):
                link(nc.vector.tensor_reduce(over[:, 1, 0:1], over[:, 0, :], AX.X, ALU.max))
                link(ts(over[:, 2, k + 1:k + 2], over[:, 1, 0:1], -1.0, float(EXPERTS), ALU.mult, ALU.add))
                link(stt(over[:, 0, :], over[:, 0, :], over[:, 1, 0:1], over[:, 0, :], ALU.is_lt, ALU.mult))
            ts(over_n[:, :], over[:, 2, 0:4], float(EXPERTS - 1), None, ALU.min).then_inc(over_ready.h, 1)
            dve.wait_ge(htok_ready.h, 4)
            dve.wait_ge(over_ready.h, 1)
            nc.vector.memset(over[:, 3, :], 0.0).then_inc(comb.h, 4)

            def hidden(turn, s):
                dve.wait_ge(mo_t.h, turn * HS + s + 1)
                stt(tb[:, 0], ta[:, 0], 1.0, views(0), ALU.add, ALU.mult).then_inc(mo_g.h, 1)
                dve.wait_ge(mo_g.h, turn * HS + s + 1)
                dve.wait_ge(u_full.h, turn * HS + s + 1)
                tt_(hd[:, :], tb[:, 0].rearrange("p t s -> p (t s)"), bank[1][:, :], ALU.mult).then_inc(mo_h.h, 1)

            def expert(turn, ahead=None):
                if ahead is not None:
                    dve.wait_ge(xg_full.h, xg_full.at(turn, 2))
                    dve.wait_ge(picked.h, picked.at(turn, 2))
                    pick_slots(ahead, place, ahead)
                hidden(turn, 0)
                with dve.Fori(0, HS - 1) as s:
                    hidden(turn, s + 1)
                if ahead is not None:
                    dve.wait_ge(put_full.h, put_full.at(turn, 1))
                    pick_gates(ahead)
                dve.wait_ge(ye_full.h, ye_full.at(turn, 1))
                nc.vector.tensor_copy(ye[:, 512:D], bank[4][:, :]).then_inc(ye_v.h, 1)
                for j, b in enumerate((0, 1, 2, 7)):
                    dve.wait_ge(comb_full.h, comb_full.at(turn, j + 1))
                    tt_(xT[:, 2 * j:2 * j + 2, :], xT[:, 2 * j:2 * j + 2, :], views(b), ALU.add).then_inc(comb.h, 1)

            with dve.Fori(0, EXPERTS - 1) as e:
                expert(e, e + 1)
            expert(EXPERTS - 1)
            dve.wait_ge(comb.h, comb.at(EXPERTS, 4))
            n_over = dve.value_load(over_n[0:1, 0:1], min_val=0, max_val=OVER)
            with dve.Fori(0, OVER) as k:
                with dve.If(n_over > k):
                    e = dve.value_load(over_n[0:1, bass.ds(k + 1, 1)], min_val=0, max_val=EXPERTS - 1)
                    turn2 = k + EXPERTS
                    pick_slots(turn2, place2, e)
                    pick_gates(e)
                    expert(turn2)
                    dve.wait_ge(comb.h, comb.at(turn2 + 1, 4))
                    nc.vector.memset(over[:, 3, :], 0.0)
            nc.vector.memset(over[:, 3, :], 0.0).then_inc(x_done.h, 1)
            dve.wait_ge(x_done.h, 1)
            norm(3, cat, Q_NL)
            for n in range(4):
                dve.wait_ge(fin_full.h, n + 1)
                nc.vector.tensor_copy(h[:, 2 * n:2 * n + 2, :], views(n)).then_inc(out_full.h, 1)

        @block.gpsimd
        def _(pool):
            nc.gpsimd.memset(ones[:, 0], 1.0 / D).then_inc(ones_set, 1)
            nc.gpsimd.memset(ones[:, 1], 1.0 / Q_LORA).then_inc(ones_set, 1)
            nc.gpsimd.memset(ones[:, 2], 1.0 / KV_LORA).then_inc(ones_set, 1)
            nc.gpsimd.memset(ones[:, 3], 1.0 / P).then_inc(ones_set, 1)
            nc.gpsimd.memset(zeros[:, 0:256], 0.0).then_inc(w_free.h, RING)
            nc.gpsimd.memset(kr[0:HD, :], 0.0).then_inc(ones_set, 1)
            nc.gpsimd.memset(zeros[:, 256:512], 0.0).then_inc(ones_set, 1)

            with pool.Fori(0, LAYERS) as layer:
                pool.wait_ge(x_ready.h, x_ready.at(layer, DT))
                pool.dma_start(par[:, :], a["params1"][bass.ds(layer, 1), :, :].rearrange("o p c -> (o p) c")).then_inc(
                    par_in.h, 16)

            for m in range(LAYERS):
                if m == 0:
                    pool.wait_ge(x_ready.h, b1_end)
                    nc.gpsimd.memset(gp[:, :, 0:CONF_TAPS - 1], 0.0).then_inc(pad0, 1)
                    nc.gpsimd.memset(ap_[:, :, 0:A_TAPS - 1], 0.0).then_inc(pad0, 1)
                    nc.gpsimd.memset(xp[:, :, 0:SSD_TAPS - 1], 0.0).then_inc(pad0, 1)
                else:
                    pool.wait_ge(x_up.h, 4)

                pool.dma_start(q2[:, :], a["params2"][m, :, :]).then_inc(par2_in.h, 16)


_LARGE = ['x', 'p', 'w_in', 'mla_w_uq', 'mla_w_ukv', 'w_branch_a', 'w_branch_b', 'w_branch_c', 'w_merge', 'w_out',
          'w_ple_gate', 'w_ple', 'w_in_2', 'w_out_2', 'ffn_w_gate_2', 'ffn_w_up_2', 'ffn_w_down_2', 'moe_router_2',
          'moe_w_gate_2', 'moe_w_up_2', 'moe_w_down_2']
_SMALL = ['mla_q_norm_g', 'mla_kv_norm_g', 'diff_lambda', 'diff_subln_g', 'b_merge', 'ln_g', 'ln_b', 'norm_mix_2',
          'conv_a_w_2', 'conv_ssd_w_2', 'conv_ssd_b_2', 'dt_bias_2', 'a_log_2', 'd_skip_2', 'ssd_norm_w_2',
          'conv_conf_w_2', 'conv_conf_b_2', 'conf_ln_g_2', 'conf_ln_b_2', 'norm_ffn_2', 'norm_final_2']


def kernel(**inputs):
    import concourse.bacc as _bacc
    from concourse.bass_utils import run_bass_kernel_spmd as _run

    nc = _bacc.Bacc("TRN2", target_bir_lowering=False, num_devices=1)
    table = constants()
    v = {name: np.asarray(inputs[name]) for name in _SMALL}
    given = {name: np.ascontiguousarray(inputs[name]) for name in _LARGE}
    given["cst"] = table
    lam = np.broadcast_to(table[0, C_LAM:C_LAM + 4].reshape(LAYERS, 1, 2), (LAYERS, P, 2))
    given["params1"] = np.ascontiguousarray(np.concatenate(
        [by_feature(v[n]) for n in ("mla_q_norm_g", "mla_kv_norm_g", "diff_subln_g", "b_merge", "ln_g", "ln_b")]
        + [lam, on_all(v["diff_lambda"].reshape(LAYERS, -1))], axis=2))
    last = np.broadcast_to(v["norm_final_2"][None], (LAYERS, D))
    given["params2"] = np.ascontiguousarray(np.concatenate(
        [by_feature(v[n]) for n in ("norm_mix_2", "conv_a_w_2", "conv_ssd_w_2", "conv_ssd_b_2")]
        + [by_feature(np.repeat(v["d_skip_2"], HD, axis=1))]
        + [by_feature(v[n]) for n in ("ssd_norm_w_2", "conv_conf_w_2", "conv_conf_b_2", "conf_ln_g_2",
                                      "conf_ln_b_2", "norm_ffn_2")]
        + [by_feature(last), on_all(v["dt_bias_2"]), on_all(v["a_log_2"])], axis=2))
    arrays, args = {}, {}
    for name, v in given.items():
        arrays[f"in_{name}_dram"] = v
        args[name] = nc.dram_tensor(f"in_{name}_dram", v.shape, mybir.dt.from_np(v.dtype), kind="ExternalInput").ap()
    out = nc.dram_tensor("out_0_dram", (1, S, D), F32, kind="ExternalOutput").ap()
    build_kernel(nc, args, out)
    r = _run(nc, [arrays], core_ids=[0])
    return r.results[0]["out_0_dram"]
```

```python
from contextlib import ExitStack

import numpy as np

import concourse.bass as bass
from concourse import mybir

F32 = mybir.dt.float32
ACT = mybir.ActivationFunctionType
ALU = mybir.AluOpType
AX = mybir.AxisListType

P = 128
S = 256
TT = S // P
D = 1024
DT = D // P
LAYERS = 2
HEADS = 8
HD = 64
ROPE = 32
MLA_D = HD + ROPE
DIFF_HEADS = 4
ALPHA = (2 * LAYERS) ** 0.25
Q_LORA, KV_LORA, PLE = 384, 256, 256
FF = 2816
EXPERTS = 8
TOP = 2
FFE = 3584
CONF_TAPS, SSD_TAPS, A_TAPS = 31, 4, 3
RING = 3
RING_E = 6
SLOT = 2048
BANKS = 4
NEG = -1e30

_n = HEADS + DIFF_HEADS
_slopes = [2.0 ** (-8.0 * (i + 1) / _n) for i in range(_n)]
_diff_at = [i * (_n // DIFF_HEADS) for i in range(DIFF_HEADS)]
DIFF_SLOPES = [_slopes[i] for i in _diff_at]
MOBA_SLOPES = [s for i, s in enumerate(_slopes) if i not in _diff_at]

C_IDENT, C_DIST, C_MASK, C_TRI, C_MASKT, C_ROT, C_COS, C_SIN, C_LAM, C_DESC, C_IOTA, C_END = (
    int(v) for v in np.cumsum([0, P, S, S, S, S, MLA_D, S, S, 4, 8, P]))


P_GQ, P_GKV, P_SUB, P_BM, P_LG, P_LB, P_LAM, P_LQK, P1_END = (
    int(v) for v in np.cumsum([0, 3, 2, 1, 24, 8, 8, 2, 4 * HD]))
Q_NM, Q_CA, Q_CS, Q_CSB, Q_DS, Q_NW, Q_CC, Q_CCB, Q_CG, Q_CB, Q_NF, Q_NL, Q_BC, P2_END = (
    int(v) for v in np.cumsum([0, 8, 2 * A_TAPS, 8 * SSD_TAPS, 8, 4, 4, 2 * CONF_TAPS, 2, 2, 2, 8, 8, 16]))


def by_feature(v):
    if v.ndim == 2:
        v = v[:, None, :]
    layers, taps, n = v.shape
    return v.reshape(layers, taps, n // P, P).transpose(0, 3, 2, 1).reshape(layers, P, -1)


def on_all(v):
    return np.broadcast_to(v[:, None, :], (v.shape[0], P, v.shape[1]))


def constants():
    c = np.zeros((P, C_END), np.float32)
    p, k = np.arange(P)[:, None], np.arange(P)[None, :]
    c[:, C_IDENT:C_IDENT + P] = p == k
    c[:, C_DIST:C_DIST + P] = k - P - p
    c[:, C_DIST + P:C_DIST + S] = np.where(k <= p, k - p, NEG)
    c[:, C_MASK + P:C_MASK + S] = np.where(k <= p, 0.0, NEG)
    c[:, C_TRI:C_TRI + P] = p <= k
    c[:, C_TRI + P:C_TRI + S] = 1.0
    c[:, C_MASKT:C_MASKT + P] = np.where(k >= p, 0.0, NEG)
    half = ROPE // 2
    for m in range(ROPE):
        if m < half:
            c[HD + m + half, C_ROT + HD + m] = -1.0
        else:
            c[HD + m - half, C_ROT + HD + m] = 1.0
    freqs = np.float32(10000.0) ** (-np.arange(0, ROPE, 2, dtype=np.float32) / np.float32(ROPE))
    ang = np.arange(S, dtype=np.float32)[None, :] * freqs[:, None].astype(np.float32)
    c[HD:MLA_D, C_COS:C_COS + S] = np.tile(np.cos(ang), (2, 1))
    c[HD:MLA_D, C_SIN:C_SIN + S] = np.tile(np.sin(ang), (2, 1))
    for li in range(LAYERS):
        lam = 0.8 - 0.6 * np.exp(-0.3 * li)
        c[:, C_LAM + 2 * li] = lam
        c[:, C_LAM + 2 * li + 1] = 1.0 - lam
    c[:, C_DESC:C_DESC + 8] = np.arange(8, 0, -1)
    c[:, C_IOTA:C_IOTA + P] = k
    return c


class Signal:

    def __init__(self, handle, per=0):
        self.h, self.per = handle, per

    def at(self, turn, n):
        return turn * self.per + n


class Groups:

    def __init__(self, table, full, drained_a, drained_v, turns_before=0):
        self.names = [n for n, _ in table]
        self.owner = [o for _, o in table]
        assert len(set(self.names)) == len(self.names)
        self.full, self.drained = full, {"a": drained_a, "v": drained_v}

    def index(self, name):
        return self.names.index(name)

    def nth(self, g):
        return sum(o == self.owner[g] for o in self.owner[:g + 1])

    def count(self, owner):
        return sum(o == owner for o in self.owner)

    def wait_full(self, eng, turn, name):
        eng.wait_ge(self.full.h, self.full.at(turn, self.index(name) + 1))
        return self.index(name) % BANKS


    def wait_drained(self, eng, turn, name):
        g = self.index(name)
        s = self.drained[self.owner[g]]
        eng.wait_ge(s.h, s.at(turn, self.nth(g)))

    def wait_bank(self, eng, turn, name):
        g = self.index(name)
        if g >= BANKS:
            self.wait_drained(eng, turn, self.names[g - BANKS])
        return g % BANKS


BATCHES = [("moba", 0), ("moba", 1), ("diff", 0), ("diff", 1), ("mla", 0), ("mla", 1)]

ORDER1 = [
    ("aq0", "a"), ("aq1", "a"), ("ak0", "v"), ("ak1", "v"), ("av0", "a"), ("av1", "a"), ("A", 0),
    ("dq0", "a"), ("dq1", "a"), ("B", 0), ("dk0", "v"), ("dk1", "v"), ("V", 0), ("A", 1),
    ("dv0", "a"), ("dv1", "a"), ("B", 1), ("mc0", "a"), ("mc1", "a"), ("V", 1), ("A", 2),
    ("mc2", "a"), ("pt", "a"), ("pl0", "a"), ("pl1", "a"), ("ms", "v"), ("B", 2), ("pl2", "a"),
    ("pl3", "a"), ("V", 2), ("A", 3), ("uq0", "a"), ("uq1", "a"), ("uq2", "a"), ("uq3", "a"),
    ("rk", "v"), ("rq0", "v"), ("rq1", "v"), ("kn0", "a"), ("kn1", "a"), ("kn2", "a"),
    ("kn3", "a"), ("rq2", "v"), ("rq3", "v"), ("mv0", "v"), ("mv1", "v"), ("B", 3),
    ("az0", "v"), ("az1", "v"), ("V", 3), ("A", 4), ("bz0", "v"), ("bz1", "v"), ("B", 4),
    ("cz0", "v"), ("cz1", "v"), ("V", 4), ("A", 5), ("dn0", "v"), ("dn1", "v"),
    ("mg0", "a"), ("mg1", "a"), ("B", 5), ("mg2", "a"), ("mg3", "a"), ("V", 5),
] + [(f"ba{j}", "v") for j in range(4)] + [
    x for c, br in ((1, "b"), (2, "c"))
    for x in [(f"mg{4 * c + j}", "a") for j in range(4)] + [(f"b{br}{j}", "v") for j in range(4)]] + [
    (f"ou{j}", "a") for j in range(4)] + [(f"pg{j}", "a") for j in range(4)] + [
    ("lm", "v"), ("lv", "v")]
STEPS = ("A", "B", "V")

UNITS1 = (
    [("w_in", c, 256, 8) for c in range(0, 1536, 256)]
    + [("w_in", c, 256, 8) for c in range(3232, 3232 + 1536, 256)]
    + [("w_in", 2048, 256, 8), ("w_in", 2304, 256, 8), ("w_in", 2560, 160, 8)]
    + [("p", 0, 256, 2), ("w_ple", 0, 1024, 2)]
    + [("w_uq", c, 192, 3) for c in range(0, 768, 192)] + [("w_ukv", 0, 1024, 2)]
    + [("w_in", c, 256, 8) for c in (1536, 1792, 2720, 2976, 4768, 5024)]
    + [x for n, w in enumerate(("w_a", "w_b", "w_c"))
       for x in [("w_merge", 1024 * n + c, 256, 8) for c in range(0, 1024, 256)]
       + [(w, c, 512, 4) for c in (0, 512)]]
    + [("w_out", c, 256, 8) for c in range(0, 1024, 256)]
    + [("w_pg", c, 256, 8) for c in range(0, 1024, 256)])
assert len(UNITS1) % RING == 0
SPLIT1 = ([f"{h}{x}{n}" for h in "ad" for x in "qkv" for n in range(2)] + ["mc0", "mc1"]
          + [f"{z}z{n}" for z in "abc" for n in range(2)] + [f"mg{j}" for j in range(12)])
SPLIT2 = ["gg", "gv", "ac", "ax", "xb0", "xb1", "xb2", "xb3", "ab", "z0", "z1"]
KINDS1 = ["split" if name in ("w_in", "w_merge") and cols == 256 else "plain" for name, _, cols, _ in UNITS1]
assert KINDS1.count("split") == len(SPLIT1) and len(SPLIT1) % 2 == 0
SPLIT_AT = [u for u, kind in enumerate(KINDS1) if kind == "split"]

ORDER2 = ([("ms", "v"), ("gg", "a"), ("gv", "v"), ("ac", "a"), ("ax", "v")]
          + [(f"xb{j}", "a") for j in range(4)]
          + [("dt", "v"), ("ab", "v"), ("cm", "v"), ("z0", "v"), ("z1", "v"), ("cv", "v"), ("acs", "v")]
          + [(f"acb{j}", "v") for j in range(4)]
          + [("xt0", "v"), ("xt1", "v"), ("cb0", "a"), ("cb1", "a"),
             ("ys0", "v"), ("ys1", "v"), ("gn", "v")]
          + [(f"wo{j}", "v") for j in range(4)])


def half_of(unit, t):
    return unit.rearrange("p (k t n) -> p t k n", t=2, n=P)[:, t]


def quarter(unit, k):
    return unit[:, k * 512:(k + 2) * 512]


def build_kernel(nc, a, out):
    ctx = ExitStack()
    with ctx:
        def sb(name, shape, stack=ctx):
            return stack.enter_context(nc.sbuf_tensor(name, shape, F32))

        def sb_r(name, shape, stack=ctx):
            return stack.enter_context(nc.sbuf_tensor(name, shape, mybir.dt.float32r))

        def sem(name):
            return ctx.enter_context(nc.semaphore(name))

        def signal(name, per=0):
            return Signal(sem(name), per)

        bank = [ctx.enter_context(nc.psum_tensor(f"bank{i}", [P, 512], F32)) for i in range(8)]
        m0 = ExitStack()
        ring = sb("ring", [P, RING, SLOT], m0)
        whi = sb_r("weights_high", [P, 2, SLOT], m0)
        wlo = sb_r("weights_low", [P, 2, SLOT], m0)
        m0.close()
        ring_e = sb("ring_experts", [P, RING + 4, SLOT])
        cst = sb("cst", [P, C_END])
        xT = sb("xT", [P, DT, S])
        m0 = ExitStack()
        xh = sb_r("x_high", [P, DT, S], m0)
        m0.close()
        sq = sb("sq", [P, DT, S])
        ones = sb("ones", [P, 4, P])
        room = sb("room", [P, 4])
        zeros = ctx.enter_context(nc.sbuf_tensor("zeros", [P, 512], mybir.dt.bfloat16))
        ident = cst[:, C_IDENT:C_IDENT + P]
        ONES = {D: ones[:, 0], Q_LORA: ones[:, 1], KV_LORA: ones[:, 2], P: ones[:, 3]}

        m1 = ExitStack()
        aqk = sb("aqk", [P, 8, S], m1)
        dqk = sb("dqk", [P, 8, S], m1)
        av = sb("av", [P, TT, 512], m1)
        dv = sb("dv", [P, TT, 512], m1)
        cq = sb("cq", [P, 5, S], m1)
        cn = sb("cn", [P, 5, S], m1)
        kr = sb("kr", [P, S], m1)
        qb = sb("qb", [P, HEADS, S], m1)
        kb = sb("kb", [P, HEADS, S], m1)
        mv = sb("mv", [P, TT, 512], m1)
        rot = sb("rot", [P, 2, 512], m1)
        zs = sb("zs", [P, 12, S], m1)
        gates = sb("gates", [P, 8, S], m1)
        xl = sb_r("x_low", [P, DT, S], m1)
        y = sb("y", [P, 12, S], m1)
        sc = sb("sc", [P, 4, 384], m1)
        pT = sb("pT", [P, 4, 384], m1)
        peT = sb("peT", [P, 2, S], m1)
        tmp = sb("tmp", [P, 2, 512], m1)
        rstd = sb("rstd", [P, 4, S], m1)
        nmax = sb("nmax", [P, 8], m1)
        psum_ = sb("sums", [P, 8], m1)
        pinv = sb("pinv", [P, 8], m1)
        lam_p = sb("lam_p", [P, 2, HD], m1)
        lam = sb("lam", [P, 4], m1)
        par = sb("par", [P, P1_END], m1)
        par2 = sb("par2", [P, 32], m1)
        pleT, merged = aqk, dqk
        r1, ou = qb, kb
        m1.close()

        m2 = ExitStack()
        h = sb("h", [P, DT, S], m2)
        cat = sb("cat", [P, DT, S], m2)
        rs2 = sb("rs2", [P, 4, S], m2)
        q2 = sb("q2", [P, P2_END], m2)
        bc = q2[:, Q_BC:Q_BC + 16]
        hf = sb("hf", [P, 2, 2, S], m2)
        ta = sb("ta", [P, 2, 2, S], m2)
        tb = sb("tb", [P, 2, 2, S], m2)
        lg = sb("lg", [P, TT, 8, 8], m2)
        gmat = sb("gmat", [P, TT, 8], m2)
        chosen = sb("chosen", [P, TT, 8], m2)
        place = sb("place", [P, TT, 8], m2)
        place2 = sb("place2", [P, TT, 8], m2)
        over = sb("over", [P, 4, 8], m2)
        over_n = m2.enter_context(nc.sbuf_tensor("over_n", [P, 4], mybir.dt.int32))
        m3 = ExitStack()
        gp = sb("gp", [P, 2, CONF_TAPS - 1 + S], m3)
        gc = sb("gc", [P, 2, S], m3)
        ap_ = sb("ap_", [P, 2, A_TAPS - 1 + S], m3)
        acs_b = sb("ac_sb", [P, 2, S], m3)
        ac_y = sb("ac_y", [P, 2, S], m3)
        xp = sb("xp", [P, 8, SSD_TAPS - 1 + S], m3)
        xc = sb("xc", [P, 8, S], m3)
        sz = sb("sz", [P, 4, S], m3)
        dtt = sb("dtt", [P, 8, TT * 8], m3)
        dtb = sb("dtb", [P, TT, 8, P], m3)
        acs = sb("acs", [P, TT, 8], m3)
        em = sb("em", [P, 8, 384], m3)
        cbm = sb("cbm", [P, 2, 384], m3)
        xdt = sb("xdt", [P, TT, 512], m3)
        xth = sb("xth", [P, 8, S], m3)
        yt = sb("yt", [P, 2, S], m3)
        hh = sb_r("h_high", [P, DT, S], m3)
        hl = sb_r("h_low", [P, DT, S], m3)
        m3.close()
        htok = sb("htok", [P, TT, D], m2)
        pick = sb("pick", [P, TT, P], m2)
        pickg = sb("pickg", [P, TT, P], m2)
        put = sb("put", [P, S], m2)
        hd = sb("hd", [P, 512], m2)
        hdT = sb("hdT", [P, 4, P], m2)
        ye = hf[:, :, :, :].rearrange("p a b s -> p (a b s)")
        xgh = sb_r("gathered_high", [P, DT, P], m2)
        xgl = sb_r("gathered_low", [P, DT, P], m2)
        ewh = sb_r("expert_weights_high", [P, 2, SLOT], m2)
        ewl = sb_r("expert_weights_low", [P, 2, SLOT], m2)
        m2.close()
        landed = [signal(f"w_landed{i}", 16 * len(UNITS1) // RING) for i in range(RING)]
        landed_e = [signal(f"expert_w_landed{i}") for i in range(RING_E)]
        w_free = signal("w_slot_free", KINDS1.count("plain"))
        e_free = signal("expert_slot_free", 14)
        eh_done, ev_done, ep_done, e_used = (signal(n, k) for n, k in (
            ("expert_w_high_done", 56), ("expert_w_low_vector", 28), ("expert_w_low_pool", 28),
            ("expert_first_unit_used", 14)))
        hi_done, lo_done = (signal(n, 2 * len(SPLIT1)) for n in ("w_high_done", "w_low_done"))
        used = signal("split_half_used", len(SPLIT1))
        xh_ready, xl_ready = signal("x_high_ready", 4), signal("x_low_ready", 4)
        h_part, hh_ready, hl_ready = (signal(n, 4) for n in ("h_tiles_ready", "h_high_ready", "h_low_ready"))
        first_units = len(UNITS1) * LAYERS

        def unit_wait(eng, n):
            eng.wait_ge(landed[n % RING].h, 16 * (n // RING + 1))

        cst_in, x_in = sem("constants_landed"), sem("x_landed")
        ones_set = sem("ones_set")
        x0_full = sem("x_transposed")
        x_ready = signal("x_ready", DT)
        par_in = signal("params_landed", 16)
        full = signal("group_full", sum(n not in STEPS for n, _ in ORDER1))
        dr_a = signal("drained_by_scalar", sum(o == "a" for _, o in ORDER1))
        dr_v = signal("drained_by_vector", sum(o == "v" for _, o in ORDER1))
        G1 = Groups([x for x in ORDER1 if x[0] not in STEPS], full, dr_a, dr_v)
        nb = len(BATCHES)
        sc_full, sc_max, p_exp, p_ready, p_turned, pT_ready, pv_full, y_ready = (
            signal(n, nb) for n in ("scores_full", "scores_max", "probs_exp", "probs_ready",
                                    "probs_turned", "probsT_ready", "pv_full", "y_ready"))
        z_tanh = signal("z_tanh", 6)
        ms_std, ms_done = (signal(n, 1) for n in ("latent_std", "latent_normed"))
        dn_sq, dn_std = (signal(n, 1) for n in ("diff_squares", "diff_std"))
        gated = signal("branch_gated", 3)
        dt_neg, dt_w = signal("dt_neg_abs", 1), signal("dt_exp_plus_1", 1)
        lamp, lame = signal("lambda_sums", 1), signal("lambda_exp", 1)
        halfb = signal("half_bias", 1)
        rope_q, kroped, kall = signal("q_roped", 4), signal("k_roped", 1), signal("k_rope_spread", 1)
        mgd = signal("merged", 8)
        r_ready = signal("r_ready", 4)
        r2_ready = signal("r_gated", 4)
        ln_sq, ln_std, normed = (signal(n, k) for n, k in (
            ("ln_squares", 4), ("ln_std", 1), ("ln_scaled", DT)))
        centred = signal("ln_centred", 3)
        vlink = signal("vector_step", 34)

        def unit_view(slot, cols, k):
            return ring[:, slot, 0:k * cols].rearrange("p (k n) -> p k n", n=cols)

        def slot_e(u):
            return (u + RING) % RING_E

        def expert_unit(u, cols, k):
            return ring_e[:, slot_e(u), 0:k * cols].rearrange("p (k n) -> p k n", n=cols)

        def views(b, n=2):
            return bank[b][:, :].rearrange("p (t s) -> p t s", t=n)

        units2 = []
        FD, FJ = FF // S, FFE // S
        for i in range(LAYERS):
            units2 += [("w_in_2", i, c, 256, 8) for c in (2568, 2312, 256, 512)]
            units2 += [("w_in_2", i, c, 256, 8) for c in range(1280, 2304, 256)]
            units2 += [("w_in_2", i, 2304, 8, 8), ("w_in_2", i, 0, 256, 8)]
            units2 += [("w_in_2", i, c, 256, 8) for c in (768, 1024)]
            units2 += [("w_out_2", i, c, 256, 8) for c in range(0, 1024, 256)]
            if i == 0:
                for steps in [(j, j + 1) for j in range(0, FD - 1, 2)] + [(FD - 1,)]:
                    for j in steps:
                        units2 += [("ffn_w_gate_2", 0, j * S, 256, 8), ("ffn_w_up_2", 0, j * S, 256, 8)]
                    units2 += [("ffn_w_down_2", 0, j * S, 1024, 2) for j in steps]
            else:
                units2 += [("moe_router_2", 0, 0, 8, 8)]
        assert len(units2) % RING == 0 and FFE % 512 == 0
        kinds2 = ["split" if cols == 256 and name in ("w_in_2", "ffn_w_gate_2", "ffn_w_up_2") else "plain"
                  for name, _, _, cols, _ in units2]
        split_at2 = [u for u, kind in enumerate(kinds2) if kind == "split"]
        first_splits = LAYERS * len(SPLIT1)
        last_plain = len(units2) - RING

        HS = FFE // 512
        KINDS_E = (["split"] * 4 + ["split", "plain", "split", "split", "plain", "split"] * (HS - 1) + ["plain"] * 2)
        PASS_E = (("moe_w_gate_2", 0), ("moe_w_down_2", 0), ("moe_w_gate_2", 1),
                  ("moe_w_up_2", 0), ("moe_w_down_2", 1), ("moe_w_up_2", 1))
        EARLY_PLAIN, EARLY_V, EARLY_P = 5, 2, 4

        def low_at(q):
            return (ev_done, ep_done)[q % 2], (EARLY_V, EARLY_P)[q % 2] + 2 * (q // 2 + 1)

        def slot_freed(kinds, u):
            v = u - RING
            if kinds[v] == "plain":
                return w_free, RING + kinds[:v + 1].count("plain")
            return lo_done, 2 * kinds[:v + 1].count("split")
        U_MOE = 3 * FJ
        OVER = TOP * S // (P + 1)
        ffn_at = 16

        def source(name, layer, c0, cols, k):
            if name in ("ffn_w_down_2",):
                return a[name][layer, c0:c0 + k * P, :].rearrange("(k p) n -> p k n", p=P)
            return a[name][layer, 0:k * P, c0:c0 + cols].rearrange("(k p) n -> p k n", p=P)

        block = ctx.enter_context(nc.Block())

        out_full, out_done = signal("out_rows_ready"), sem("out_written")
        full2 = signal("group2_full", len(ORDER2))
        over_ready = signal("over_list_ready")

        @block.sync
        def _(sp):
            sp.dma_start(cst[:, :], a["cst"]).then_inc(cst_in, 16)
            sp.dma_start(sq[:, :, :].rearrange("p (t a) s -> p t (a s)", t=TT),
                         a["x"][0].rearrange("(t p) d -> p t d", p=P)).then_inc(x_in, 16)
            with sp.Fori(0, LAYERS) as layer:
                for u, (name, c0, cols, k) in enumerate(UNITS1):
                    s, n = slot_freed(KINDS1, u) if u >= RING else (w_free, u + 1)
                    sp.wait_ge(s.h, s.at(layer, n))
                    src = {"p": "p", "w_a": "w_branch_a", "w_b": "w_branch_b", "w_c": "w_branch_c",
                           "w_pg": "w_ple_gate", "w_uq": "mla_w_uq", "w_ukv": "mla_w_ukv"}.get(name, name)
                    dram = a[src][bass.ds(layer, 1), 0:k * P, c0:c0 + cols] if name != "p" else \
                        a["p"][bass.ds(layer, 1), 0, :, :]
                    dram = dram.rearrange("o (k p) n -> p (o k) n", p=P)
                    sp.dma_start(unit_view(u % RING, cols, k), dram).then_inc(landed[u % RING].h, 16)
            for u, unit in enumerate(units2):
                s, n = slot_freed(kinds2, u) if u >= RING else (w_free, u + 1)
                sp.wait_ge(s.h, s.at(LAYERS, n))
                sp.dma_start(unit_view(u % RING, unit[3], unit[4]), source(*unit)).then_inc(
                    landed[u % RING].h, 16)
            def at_step(first, n):
                return slice(first, first + n) if isinstance(first, int) else bass.ds(first, n)

            def expert(turn, e):
                def unit(u, name, half, step, s=0):
                    v, before = u - RING_E, 0
                    if v < 0:
                        v, before = v + U_MOE, -1
                    if KINDS_E[v] == "plain":
                        n = KINDS_E[:v + 1].count("plain") + 14 * before
                        sp.wait_ge(e_free.h, turn * 14 + s * 2 + (EARLY_PLAIN + n))
                    else:
                        low_done, n = low_at(KINDS_E[:v].count("split"))
                        sp.wait_ge(low_done.h, turn * 28 + s * 4 + (n + 28 * before))
                    rows = a[name][0]
                    if name == "moe_w_down_2":
                        dram = rows[bass.ds(e, 1), at_step(step * 512 + half * S, S), :]
                        view = expert_unit(u, 1024, 2)
                    else:
                        dram = rows[bass.ds(e, 1), half * 512:half * 512 + 512, at_step(step * 512, 512)]
                        view = expert_unit(u, 512, 4)
                    sp.dma_start(view, dram.rearrange("o (k p) n -> p (o k) n", p=P)).then_inc(
                        landed_e[slot_e(u)].h, 16)

                for u in range(4):
                    unit(u, ("moe_w_gate_2", "moe_w_up_2")[u // 2], u % 2, 0)
                for u, (name, half) in enumerate(PASS_E):
                    unit(4 + u, name, half, int(name != "moe_w_down_2"))
                with sp.Fori(0, HS - 2) as s:
                    for u, (name, half) in enumerate(PASS_E):
                        unit(4 + RING_E + u, name, half, s + (1 if name == "moe_w_down_2" else 2), s)
                for u in range(2):
                    unit(U_MOE - 2 + u, "moe_w_down_2", u, HS - 1)

            sp.wait_ge(e_free.h, EARLY_PLAIN - RING + 1)
            with sp.Fori(0, EXPERTS) as e:
                expert(e, e)
            sp.wait_ge(over_ready.h, 1)
            n_over = sp.value_load(over_n[0:1, 0:1], min_val=0, max_val=OVER)
            with sp.Fori(0, OVER) as k:
                with sp.If(n_over > k):
                    e = sp.value_load(over_n[0:1, bass.ds(k + 1, 1)], min_val=0, max_val=EXPERTS - 1)
                    expert(k + EXPERTS, e)
            for t in range(TT):
                sp.wait_ge(out_full.h, 2 * (t + 1))
                sp.dma_start(out[0, t * P:(t + 1) * P, :],
                             h[:, :, :].rearrange("p (t a) s -> p t (a s)", t=TT)[:, t, :]).then_inc(out_done, 16)
            sp.wait_ge(out_done, 16 * TT)

        d2a = signal("drained2_by_scalar", sum(o == "a" for _, o in ORDER2))
        d2v = signal("drained2_by_vector", sum(o == "v" for _, o in ORDER2))
        G2 = Groups(ORDER2, full2, d2a, d2v)
        par2_in = signal("mixer_params_landed", 16)
        sq_ready, std_ready = signal("norm_squares", 4), signal("norm_std", 1)

        xc_half, xc_t, xc_done = signal("xbc_conv", 4), signal("xbc_tanh", 4), signal("xbc_done", 4)
        z_t = signal("gate_z_tanh", 2)
        dte, dtl, dta = signal("dt_exp", 1), signal("dt_ln", 1), signal("dt_done", 1)
        dtb_r = signal("dt_spread", 1)
        em_exp, em_r = signal("decay_exp", 4), signal("decay_cb", 4)
        cf_sum, cf_sq, cf_std, cf_half, cf_t, cf_done = (signal(n, 1) for n in (
            "conf_conv", "conf_squares", "conf_std", "conf_scaled", "conf_tanh", "conf_done"))
        yz_r, yz_sq, yz_std, yn_done = (signal(n, k) for n, k in (
            ("yz_ready", 1), ("yz_squares", 1), ("yz_std", 1), ("yn_done", 2)))
        x_up = signal("x_updated")
        pad0 = sem("pads_cleared")
        b1_end = (LAYERS + 1) * DT
        ff_full, ff_t, ff_g, ff_h, ff_down = (signal(n) for n in (
            "ffn_full", "ffn_tanh", "ffn_gate_done", "ffn_h_ready", "ffn_down_done"))
        g_full, u_full, mo_t, mo_g, mo_h, hT_full, hT_ready = (signal(n, HS) for n in (
            "expert_gate_full", "expert_up_full", "expert_tanh", "expert_silu", "expert_hidden",
            "hidden_turned", "hiddenT_ready"))
        picked = signal("tokens_picked", 2)
        xg_full, xg_ready, xgl_ready = signal("gather_full", 2), signal("gathered_high", 2), signal("gathered_low", 2)
        put_full, put_ready = signal("gates_turned", 1), signal("gatesT_ready", 1)
        ye_full, ye_a, ye_v = (signal(n, 1) for n in ("result_e_full", "result_e_scalar", "result_e_vector"))
        comb_full = signal("combine_full", 4)
        comb = signal("combined", 4)
        rt_full, rt_top, rt_exp, rt_mask, rt_place, htok_full, htok_ready, x_done = (
            signal(n) for n in ("router_full", "router_top", "router_exp", "router_chosen", "places_full",
                                "h_turned", "h_tokens_ready", "experts_added"))
        nrm = {n: signal("norm_x_" + n) for n in ("sq", "full", "eps", "std", "h")}
        fin_full = signal("result_full")

        @block.tensor
        def _(pe):
            owed = [None]

            def mm(dst, w, x, start, stop, share=False):
                ins = pe.matmul(dst, w, x, start=start, stop=stop, skip_group_check=share)
                if owed[0]:
                    ins.then_inc(owed[0].h, 1)
                    owed[0] = None
                return ins

            def split_project(b, slot, lo_at, x, count, wait_x=None):
                wh, wl = (w[:, slot, :].rearrange("p (k n) -> p k n", n=S) for w in (whi, wlo))
                for t in range(2):
                    pe.wait_ge(lo_done.h, lo_at + t)
                    cols = slice(t * P, (t + 1) * P)
                    for kk in range(DT):
                        if wait_x and t == 0 and kk % 2 == 0:
                            wait_x(kk // 2)
                        mm(views(b)[:, t, :], wh[:, kk, cols], x[0][:, kk, :], kk == 0, False)
                        mm(views(b)[:, t, :], wh[:, kk, cols], x[1][:, kk, :], False, False)
                        ins = mm(views(b)[:, t, :], wl[:, kk, cols], x[0][:, kk, :], False, kk == DT - 1)
                    ins.then_inc((used if t == 0 else count).h, 1)

            def split_values(b, slot, lo_at, x, count):
                wh, wl = (w[:, slot, :].rearrange("p (k n) -> p k n", n=S) for w in (whi, wlo))
                pe.wait_ge(lo_done.h, lo_at + 1)
                for t in range(TT):
                    rows = slice(t * P, (t + 1) * P)
                    for kk in range(DT):
                        mm(views(b)[:, t, :], x[0][:, kk, rows], wh[:, kk, :], kk == 0, False)
                        mm(views(b)[:, t, :], x[1][:, kk, rows], wh[:, kk, :], False, False)
                        ins = mm(views(b)[:, t, :], x[0][:, kk, rows], wl[:, kk, :], False, kk == DT - 1)
                    ins.then_inc((used if t == 0 else count).h, 1)

            pe.wait_ge(cst_in, 16)
            pe.wait_ge(x_in, 16)
            xtok = sq[:, :, :].rearrange("p (t a) s -> p t (a s)", t=TT)
            for b in range(4):
                for t in range(2):
                    for tt in range(TT):
                        ins = pe.transpose(views(b)[:, t, tt * P:(tt + 1) * P],
                                           xtok[:, tt, (2 * b + t) * P:(2 * b + t + 1) * P], ident)
                ins.then_inc(x0_full, 1)
            pe.wait_ge(ones_set, 6)

            def layer_body(layer):
                unit, splits = [0], [0]

                def turn_to(kind):
                    u = unit[0]
                    unit[0] += 1
                    assert KINDS1[u] == kind
                    owed[0] = w_free if u and KINDS1[u - 1] == "plain" else None
                    return u

                def take(cols, k):
                    u = turn_to("plain")
                    s = landed[u % RING]
                    pe.wait_ge(s.h, s.at(layer, 16 * (u // RING + 1)))
                    return unit_view(u % RING, cols, k)

                def take_split(name):
                    turn_to("split")
                    q = splits[0]
                    splits[0] += 1
                    assert SPLIT1[q] == name
                    return q % 2, lo_done.at(layer, 2 * q + 1), (xh, xl), full

                def begin(name):
                    return G1.wait_bank(pe, layer, name)

                def project(name, w, x, k, m=P, wait_x=None):
                    b = begin(name)
                    for t in range(2):
                        for kk in range(k):
                            if wait_x and t == 0 and kk % 2 == 0:
                                wait_x(kk // 2)
                            ins = mm(views(b)[0:m, t, :], w[:, kk, t * m:(t + 1) * m], x[:, kk, :],
                                     kk == 0, kk == k - 1)
                    ins.then_inc(full.h, 1)

                def scores(n):
                    kind, b = BATCHES[n]
                    if kind == "moba":
                        G1.wait_drained(pe, layer, "aq1")
                        G1.wait_drained(pe, layer, "ak1")
                    elif kind == "diff":
                        G1.wait_drained(pe, layer, "dq1")
                        G1.wait_drained(pe, layer, "dk1")
                    else:
                        pe.wait_ge(rope_q.h, rope_q.at(layer, 4))
                        pe.wait_ge(kall.h, kall.at(layer, 1))
                        G1.wait_drained(pe, layer, "kn3")
                    if n >= 1:
                        pe.wait_ge(pT_ready.h, pT_ready.at(layer, n))

                    def qk(m):
                        if kind == "mla":
                            return qb[0:MLA_D, 4 * b + m, :], kb[0:MLA_D, 4 * b + m, :]
                        q = aqk if kind == "moba" else dqk
                        part = slice(HD * (m % 2), HD * (m % 2) + HD)
                        return q[part, 2 * b + m // 2, :], q[part, 4 + 2 * b + m // 2, :]

                    for m in range(4):
                        q, k = qk(m)
                        mm(bank[4 + m % 2][:, (m // 2) * S:(m // 2) * S + S], q[:, P:S], k, True, True)
                    for m in (0, 2, 1, 3):
                        q, k = qk(m)
                        if m == 1 and n >= 1:
                            pe.wait_ge(y_ready.h, y_ready.at(layer, n))
                        ins = mm(bank[6 + m % 2][:, (m // 2) * P:(m // 2) * P + P], q[:, 0:P], k[:, 0:P],
                                 True, True)
                    ins.then_inc(sc_full.h, 1)

                def turn(n):
                    pe.wait_ge(p_ready.h, p_ready.at(layer, n + 1))
                    maps = 2 if BATCHES[n][0] == "diff" else 4
                    for b, c0 in ((4, 256), (5, 0), (6, 128)):
                        for m in range(maps):
                            ins = pe.transpose(bank[b][:, m * P:(m + 1) * P], sc[:, m, c0:c0 + P], ident)
                    ins.then_inc(p_turned.h, 1)

                def pv(n):
                    kind, b = BATCHES[n]
                    pe.wait_ge(pT_ready.h, pT_ready.at(layer, n + 1))
                    if kind == "mla":
                        G1.wait_drained(pe, layer, "mv1")
                    else:
                        G1.wait_drained(pe, layer, "av1" if kind == "moba" else "dv1")
                    maps = 2 if kind == "diff" else 4
                    for m in range(maps):
                        if kind == "diff":
                            v = dv[:, :, (2 * b + m) * P:(2 * b + m + 1) * P]
                            dst = views(7)[:, m, :]
                        else:
                            v = (av if kind == "moba" else mv)[:, :, (4 * b + m) * HD:(4 * b + m + 1) * HD]
                            dst = views(7)[HD * (m % 2):HD * (m % 2) + HD, m // 2, :]
                        mm(dst, v[:, 0, :], pT[:, m, 0:S], True, False)
                        ins = mm(dst[:, P:S], v[:, 1, :], pT[:, m, S:S + P], False, True)
                    ins.then_inc(pv_full.h, 1)

                def wait_x(pair):
                    pe.wait_ge(xl_ready.h, xl_ready.at(layer, pair + 1))

                for name, who in ORDER1:
                    if name == "A":
                        scores(who)
                    elif name == "B":
                        turn(who)
                    elif name == "V":
                        pv(who)
                    elif name in ("av0", "av1", "dv0", "dv1"):
                        split_values(begin(name), *take_split(name))
                    elif name == "mc2":
                        w = take(160, 8)
                        b = begin(name)
                        for kk in range(8):
                            mm(views(b)[:, 0, :], w[:, kk, 0:P], xT[:, kk, :], kk == 0, kk == 7)
                        for kk in range(8):
                            ins = mm(views(b)[HD:MLA_D, 1, :], w[:, kk, P:P + ROPE], xT[:, kk, :],
                                     kk == 0, kk == 7)
                        ins.then_inc(full.h, 1)
                    elif name == "ms":
                        G1.wait_drained(pe, layer, "mc2")
                        b = begin(name)
                        for kk in range(3):
                            mm(views(b)[:, 0, :], ONES[Q_LORA], gates[:, kk, :], kk == 0, kk == 2)
                        for kk in range(2):
                            ins = mm(views(b)[:, 1, :], ONES[KV_LORA], gates[:, 3 + kk, :], kk == 0, kk == 1)
                        ins.then_inc(full.h, 1)
                    elif name == "pt":
                        w = take(256, 2)
                        b = begin(name)
                        for kk in range(2):
                            for t in range(TT):
                                ins = pe.transpose(views(b)[:, kk, t * P:(t + 1) * P],
                                                   w[:, t, kk * P:(kk + 1) * P], ident)
                                if kk + t == 0:
                                    ins.then_inc(owed[0].h, 1)
                        owed[0] = None
                        ins.then_inc(full.h, 1)
                    elif name[:2] == "pl":
                        j = int(name[2])
                        if j == 0:
                            w = take(1024, 2)
                            G1.wait_drained(pe, layer, "pt")
                        project(name, w[:, :, 256 * j:256 * j + 256], peT, 2)
                    elif name[:2] == "uq":
                        if name == "uq0":
                            pe.wait_ge(ms_done.h, ms_done.at(layer, 1))
                        project(name, take(192, 3), cn, 3, m=MLA_D)
                    elif name[:1] == "r":
                        if name == "rk":
                            G1.wait_drained(pe, layer, "mc2")
                            src, width = kr[0:MLA_D, :], S
                        else:
                            j = int(name[2])
                            G1.wait_drained(pe, layer, f"uq{j}")
                            src, width = qb[0:MLA_D, 2 * j:2 * j + 2, :], 2 * S
                        b = begin(name)
                        mm(bank[b][0:MLA_D, 0:width], cst[0:MLA_D, C_ROT:C_ROT + MLA_D], src,
                           True, True).then_inc(full.h, 1)
                    elif name[:2] == "kn":
                        j = int(name[2])
                        if j == 0:
                            w = take(1024, 2)
                        b = begin(name)
                        for t in range(2):
                            for kk in range(2):
                                c0 = (2 * j + t) * 2 * HD
                                ins = mm(views(b)[0:HD, t, :], w[:, kk, c0:c0 + HD], cn[:, 3 + kk, :],
                                         kk == 0, kk == 1)
                        ins.then_inc(full.h, 1)
                    elif name[:2] == "mv":
                        t = int(name[2])
                        b = begin(name)
                        for kk in range(2):
                            wv = w[:, kk, :].rearrange("p (h d) -> p h d", d=2 * HD)[:, :, HD:2 * HD]
                            ins = mm(bank[b][:, :].rearrange("p (h d) -> p h d", d=HD),
                                     cn[:, 3 + kk, t * P:(t + 1) * P], wv, kk == 0, kk == 1)
                        ins.then_inc(full.h, 1)
                    elif name[:2] == "dn":
                        j = int(name[2])
                        if j == 0:
                            pe.wait_ge(dn_sq.h, dn_sq.at(layer, 1))
                        b = begin(name)
                        mm(bank[b][:, :], ONES[P], gates[:, 2 * j:2 * j + 2, :], True, True).then_inc(full.h, 1)
                    elif name[:2] in ("ba", "bb", "bc"):
                        j, c = int(name[2]), "abc".index(name[1])
                        if j % 2 == 0:
                            w = take(512, 4)
                        if j == 0:
                            pe.wait_ge(gated.h, gated.at(layer, {"a": 1, "c": 2, "b": 3}[name[1]]))
                        project(name, w[:, :, 256 * (j % 2):256 * (j % 2) + 256], y[:, 4 * c:4 * c + 4, :], 4)
                    elif name[:2] == "ou":
                        project(name, take(256, 8), merged, 8, wait_x=None if name != "ou0" else (
                            lambda j: pe.wait_ge(mgd.h, mgd.at(layer, 5 + j))))
                    elif name[:2] == "pg":
                        project(name, take(256, 8), r1, 8, wait_x=None if name != "pg0" else (
                            lambda j: pe.wait_ge(r_ready.h, r_ready.at(layer, 1 + j))))
                    elif name in ("lm", "lv"):
                        b = begin(name)
                        owed[0] = w_free if name == "lm" else None
                        src, ready = (merged, r2_ready) if name == "lm" else (sq, ln_sq)
                        for kk in range(DT):
                            if kk % 2 == 0:
                                pe.wait_ge(ready.h, ready.at(layer, kk // 2 + 1))
                            ins = mm(views(b)[:, 0, :], ONES[D], src[:, kk, :], kk == 0, kk == DT - 1)
                        ins.then_inc(full.h, 1)
                    else:
                        split_project(begin(name), *take_split(name), wait_x if name == "aq0" else None)
                assert unit[0] == len(UNITS1)

            with pe.Fori(0, LAYERS) as layer:
                layer_body(layer)

            unit, splits = [0], [0]

            def owed_by(u):
                if not u or kinds2[u - 1] == "split":
                    return None
                return e_free if u - 1 >= last_plain else w_free

            def turn_to(kind):
                u = unit[0]
                unit[0] += 1
                assert kinds2[u] == kind
                owed[0] = owed_by(u)
                return u

            def take(cols, k):
                u = turn_to("plain")
                unit_wait(pe, first_units + u)
                return unit_view(u % RING, cols, k)

            def take_split(count):
                turn_to("split")
                q = splits[0]
                splits[0] += 1
                return q % 2, 2 * (first_splits + q) + 1, (hh, hl), count

            def wait_h(k):
                return lambda pair: pe.wait_ge(hl_ready.h, hl_ready.at(k, pair + 1))

            def mixer(m):
                def begin(name):
                    return G2.wait_bank(pe, m, name)

                def project(name, w, x, k=DT):
                    b = begin(name)
                    for t in range(2):
                        for kk in range(k):
                            ins = mm(views(b)[:, t, :], w[:, kk, t * P:(t + 1) * P], x[:, kk, :],
                                     kk == 0, kk == k - 1)
                    ins.then_inc(full2.h, 1)

                def project_out(name, w):
                    b = begin(name)
                    for t in range(2):
                        for n, kk in enumerate((0, 1, 6, 7, 2, 3, 4, 5)):
                            if name == "wo0" and t == 0 and kk in (2, 4):
                                pe.wait_ge(yn_done.h, yn_done.at(m, kk // 2))
                            ins = mm(views(b)[:, t, :], w[:, kk, t * P:(t + 1) * P], cat[:, kk, :],
                                     n == 0, n == DT - 1)
                    ins.then_inc(full2.h, 1)

                def mean(name, src, tiles, t=0, width=D, wait_x=None):
                    b = G2.index(name) % BANKS
                    for n, kk in enumerate(tiles):
                        if wait_x and kk % 2 == 0:
                            wait_x(kk // 2)
                        ins = mm(views(b)[:, t, :], ONES[width], src[:, kk, :], n == 0, n == len(tiles) - 1)
                    return ins

                for name, _ in ORDER2:
                    if name == "ms":
                        begin(name)
                        mean(name, sq, range(DT), wait_x=lambda j: pe.wait_ge(
                            sq_ready.h, sq_ready.at(m, j + 1))).then_inc(full2.h, 1)

                    elif name == "dt":
                        w = take(8, 8)
                        b = begin(name)
                        for t in range(TT):
                            for kk in range(DT):
                                ins = mm(bank[b][:, 8 * t:8 * t + 8], h[:, kk, t * P:(t + 1) * P],
                                         w[:, kk, :], kk == 0, kk == DT - 1)
                        ins.then_inc(full2.h, 1)
                    elif name == "acs":
                        pe.wait_ge(dta.h, dta.at(m, 1))
                        b = begin(name)
                        x = dtt[:, 7, :].rearrange("p (t e) -> p t e", t=TT)
                        mm(bank[b][:, 0:8], cst[:, C_TRI:C_TRI + P], x[:, 0, :], True, True)
                        mm(bank[b][:, 8:16], cst[:, C_TRI + P:C_TRI + S], x[:, 0, :], True, False)
                        mm(bank[b][:, 8:16], cst[:, C_TRI:C_TRI + P], x[:, 1, :], False, True).then_inc(
                            full2.h, 1)
                    elif name[:3] == "acb":
                        j = int(name[3])
                        if j == 0:
                            pe.wait_ge(dtb_r.h, dtb_r.at(m, 1))
                        b = begin(name)
                        for t in range(2):
                            mm(views(b)[:, t, :], dtb[:, 0, 2 * j + t, :], cst[:, C_TRI:C_TRI + S], True, False)
                            ins = mm(views(b)[:, t, P:S], dtb[:, 1, 2 * j + t, :], cst[:, C_TRI:C_TRI + P],
                                     False, True)
                        ins.then_inc(full2.h, 1)
                    elif name[:2] == "xt":
                        t = int(name[2])
                        if t == 0:
                            pe.wait_ge(xc_done.h, xc_done.at(m, 2))
                        b = begin(name)
                        for kk in range(4):
                            ins = pe.transpose(bank[b][:, kk * P:(kk + 1) * P], xc[:, kk, t * P:(t + 1) * P], ident)
                        ins.then_inc(full2.h, 1)
                    elif name[:2] == "cb":
                        g = int(name[2])
                        if g == 0:
                            pe.wait_ge(xc_done.h, xc_done.at(m, 4))
                        b = begin(name)
                        mm(bank[b][:, 0:S], xc[:, 4 + g, 0:P], xc[:, 6 + g, :], True, True)
                        mm(bank[b][:, S:S + P], xc[:, 4 + g, P:S], xc[:, 6 + g, P:S], True, True).then_inc(full2.h, 1)
                    elif name in ("cm", "cv"):
                        s = cf_sum if name == "cm" else cf_sq
                        pe.wait_ge(s.h, s.at(m, 1))
                        begin(name)
                        mean(name, gc if name == "cm" else sq, (0, 1) if name == "cm" else (4, 5), 0, KV_LORA).then_inc(full2.h, 1)
                    elif name[:2] == "ys":
                        j = int(name[2])
                        if j == 0:
                            G2.wait_drained(pe, m, "xt1")
                        pe.wait_ge(em_r.h, em_r.at(m, 2 * j + 2))
                        b = begin(name)
                        for hh in range(4 * j, 4 * j + 4):
                            dst = views(b)[HD * (hh % 2):HD * (hh % 2) + HD, (hh % 4) // 2, :]
                            mm(dst, xdt[:, 0, hh * HD:(hh + 1) * HD], em[:, hh, 0:S], True, False)
                            ins = mm(dst[:, P:S], xdt[:, 1, hh * HD:(hh + 1) * HD], em[:, hh, S:S + P], False, True)
                        ins.then_inc(full2.h, 1)
                    elif name == "gn":
                        pe.wait_ge(yz_sq.h, yz_sq.at(m, 1))
                        begin(name)
                        mean(name, sq, (0, 1), 0, KV_LORA)
                        mean(name, sq, (2, 3), 1, KV_LORA).then_inc(full2.h, 1)
                    elif name[:2] == "wo":
                        if name == "wo0":
                            G2.wait_drained(pe, m, "ab")
                            pe.wait_ge(cf_done.h, cf_done.at(m, 1))
                        project_out(name, take(256, 8))
                    else:
                        split_project(begin(name), *take_split(full2), wait_h(2 * m) if name == "gg" else None)

            def norm(n):
                if n < 3:
                    G2.wait_drained(pe, n - 1, [f"wo{j}" for j in range(4) if G2.index(f"wo{j}") % BANKS == 0][0])
                for kk in range(DT):
                    if kk % 2 == 0:
                        pe.wait_ge(nrm["sq"].h, 4 * (n - 1) + kk // 2 + 1)
                    ins = mm(views(0)[:, 0, :], ONES[D], sq[:, kk, :], kk == 0, kk == DT - 1)
                ins.then_inc(nrm["full"].h, 1)
                if n > 1:
                    pe.wait_ge(nrm["h"].h, n - 1)

            def down(w, x):
                for kk in range(2):
                    for t in range(DT):
                        ins = mm(views(4 + t // 2)[:, t % 2, :], w[:, kk, t * P:(t + 1) * P], x[:, kk, :],
                                 False, False, share=True)
                return ins

            def clear_sums():
                for b in range(4, 8):
                    pe.matmul(bank[b][:, :], zeros[:, 0:P], zeros[:, :], start=True, stop=True)

            mixer(0)
            norm(1)
            clear_sums()
            n0 = first_units + ffn_at
            pe.wait_ge(hl_ready.h, hl_ready.at(1, 4))
            with pe.Fori(0, FD // 2) as jj:
                for u in range(6):
                    owed[0] = owed_by(ffn_at + u)
                    if u < 4:
                        q = len(SPLIT2) + u
                        split_project(u, q % 2, jj * 8 + (2 * (first_splits + q) + 1), (hh, hl), ff_full)
                    else:
                        s = landed[(n0 + u) % RING]
                        pe.wait_ge(s.h, jj * 32 + 16 * ((n0 + u) // RING + 1))
                        pe.wait_ge(ff_h.h, jj * 2 + (u - 3))
                        down(unit_view((n0 + u) % RING, 1024, 2), hf[:, u - 4]).then_inc(ff_down.h, 1)
            unit[0] = ffn_at + 3 * (FD - 1)
            splits[0] = len(SPLIT2) + 2 * (FD - 1)
            split_project(0, *take_split(ff_full))
            split_project(1, *take_split(ff_full))
            pe.wait_ge(ff_h.h, FD)
            down(take(1024, 2), hf[:, 0]).then_inc(ff_down.h, 1)
            mixer(1)
            norm(2)
            w = take(8, 8)
            for t in range(TT):
                for kk in range(DT):
                    ins = mm(bank[1][:, 8 * t:8 * t + 8], h[:, kk, t * P:(t + 1) * P], w[:, kk, :],
                             kk == 0, kk == DT - 1)
            ins.then_inc(rt_full.h, 1)
            assert unit[0] == len(units2)
            for t in range(TT):
                for half in range(2):
                    for kk in range(4):
                        ins = pe.transpose(bank[4 + 2 * t + half][:, kk * P:(kk + 1) * P],
                                           h[:, 4 * half + kk, t * P:(t + 1) * P], ident)
                        if t + half + kk == 0:
                            ins.then_inc(e_free.h, 1)
                    ins.then_inc(htok_full.h, 1)
            pe.wait_ge(rt_mask.h, 1)
            tri, all_ = cst[:, C_TRI:C_TRI + P], cst[:, C_TRI + P:C_TRI + S]
            mm(bank[2][:, 0:8], tri, chosen[:, 0, :], True, True)
            mm(bank[2][:, 8:16], all_, chosen[:, 0, :], True, False)
            mm(bank[2][:, 8:16], tri, chosen[:, 1, :], False, True)
            mm(bank[2][:, 16:24], all_, chosen[:, 0, :], True, False)
            mm(bank[2][:, 16:24], all_, chosen[:, 1, :], False, True).then_inc(rt_place.h, 1)
            pe.wait_ge(htok_ready.h, 4)

            def gather(turn, half):
                if half == 0:
                    pe.wait_ge(picked.h, picked.at(turn, 1))
                for kk in range(4):
                    for t in range(TT):
                        ins = mm(bank[5 + half][:, kk * P:(kk + 1) * P],
                                 htok[:, t, (4 * half + kk) * P:(4 * half + kk + 1) * P], pick[:, t, :],
                                 t == 0, t == TT - 1)
                ins.then_inc(xg_full.h, 1)

            def expert(turn, ahead=None):
                def product(q, s, count, between=None):
                    u, half = q % 2, q % 2
                    b = (q % 4) // 2
                    low_done, n = low_at(q)
                    pe.wait_ge(low_done.h, turn * 28 + s * 4 + n)
                    wh, wl = (w[:, u, :].rearrange("p (k n) -> p k n", n=512) for w in (ewh, ewl))
                    for kk in range(4):
                        k = 4 * half + kk
                        mm(bank[b][:, :], xgh[:, k, :], wh[:, kk, :], k == 0, False)
                        mm(bank[b][:, :], xgl[:, k, :], wh[:, kk, :], False, False)
                        ins = mm(bank[b][:, :], xgh[:, k, :], wl[:, kk, :], False, k == DT - 1)
                        if kk == 1 and between:
                            between()
                    ins.then_inc((count if half else e_used).h, 1)

                def turn_hidden(s):
                    pe.wait_ge(mo_h.h, turn * HS + s + 1)
                    for c in range(4):
                        ins = pe.transpose(bank[2][:, c * P:(c + 1) * P], hd[:, c * P:(c + 1) * P], ident)
                    ins.then_inc(hT_full.h, 1)

                def down_(u, half, s, at=0):
                    if half == 0:
                        pe.wait_ge(hT_ready.h, turn * HS + s + 1)
                    pe.wait_ge(landed_e[slot_e(u)].h, turn * (16 * U_MOE // RING_E) + at + 16 * (u // RING_E + 1))
                    w = expert_unit(u, 1024, 2)
                    for kk in range(2):
                        for n in range(2):
                            ins = mm(bank[3 + n][:, :], hdT[:, 2 * half + kk, :],
                                     w[:, kk, n * 512:n * 512 + 512], False, False, share=True)
                    return ins

                pe.wait_ge(xgl_ready.h, xgl_ready.at(turn, 2))
                pe.wait_ge(comb.h, comb.at(turn, 1))
                product(0, 0, None)
                product(1, 0, g_full)
                pe.wait_ge(comb.h, comb.at(turn, 2))
                product(2, 0, None)
                product(3, 0, u_full)
                pe.wait_ge(comb.h, comb.at(turn, 4))
                for b in (3, 4):
                    pe.matmul(bank[b][:, :], zeros[:, 0:P], zeros[:, :], start=True, stop=True)
                with pe.Fori(0, HS - 1) as s:
                    pe.wait_ge(mo_g.h, turn * HS + s + 1)
                    product(4, s, None, lambda: turn_hidden(s))
                    down_(5, 0, s, s * 16).then_inc(e_free.h, 1)
                    product(5, s, g_full)
                    product(6, s, None)
                    down_(8, 1, s, s * 16).then_inc(e_free.h, 1)
                    product(7, s, u_full)
                if ahead is not None:
                    gather(ahead, 0)
                turn_hidden(HS - 1)
                pe.wait_ge(picked.h, picked.at(turn, 2))
                for t in range(TT):
                    ins = pe.transpose(bank[7][:, t * P:(t + 1) * P], pickg[:, t, :], ident)
                ins.then_inc(put_full.h, 1)
                down_(U_MOE - 2, 0, HS - 1).then_inc(e_free.h, 1)
                down_(U_MOE - 1, 1, HS - 1).then_inc(ye_full.h, 1)
                owed[0] = e_free
                if ahead is not None:
                    gather(ahead, 1)
                pe.wait_ge(ye_a.h, ye_a.at(turn, 1))
                pe.wait_ge(ye_v.h, ye_v.at(turn, 1))
                pe.wait_ge(put_ready.h, put_ready.at(turn, 1))
                for j, b in enumerate((0, 1, 2, 7)):
                    for t in range(2):
                        ins = mm(views(b)[:, t, :], ye[:, (2 * j + t) * P:(2 * j + t + 1) * P], put[:, :], True, True)
                    ins.then_inc(comb_full.h, 1)

            gather(0, 0)
            gather(0, 1)
            with pe.Fori(0, EXPERTS - 1) as e:
                expert(e, e + 1)
            expert(EXPERTS - 1)
            pe.wait_ge(over_ready.h, 1)
            n_over = pe.value_load(over_n[0:1, 0:1], min_val=0, max_val=OVER)
            with pe.Fori(0, OVER) as k:
                with pe.If(n_over > k):
                    gather(k + EXPERTS, 0)
                    gather(k + EXPERTS, 1)
                    expert(k + EXPERTS)
            norm(3)
            for t in range(TT):
                for half in range(2):
                    for kk in range(4):
                        ins = pe.transpose(bank[2 * t + half][:, kk * P:(kk + 1) * P],
                                           cat[:, 4 * half + kk, t * P:(t + 1) * P], ident)
                    ins.then_inc(fin_full.h, 1)


        @block.scalar
        def _(act):
            def fn(dst, src, func, **kw):
                return nc.scalar.activation(dst, src, func, **kw)

            def copy(dst, src, scale=1.0):
                return nc.scalar.activation(dst, src, ACT.Copy, scale=scale)

            def split(slot, landed_at, q_slot, free):
                act.wait_ge(landed[slot].h, landed_at)
                for t in range(2):
                    if free:
                        free(t)
                    copy(half_of(whi[:, q_slot, :], t), half_of(ring[:, slot, :], t)).then_inc(hi_done.h, 1)

            def split1(layer, q):
                u = SPLIT_AT[q] if q < len(SPLIT1) else len(UNITS1) + SPLIT_AT[q - len(SPLIT1)]
                before = SPLIT1[q - 2]

                def free(t):
                    if t == 0 and before[1] != "v":
                        act.wait_ge(used.h, used.at(layer, q - 1))
                    else:
                        G1.wait_full(act, layer, before)
                split(u % RING, landed[0].at(layer, 16 * (u // RING + 1)), q % 2, free)

            for q in range(2):
                split(SPLIT_AT[q], 16, q, None)
            for b in range(4):
                act.wait_ge(x0_full, b + 1)
                copy(xT[:, 2 * b:2 * b + 2, :], views(b)).then_inc(x_ready.h, 2)

            def layer_body(layer):
                def drain(name, dst, scale=1.0, rows=slice(0, P)):
                    b = G1.wait_full(act, layer, name)
                    copy(dst, views(b)[rows], scale).then_inc(dr_a.h, 1)

                def exps(n):
                    act.wait_ge(sc_max.h, sc_max.at(layer, n + 1))
                    for m in range(4):
                        fn(sc[:, m, 0:S], sc[:, m, 0:S], ACT.Exp, bias=nmax[:, m:m + 1],
                           accum_out=psum_[:, m:m + 1])
                        ins = fn(sc[:, m, S:384], sc[:, m, S:384], ACT.Exp, bias=nmax[:, 4 + m:5 + m],
                                 accum_out=psum_[:, 4 + m:5 + m])
                    ins.then_inc(p_exp.h, 1)

                def take_turned(n):
                    act.wait_ge(p_turned.h, p_turned.at(layer, n + 1))
                    maps = 2 if BATCHES[n][0] == "diff" else 4
                    for i, b in enumerate((4, 5, 6)):
                        ins = copy(pT[:, 0:maps, i * P:(i + 1) * P],
                                   bank[b][:, 0:maps * P].rearrange("p (m q) -> p m q", m=maps))
                    ins.then_inc(pT_ready.h, 1)

                def take_y(n):
                    kind, b = BATCHES[n]
                    act.wait_ge(pv_full.h, pv_full.at(layer, n + 1))
                    t0 = {"moba": 0, "mla": 4, "diff": 8}[kind] + 2 * b
                    copy(y[:, t0:t0 + 2, :], views(7)).then_inc(y_ready.h, 1)

                def after(name):
                    split1(layer, SPLIT1.index(name) + 2)

                def gate_tanh(names, first):
                    for i, name in enumerate(names):
                        b = G1.wait_full(act, layer, name)
                        if first + i >= 2:
                            G1.wait_drained(act, layer, ["az0", "az1", "bz0", "bz1", "cz0", "cz1"][first + i - 2])
                        fn(tmp[:, i, :], bank[b][:, :], ACT.Tanh, scale=0.5).then_inc(z_tanh.h, 1)
                        after(name)

                def merge_gate(j):
                    if j not in (3, 7, 10, 11):
                        after(f"mg{j}")
                    b = G1.wait_full(act, layer, f"mg{j}")
                    if j >= 4:
                        G1.wait_drained(act, layer, f"b{'abc'[j // 4 - 1]}{j % 4}")
                    for t in range(2):
                        ins = fn(gates[:, 2 * (j % 4) + t, :], views(b)[:, t, :], ACT.Tanh, scale=0.5,
                                 bias=par2[:, 2 * j + t:2 * j + t + 1])
                    ins.then_inc(dr_a.h, 1)
                    if j == 7:
                        after("mg7")

                scale = HD ** -0.5
                after("aq0")
                drain("aq0", aqk[:, 0:2, :], scale)
                after("aq1")
                drain("aq1", aqk[:, 2:4, :], scale)
                after("ak0")
                after("ak1")
                after("av0")
                drain("av0", av[:, :, 0:S])
                after("av1")
                drain("av1", av[:, :, S:512])
                act.wait_ge(lamp.h, lamp.at(layer, 1))
                fn(lam[:, 0:2], lam[:, 0:2], ACT.Exp).then_inc(lame.h, 1)
                exps(0)
                after("dq0")
                drain("dq0", dqk[:, 0:2, :], scale)
                after("dq1")
                drain("dq1", dqk[:, 2:4, :], scale)
                take_turned(0)
                after("dk0")
                after("dk1")
                take_y(0)
                exps(1)
                after("dv0")
                drain("dv0", dv[:, :, 0:S])
                after("dv1")
                drain("dv1", dv[:, :, S:512])
                take_turned(1)
                for i, name in enumerate(("mc0", "mc1")):
                    b = G1.wait_full(act, layer, name)
                    copy(cq[:, 2 * i:2 * i + 2, :], views(b))
                    fn(gates[:, 2 * i:2 * i + 2, :], views(b), ACT.Square).then_inc(dr_a.h, 1)
                take_y(1)
                exps(2)
                b = G1.wait_full(act, layer, "mc2")
                copy(cq[:, 4, :], views(b)[:, 0, :])
                fn(gates[:, 4, :], views(b)[:, 0, :], ACT.Square)
                copy(kr[HD:MLA_D, :], views(b)[HD:MLA_D, 1, :]).then_inc(dr_a.h, 1)
                drain("pt", peT[:, :, :])
                for j in range(2):
                    drain(f"pl{j}", pleT[:, 2 * j:2 * j + 2, :])
                G1.wait_drained(act, layer, "ms")
                fn(rstd[:, 0:2, :], rstd[:, 0:2, :], ACT.Sqrt).then_inc(ms_std.h, 1)
                take_turned(2)
                for j in range(2, 4):
                    drain(f"pl{j}", pleT[:, 2 * j:2 * j + 2, :])
                take_y(2)
                exps(3)
                for j in range(4):
                    drain(f"uq{j}", qb[0:MLA_D, 2 * j:2 * j + 2, :], MLA_D ** -0.5, slice(0, MLA_D))
                for j in range(4):
                    drain(f"kn{j}", kb[0:HD, 2 * j:2 * j + 2, :], 1.0, slice(0, HD))
                    if j % 2:
                        after(f"mc{j // 2}")
                act.wait_ge(kroped.h, kroped.at(layer, 1))
                copy(kb[HD:MLA_D, :, :], kr[HD:MLA_D, :].unsqueeze(1).broadcast_to([ROPE, HEADS, S])).then_inc(
                    kall.h, 1)
                take_turned(3)
                gate_tanh(("az0", "az1"), 0)
                take_y(3)
                act.wait_ge(y_ready.h, y_ready.at(layer, 4))
                fn(gates[:, 0:4, :], y[:, 8:12, :], ACT.Square).then_inc(dn_sq.h, 1)
                exps(4)
                gate_tanh(("bz0", "bz1"), 2)
                take_turned(4)
                gate_tanh(("cz0", "cz1"), 4)
                take_y(4)
                exps(5)
                G1.wait_drained(act, layer, "dn1")
                fn(rstd[:, :, :], rstd[:, :, :], ACT.Sqrt).then_inc(dn_std.h, 1)
                act.wait_ge(halfb.h, halfb.at(layer, 1))
                merge_gate(0)
                merge_gate(1)
                take_turned(5)
                merge_gate(2)
                merge_gate(3)
                take_y(5)
                after("mg3")
                for j in range(4, 12):
                    merge_gate(j)
                for j in range(4):
                    drain(f"ou{j}", ou[:, 2 * j:2 * j + 2, :], 0.5)
                for j in range(4):
                    b = G1.wait_full(act, layer, f"pg{j}")
                    if j >= 2:
                        act.wait_ge(r2_ready.h, r2_ready.at(layer, j - 1))
                    fn(tmp[:, j % 2, :], bank[b][:, :], ACT.Tanh, scale=0.5).then_inc(dr_a.h, 1)
                    if j >= 2:
                        after(f"mg{8 + j}")
                for j in range(4):
                    if j < 3:
                        act.wait_ge(centred.h, centred.at(layer, j + 1))
                    else:
                        G1.wait_drained(act, layer, "lm")
                    fn(sq[:, 2 * j:2 * j + 2, :], r1[:, 2 * j:2 * j + 2, :], ACT.Square).then_inc(ln_sq.h, 1)
                G1.wait_drained(act, layer, "lv")
                fn(rstd[:, 0, :], rstd[:, 0, :], ACT.Sqrt).then_inc(ln_std.h, 1)
                for t in range(DT):
                    act.wait_ge(normed.h, normed.at(layer, t + 1))
                    fn(xT[:, t, :], r1[:, t, :], ACT.Identity, bias=par[:, P_LB + t:P_LB + t + 1]).then_inc(
                        x_ready.h, 1)

            with act.Fori(0, LAYERS) as layer:
                layer_body(layer)

            def square(j):
                return fn(sq[:, 2 * j:2 * j + 2, :], xT[:, 2 * j:2 * j + 2, :], ACT.Square)

            def split2(i, free, times=0, u=None):
                n = first_units + (split_at2[i] if u is None else u)
                split(n % RING, times + 16 * (n // RING + 1), i % 2, free)

            def after(m, name):
                i = m * (len(SPLIT2) + 2 * FD) + SPLIT2.index(name)

                def free(t):
                    if t == 0:
                        act.wait_ge(used.h, first_splits + i + 1)
                    else:
                        G2.wait_full(act, m, name)
                if i + 2 < len(split_at2):
                    split2(i + 2, free)

            def high_parts(k):
                for n in range(4):
                    act.wait_ge(h_part.h, h_part.at(k, n + 1))
                    copy(hh[:, 2 * n:2 * n + 2, :], h[:, 2 * n:2 * n + 2, :]).then_inc(hh_ready.h, 1)

            def mixer(m):
                for j in range(4):
                    if m:
                        act.wait_ge(x_up.h, j + 1)
                    elif j == 0:
                        act.wait_ge(x_ready.h, b1_end)
                    square(j).then_inc(sq_ready.h, 1)
                G2.wait_drained(act, m, "ms")
                fn(rs2[:, 0, :], rs2[:, 0, :], ACT.Sqrt).then_inc(std_ready.h, 1)
                high_parts(2 * m)
                after(m, "gg")
                b = G2.wait_full(act, m, "gg")
                fn(ta[:, 0], views(b), ACT.Tanh, scale=0.5).then_inc(d2a.h, 1)
                after(m, "gv")
                after(m, "ac")
                b = G2.wait_full(act, m, "ac")
                copy(acs_b[:, :, :], views(b)).then_inc(d2a.h, 1)
                after(m, "ax")
                act.wait_ge(pad0, 3)
                for j in range(4):
                    after(m, f"xb{j}")
                    b = G2.wait_full(act, m, f"xb{j}")
                    copy(xp[:, 2 * j:2 * j + 2, SSD_TAPS - 1:], views(b)).then_inc(d2a.h, 1)
                after(m, "ab")
                for j in range(4):
                    act.wait_ge(xc_half.h, xc_half.at(m, j + 1))
                    fn(xth[:, 2 * j:2 * j + 2, :], xc[:, 2 * j:2 * j + 2, :], ACT.Tanh).then_inc(xc_t.h, 1)
                act.wait_ge(dt_neg.h, dt_neg.at(m, 1))
                act.wait_ge(par2_in.h, par2_in.at(m, par2_in.per))
                fn(bc[:, 8:16], bc[:, 8:16], ACT.Exp)
                fn(dtt[:, 2, :], dtt[:, 1, :], ACT.Exp).then_inc(dte.h, 1)
                act.wait_ge(dt_w.h, dt_w.at(m, 1))
                fn(dtt[:, 4, :], dtt[:, 3, :], ACT.Ln).then_inc(dtl.h, 1)
                G2.wait_drained(act, m, "cm")
                fn(sq[:, 4:6, :], gc[:, :, :], ACT.Square).then_inc(cf_sq.h, 1)
                for j in range(2):
                    b = G2.wait_full(act, m, f"z{j}")
                    if j == 0:
                        G2.wait_drained(act, m, "gv")
                    fn(ta[:, j], views(b), ACT.Tanh, scale=0.5).then_inc(z_t.h, 1)

                G2.wait_drained(act, m, "cv")
                fn(rs2[:, 1, :], rs2[:, 1, :], ACT.Sqrt).then_inc(cf_std.h, 1)
                act.wait_ge(cf_half.h, cf_half.at(m, 1))
                fn(yt[:, :, :], gc[:, :, :], ACT.Tanh).then_inc(cf_t.h, 1)
                for j in range(4):
                    G2.wait_drained(act, m, f"acb{j}")
                    fn(em[:, 2 * j:2 * j + 2, :], em[:, 2 * j:2 * j + 2, :], ACT.Exp).then_inc(em_exp.h, 1)
                for g in range(2):
                    b = G2.wait_full(act, m, f"cb{g}")
                    copy(cbm[:, g, :], bank[b][:, 0:384]).then_inc(d2a.h, 1)
                act.wait_ge(yz_r.h, yz_r.at(m, 1))
                fn(sq[:, 0:4, :], cat[:, 2:6, :], ACT.Square).then_inc(yz_sq.h, 1)
                G2.wait_drained(act, m, "gn")
                fn(rs2[:, 2:4, :], rs2[:, 2:4, :], ACT.Sqrt).then_inc(yz_std.h, 1)
                if m == 0:
                    after(m, "z0")
                    after(m, "z1")

            def norm(n):
                for j in range(4):
                    if n < 3:
                        G2.wait_drained(act, n - 1, f"wo{j}")
                    square(j).then_inc(nrm["sq"].h, 1)
                act.wait_ge(nrm["eps"].h, n)
                fn(rs2[:, 0, :], rs2[:, 0, :], ACT.Sqrt).then_inc(nrm["std"].h, 1)

            mixer(0)
            norm(1)
            high_parts(1)

            def after_up(jj, g):
                def free(t):
                    if t == 0:
                        act.wait_ge(used.h, jj * 4 + (first_splits + len(SPLIT2) + g + 1))
                    else:
                        act.wait_ge(ff_full.h, jj * 4 + (g + 1))
                split2(len(SPLIT2) + g + 2, free, jj * 32)

            with act.Fori(0, FD // 2) as jj:
                for half in range(2):
                    after_up(jj, 2 * half)
                    act.wait_ge(ff_full.h, jj * 4 + (2 * half + 1))
                    fn(ta[:, half], views(2 * half), ACT.Tanh, scale=0.5).then_inc(ff_t.h, 1)
                    after_up(jj, 2 * half + 1)
            act.wait_ge(ff_full.h, 2 * FD - 1)
            fn(ta[:, 0], views(0), ACT.Tanh, scale=0.5).then_inc(ff_t.h, 1)
            after_up(0, 2 * FD - 2)
            after_up(0, 2 * FD - 1)
            mixer(1)
            norm(2)
            act.wait_ge(rt_top.h, 1)
            fn(lg[:, :, 6, 0:1], lg[:, :, 5, 0:1], ACT.Exp).then_inc(rt_exp.h, 1)
            for n in range(4):
                act.wait_ge(htok_full.h, n + 1)
                copy(htok[:, n // 2, (n % 2) * 512:(n % 2) * 512 + 512], bank[4 + n][:, :]).then_inc(htok_ready.h, 1)

            def gathered(turn, half):
                act.wait_ge(xg_full.h, xg_full.at(turn, half + 1))
                copy(xgh[:, 4 * half:4 * half + 4, :], views(5 + half, 4)).then_inc(xg_ready.h, 1)

            def tanh(turn, s):
                act.wait_ge(g_full.h, turn * HS + s + 1)
                fn(ta[:, 0], views(0), ACT.Tanh, scale=0.5).then_inc(mo_t.h, 1)

            def turned(turn, s):
                act.wait_ge(hT_full.h, turn * HS + s + 1)
                copy(hdT[:, :, :], views(2, 4)).then_inc(hT_ready.h, 1)

            def high(turn, q, s=0, first=False):
                u = [n for n, kind in enumerate(KINDS_E) if kind == "split"][q]
                act.wait_ge(landed_e[slot_e(u)].h, turn * (16 * U_MOE // RING_E) + s * 16 + 16 * (u // RING_E + 1))
                if not first:
                    if q % 2 == 0:
                        act.wait_ge(e_used.h, turn * 14 + s * 2 + q // 2)
                    else:
                        count = g_full if q % 4 == 3 else u_full
                        act.wait_ge(count.h, turn * HS + s + (1 if q % 4 == 3 else 0) + q // 4)
                for k in (0, 2):
                    copy(quarter(ewh[:, q % 2], k), quarter(ring_e[:, slot_e(u)], k)).then_inc(eh_done.h, 1)

            def expert(turn, ahead=None):
                high(turn, 2)
                high(turn, 3)
                tanh(turn, 0)
                with act.Fori(0, HS - 1) as s:
                    high(turn, 4, s)
                    high(turn, 5, s)
                    turned(turn, s)
                    high(turn, 6, s)
                    high(turn, 7, s)
                    tanh(turn, s + 1)
                if ahead is not None:
                    high(ahead, 0)
                    high(ahead, 1)
                    gathered(ahead, 0)
                turned(turn, HS - 1)
                act.wait_ge(put_full.h, put_full.at(turn, 1))
                copy(put[:, :], bank[7][:, 0:S]).then_inc(put_ready.h, 1)
                act.wait_ge(ye_full.h, ye_full.at(turn, 1))
                copy(ye[:, 0:512], bank[3][:, :]).then_inc(ye_a.h, 1)
                if ahead is not None:
                    gathered(ahead, 1)

            high(0, 0, first=True)
            high(0, 1, first=True)
            gathered(0, 0)
            gathered(0, 1)
            with act.Fori(0, EXPERTS - 1) as e:
                expert(e, e + 1)
            expert(EXPERTS - 1)
            act.wait_ge(over_ready.h, 1)
            n_over = act.value_load(over_n[0:1, 0:1], min_val=0, max_val=OVER)
            with act.Fori(0, OVER) as k:
                with act.If(n_over > k):
                    high(k + EXPERTS, 0)
                    high(k + EXPERTS, 1)
                    gathered(k + EXPERTS, 0)
                    gathered(k + EXPERTS, 1)
                    expert(k + EXPERTS)
            act.wait_ge(x_done.h, 1)
            norm(3)

        @block.vector
        def _(dve):
            link_at = [0, 0]

            def tt_(dst, x, z, op):
                return nc.vector.tensor_tensor(dst, x, z, op)

            def ts(dst, x, s1, s2=None, op0=ALU.mult, op1=None):
                if op1 is None:
                    return nc.vector.tensor_scalar(dst, x, s1, None, op0)
                return nc.vector.tensor_scalar(dst, x, s1, s2, op0, op1)

            def stt(dst, x, s1, z, op0, op1):
                return nc.vector.scalar_tensor_tensor(out=dst, in0=x, scalar=s1, in1=z, op0=op0, op1=op1)

            turn = [0]

            def link(ins):
                link_at[0] += 1
                ins.then_inc(vlink.h, 1)
                dve.wait_ge(vlink.h, vlink.at(turn[0], link_at[0]))

            def layer_body(layer):
                turn[0] = layer

                def drain(name, dst):
                    b = G1.wait_full(dve, layer, name)
                    nc.vector.tensor_copy(dst, views(b)).then_inc(dr_v.h, 1)

                def softmax(n):
                    kind, bb = BATCHES[n]
                    dve.wait_ge(sc_full.h, sc_full.at(layer, n + 1))
                    dist = cst[:, C_DIST:C_DIST + S] if kind != "mla" else cst[:, C_MASK:C_MASK + S]
                    for m in range(4):
                        slope = {"moba": MOBA_SLOPES[(4 * bb + m) % 8], "mla": 1.0,
                                 "diff": DIFF_SLOPES[(2 * bb + m // 2) % 4]}[kind]
                        stt(sc[:, m, 0:S], dist, slope, bank[4 + m % 2][:, (m // 2) * S:(m // 2) * S + S],
                            ALU.mult, ALU.add)
                        ins = stt(sc[:, m, S:384], dist[:, P:S], slope,
                                  bank[6 + m % 2][:, (m // 2) * P:(m // 2) * P + P], ALU.mult, ALU.add)
                    link(ins)
                    nc.vector.tensor_reduce(nmax[:, 0:4], sc[:, :, 0:S], AX.X, ALU.max, negate=True)
                    nc.vector.tensor_reduce(nmax[:, 4:8], sc[:, :, S:384], AX.X, ALU.max, negate=True).then_inc(
                        sc_max.h, 1)
                    dve.wait_ge(p_exp.h, p_exp.at(layer, n + 1))
                    link(nc.vector.reciprocal(pinv[:, :], psum_[:, :]))
                    if kind == "diff":
                        second = pinv[:, :].rearrange("p (m c) -> p m c", c=2)[:, :, 1]
                        link(ts(second, second, lam[:, 2:3]))
                    tt_(sc[:, :, 0:S], sc[:, :, 0:S], pinv[:, 0:4].unsqueeze(2).broadcast_to([P, 4, S]), ALU.mult)
                    ins = tt_(sc[:, :, S:384], sc[:, :, S:384],
                              pinv[:, 4:8].unsqueeze(2).broadcast_to([P, 4, P]), ALU.mult)
                    if kind == "diff":
                        link(ins)
                        link(tt_(sc[:, 0, :], sc[:, 0, :], sc[:, 1, :], ALU.add))
                        ins = tt_(sc[:, 1, :], sc[:, 2, :], sc[:, 3, :], ALU.add)
                    ins.then_inc(p_ready.h, 1)

                def silu2(name, i, k):
                    b = G1.wait_full(dve, layer, name)
                    dve.wait_ge(z_tanh.h, z_tanh.at(layer, k + 1))
                    stt(zs[:, 2 * k:2 * k + 2, :], tmp[:, i, :].rearrange("p (t s) -> p t s", t=2), 1.0,
                        views(b), ALU.add, ALU.mult).then_inc(dr_v.h, 1)

                def gate(c):
                    stt(y[:, 4 * c:4 * c + 4, :], zs[:, 4 * c:4 * c + 4, :], 0.5, y[:, 4 * c:4 * c + 4, :],
                        ALU.mult, ALU.mult).then_inc(gated.h, 1)

                def x_low(i):
                    dve.wait_ge(xh_ready.h, xh_ready.at(layer, i + 1))
                    pair = slice(2 * i, 2 * i + 2)
                    tt_(xl[:, pair, :], xT[:, pair, :], xh[:, pair, :].bitcast(F32), ALU.subtract).then_inc(
                        xl_ready.h, 1)

                for i in range(4):
                    dve.wait_ge(x_ready.h, x_ready.at(layer, 2 * i + 2))
                    nc.vector.tensor_copy(xh[:, 2 * i:2 * i + 2, :], xT[:, 2 * i:2 * i + 2, :]).then_inc(
                        xh_ready.h, 1)
                    if i:
                        x_low(i - 1)
                x_low(3)
                drain("ak0", aqk[:, 4:6, :])
                drain("ak1", aqk[:, 6:8, :])
                dve.wait_ge(par_in.h, par_in.at(layer, par_in.per))
                ts(par2[:, 0:24], par[:, P_BM:P_BM + 24], 0.5).then_inc(halfb.h, 1)
                ts(par2[:, 24:25], par[:, P_SUB:P_SUB + 1], par[:, P_LAM + 1:P_LAM + 2])
                lv = par[:, P_LQK:P1_END].rearrange("p (a b d) -> p a b d", b=2, d=HD)
                link(tt_(lam_p[:, :, :], lv[:, :, 0, :], lv[:, :, 1, :], ALU.mult))
                nc.vector.tensor_reduce(lam[:, 0:2], lam_p[:, :, :], AX.X, ALU.add).then_inc(lamp.h, 1)
                dve.wait_ge(lame.h, lame.at(layer, 1))
                link(tt_(lam[:, 3:4], lam[:, 1:2], lam[:, 0:1], ALU.subtract))
                link(tt_(lam[:, 2:3], lam[:, 3:4], par[:, P_LAM:P_LAM + 1], ALU.subtract))
                softmax(0)
                drain("dk0", dqk[:, 4:6, :])
                drain("dk1", dqk[:, 6:8, :])
                softmax(1)
                softmax(2)
                b = G1.wait_full(dve, layer, "ms")
                ts(rstd[:, 0:2, :], views(b), 1e-6, None, ALU.add).then_inc(dr_v.h, 1)
                dve.wait_ge(ms_std.h, ms_std.at(layer, 1))
                link(nc.vector.reciprocal(rstd[:, 0:2, :], rstd[:, 0:2, :]))
                for t in range(5):
                    ins = stt(cn[:, t, :], cq[:, t, :], par[:, P_GQ + t:P_GQ + t + 1], rstd[:, int(t >= 3), :],
                              ALU.mult, ALU.mult)
                ins.then_inc(ms_done.h, 1)
                softmax(3)

                def rope(name, dst, j):
                    b = G1.wait_full(dve, layer, name)
                    n = 1 if name == "rk" else 2
                    r = slice(HD, MLA_D)

                    def table(c):
                        return cst[r, c:c + S].unsqueeze(1).broadcast_to([ROPE, n, S])
                    got = bank[b][r, 0:n * S].rearrange("p (t s) -> p t s", t=n)
                    turned = rot[r, j % 2, 0:n * S].rearrange("p (t s) -> p t s", t=n)
                    tt_(turned, got, table(C_SIN), ALU.mult).then_inc(dr_v.h, 1)
                    link(tt_(dst, dst, table(C_COS), ALU.mult))
                    G1.wait_drained(dve, layer, name)
                    return tt_(dst, dst, turned, ALU.add)

                rope("rk", kr[HD:MLA_D, :].unsqueeze(1), 0).then_inc(kroped.h, 1)
                for j in range(4):
                    rope(f"rq{j}", qb[HD:MLA_D, 2 * j:2 * j + 2, :], j + 1).then_inc(rope_q.h, 1)
                for t in range(TT):
                    b = G1.wait_full(dve, layer, f"mv{t}")
                    nc.vector.tensor_copy(mv[:, t, :], bank[b][:, :]).then_inc(dr_v.h, 1)
                silu2("az0", 0, 0)
                silu2("az1", 1, 1)
                dve.wait_ge(y_ready.h, y_ready.at(layer, 2))
                G1.wait_drained(dve, layer, "az1")
                gate(0)
                softmax(4)
                silu2("bz0", 0, 2)
                silu2("bz1", 1, 3)
                silu2("cz0", 0, 4)
                silu2("cz1", 1, 5)
                softmax(5)
                for j in range(2):
                    b = G1.wait_full(dve, layer, f"dn{j}")
                    ts(rstd[:, 2 * j:2 * j + 2, :], views(b), 1e-5, None, ALU.add).then_inc(dr_v.h, 1)
                dve.wait_ge(dn_std.h, dn_std.at(layer, 1))
                link(nc.vector.reciprocal(rstd[:, :, :], rstd[:, :, :]))
                link(stt(y[:, 8:12, :], y[:, 8:12, :], par2[:, 24:25], rstd[:, :, :], ALU.mult, ALU.mult))
                G1.wait_drained(dve, layer, "cz1")
                gate(2)
                dve.wait_ge(y_ready.h, y_ready.at(layer, 6))
                gate(1)
                for c, br in enumerate("abc"):
                    for j in range(4):
                        b = G1.wait_full(dve, layer, f"b{br}{j}")
                        g = gates[:, 2 * j:2 * j + 2, :]
                        G1.wait_drained(dve, layer, f"mg{4 * c + j}")
                        dst = merged[:, 2 * j:2 * j + 2, :]
                        if c == 0:
                            stt(dst, g, 1.0, views(b), ALU.add, ALU.mult).then_inc(dr_v.h, 1)
                            continue
                        u = tmp[:, j % 2, :].rearrange("p (t s) -> p t s", t=2)
                        stt(u, g, 1.0, views(b), ALU.add, ALU.mult).then_inc(dr_v.h, 1)
                        G1.wait_drained(dve, layer, f"b{br}{j}")
                        if c == 2:
                            dve.wait_ge(mgd.h, mgd.at(layer, j + 1))
                        tt_(dst, dst, u, ALU.add).then_inc(mgd.h, 1)
                for j in range(4):
                    G1.wait_drained(dve, layer, f"ou{j}")
                    stt(r1[:, 2 * j:2 * j + 2, :], xT[:, 2 * j:2 * j + 2, :], ALPHA, ou[:, 2 * j:2 * j + 2, :],
                        ALU.mult, ALU.add).then_inc(r_ready.h, 1)
                for j in range(4):
                    G1.wait_drained(dve, layer, f"pg{j}")
                    u = tmp[:, j % 2, :].rearrange("p (t s) -> p t s", t=2)
                    link(stt(u, u, 1.0, pleT[:, 2 * j:2 * j + 2, :], ALU.add, ALU.mult))
                    stt(merged[:, 2 * j:2 * j + 2, :], u, 0.5, r1[:, 2 * j:2 * j + 2, :], ALU.mult, ALU.add).then_inc(
                        r2_ready.h, 1)
                b = G1.wait_full(dve, layer, "lm")
                for j in range(4):
                    pair = slice(2 * j, 2 * j + 2)
                    tt_(r1[:, pair, :], merged[:, pair, :], views(b)[:, 0:1, :].broadcast_to([P, 2, S]),
                        ALU.subtract).then_inc((centred if j < 3 else dr_v).h, 1)
                b = G1.wait_full(dve, layer, "lv")
                ts(rstd[:, 0, :], views(b)[:, 0, :], 1e-5, None, ALU.add).then_inc(dr_v.h, 1)
                dve.wait_ge(ln_std.h, ln_std.at(layer, 1))
                link(nc.vector.reciprocal(rstd[:, 0, :], rstd[:, 0, :]))
                for t in range(DT):
                    stt(r1[:, t, :], r1[:, t, :], par[:, P_LG + t:P_LG + t + 1], rstd[:, 0, :],
                        ALU.mult, ALU.mult).then_inc(normed.h, 1)

            dve.wait_ge(x0_full, 4)
            with dve.Fori(0, LAYERS) as layer:
                layer_body(layer)
            assert link_at[0] == vlink.per, f"vector steps of a layer: {link_at[0]}"
            turn[0], link_at[0] = LAYERS, 0

            def low_part(k, n):
                dve.wait_ge(hh_ready.h, hh_ready.at(k, n + 1))
                pair = slice(2 * n, 2 * n + 2)
                tt_(hl[:, pair, :], h[:, pair, :], hh[:, pair, :].bitcast(F32), ALU.subtract).then_inc(
                    hl_ready.h, 1)

            def mixer(m):
                def drain(name):
                    return G2.wait_full(dve, m, name)

                dve.wait_ge(par2_in.h, par2_in.at(m, par2_in.per))
                for c0, c1 in ((Q_CS, Q_DS), (Q_CC, Q_CCB), (Q_CG, Q_CB + 2)):
                    ins = ts(q2[:, c0:c1], q2[:, c0:c1], 0.5)
                link(ins)
                b = drain("ms")
                ts(rs2[:, 0, :], views(b)[:, 0, :], 1e-5, None, ALU.add).then_inc(d2v.h, 1)
                dve.wait_ge(std_ready.h, std_ready.at(m, 1))
                link(nc.vector.reciprocal(rs2[:, 0, :], rs2[:, 0, :]))
                for t in range(DT):
                    ins = stt(h[:, t, :], xT[:, t, :], q2[:, Q_NM + t:Q_NM + t + 1], rs2[:, 0, :],
                              ALU.mult, ALU.mult)
                    if t % 2:
                        ins.then_inc(h_part.h, 1)
                        if t > 1:
                            low_part(2 * m, t // 2 - 1)
                low_part(2 * m, 3)
                dve.wait_ge(pad0, 3)
                b = drain("gv")
                G2.wait_drained(dve, m, "gg")
                stt(gp[:, :, CONF_TAPS - 1:], ta[:, 0], 1.0, views(b), ALU.add, ALU.mult).then_inc(d2v.h, 1)
                G2.wait_drained(dve, m, "gv")

                def conv(dsts, srcs, cols, bias, k0, k1):
                    for k in range(k0, k1):
                        for dst, src, c, bb in zip(dsts, srcs, cols, bias):
                            x = src[:, k:k + S]
                            if k == 0 and bb is not None:
                                ins = ts(dst, x, q2[:, c:c + 1], q2[:, bb:bb + 1], ALU.mult, ALU.add)
                            elif k == 0:
                                ins = ts(dst, x, q2[:, c:c + 1])
                            else:
                                ins = stt(dst, x, q2[:, c + k:c + k + 1], dst, ALU.mult, ALU.add)
                        if k < k1 - 1:
                            link(ins)
                    return ins

                def conf(k0, k1):
                    return conv([gc[:, t, :] for t in range(2)], [gp[:, t, :] for t in range(2)],
                                [Q_CC + CONF_TAPS * t for t in range(2)], [Q_CCB, Q_CCB + 1], k0, k1)

                link(conf(0, 16))
                b = drain("ax")
                G2.wait_drained(dve, m, "ac")
                tt_(ap_[:, :, A_TAPS - 1:], acs_b[:, :, :], views(b), ALU.mult).then_inc(d2v.h, 1)
                G2.wait_drained(dve, m, "ax")
                conv([ac_y[:, t, :] for t in range(2)], [ap_[:, t, :] for t in range(2)],
                     [Q_CA + A_TAPS * t for t in range(2)], [None, None], 0, A_TAPS).then_inc(vlink.h, 1)
                link_at[0] += 1
                ac_link = list(link_at)
                conf(16, CONF_TAPS).then_inc(cf_sum.h, 1)
                for j in range(4):
                    G2.wait_drained(dve, m, f"xb{j}")
                    conv([xc[:, t, :] for t in (2 * j, 2 * j + 1)], [xp[:, t, :] for t in (2 * j, 2 * j + 1)],
                         [Q_CS + SSD_TAPS * t for t in (2 * j, 2 * j + 1)],
                         [Q_CSB + t for t in (2 * j, 2 * j + 1)], 0, SSD_TAPS).then_inc(xc_half.h, 1)
                    if j:
                        silu_x(m, j - 1)
                b = drain("dt")
                v2 = dtt[:, 0, :].rearrange("p (t e) -> p t e", t=TT)
                tt_(v2, bank[b][:, 0:16].rearrange("p (t e) -> p t e", t=TT),
                    bc[:, 0:8].unsqueeze(1).broadcast_to([P, TT, 8]), ALU.add).then_inc(d2v.h, 1)
                G2.wait_drained(dve, m, "dt")
                stt(dtt[:, 1, :], dtt[:, 0, :], -1.0, dtt[:, 0, :], ALU.mult, ALU.min).then_inc(dt_neg.h, 1)
                b = drain("ab")
                dve.wait_ge(vlink.h, vlink.at(LAYERS, ac_link[0]))
                tt_(cat[:, 0:2, :], views(b), ac_y[:, :, :], ALU.mult).then_inc(d2v.h, 1)
                b = drain("cm")
                tt_(gc[:, :, :], gc[:, :, :], views(b)[:, 0:1, :].broadcast_to([P, 2, S]), ALU.subtract).then_inc(d2v.h, 1)
                dve.wait_ge(dte.h, dte.at(m, 1))
                ts(dtt[:, 3, :], dtt[:, 2, :], 1.0, None, ALU.add).then_inc(dt_w.h, 1)
                silu_x(m, 3)
                dve.wait_ge(dt_w.h, dt_w.at(m, 1))
                link(ts(dtt[:, 5, :], dtt[:, 3, :], 1.0, None, ALU.is_equal))
                dve.wait_ge(dtl.h, dtl.at(m, 1))
                tt_(dtt[:, 4, :], dtt[:, 4, :], dtt[:, 5, :], ALU.add)
                link(stt(dtt[:, 3, :], dtt[:, 3, :], -1.0, dtt[:, 5, :], ALU.add, ALU.add))
                link(nc.vector.reciprocal(dtt[:, 3, :], dtt[:, 3, :]))
                link(tt_(dtt[:, 4, :], dtt[:, 4, :], dtt[:, 3, :], ALU.mult))
                link(tt_(dtt[:, 4, :], dtt[:, 4, :], dtt[:, 2, :], ALU.mult))
                link(stt(dtt[:, 6, :], dtt[:, 0, :], 0.0, dtt[:, 4, :], ALU.max, ALU.add))
                stt(dtt[:, 7, :].rearrange("p (t e) -> p t e", t=TT),
                    dtt[:, 6, :].rearrange("p (t e) -> p t e", t=TT), -1.0,
                    bc[:, 8:16].unsqueeze(1).broadcast_to([P, TT, 8]), ALU.mult, ALU.mult).then_inc(dta.h, 1)
                dve.wait_ge(dta.h, dta.at(m, 1))
                nc.vector.tensor_copy(dtb[:, :, :, :].rearrange("p t e k -> p (t e) k"),
                                      dtt[:, 7, :].unsqueeze(2).broadcast_to([P, TT * 8, P])).then_inc(dtb_r.h, 1)
                for j in range(2):
                    b = drain(f"z{j}")
                    dve.wait_ge(z_t.h, z_t.at(m, j + 1))
                    stt(sz[:, 2 * j:2 * j + 2, :], ta[:, j], 1.0, views(b), ALU.add, ALU.mult).then_inc(d2v.h, 1)
                b = drain("cv")
                ts(rs2[:, 1, :], views(b)[:, 0, :], 1e-5, None, ALU.add).then_inc(d2v.h, 1)
                b = drain("acs")
                nc.vector.tensor_copy(acs[:, :, :], bank[b][:, 0:16].rearrange("p (t e) -> p t e", t=TT)).then_inc(
                    d2v.h, 1)
                dve.wait_ge(cf_std.h, cf_std.at(m, 1))
                link(nc.vector.reciprocal(rs2[:, 1, :], rs2[:, 1, :]))
                for t in range(2):
                    ins = stt(gc[:, t, :], gc[:, t, :], q2[:, Q_CG + t:Q_CG + t + 1], rs2[:, 1, :], ALU.mult, ALU.mult)
                link(ins)
                for t in range(2):
                    ins = ts(gc[:, t, :], gc[:, t, :], q2[:, Q_CB + t:Q_CB + t + 1], None, ALU.add)
                ins.then_inc(cf_half.h, 1)
                G2.wait_drained(dve, m, "acs")
                for j in range(4):
                    b = drain(f"acb{j}")
                    mask = cst[:, C_MASKT:C_MASKT + S]
                    for t in range(2):
                        e = 2 * j + t
                        stt(em[:, e, 0:S], views(b)[:, t, :], acs[:, 0, e:e + 1], mask, ALU.subtract, ALU.add)
                        ins = stt(em[:, e, S:384], views(b)[:, t, P:S], acs[:, 1, e:e + 1], mask[:, 0:P],
                                  ALU.subtract, ALU.add)
                    ins.then_inc(d2v.h, 1)
                for t in range(TT):
                    b = drain(f"xt{t}")
                    tt_(xdt[:, t, :].rearrange("p (e d) -> p e d", d=HD),
                        bank[b][:, :].rearrange("p (e d) -> p e d", d=HD),
                        dtt[:, 6, 8 * t:8 * t + 8].unsqueeze(2).broadcast_to([P, 8, HD]), ALU.mult).then_inc(d2v.h, 1)
                dve.wait_ge(cf_t.h, cf_t.at(m, 1))
                stt(cat[:, 6:8, :], yt[:, :, :], 1.0, gc[:, :, :], ALU.add, ALU.mult).then_inc(cf_done.h, 1)
                for j in range(4):
                    dve.wait_ge(em_exp.h, em_exp.at(m, j + 1))
                    G2.wait_drained(dve, m, f"cb{j // 2}")
                    tt_(em[:, 2 * j:2 * j + 2, :], em[:, 2 * j:2 * j + 2, :],
                        cbm[:, j // 2:j // 2 + 1, :].broadcast_to([P, 2, 384]), ALU.mult).then_inc(em_r.h, 1)
                for j in range(2):
                    b = drain(f"ys{j}")
                    for t in range(2):
                        k = 2 * j + t
                        ins = stt(cat[:, 2 + k, :], xc[:, k, :], q2[:, Q_DS + k:Q_DS + k + 1], views(b)[:, t, :],
                                  ALU.mult, ALU.add)
                    ins.then_inc(d2v.h, 1)
                G2.wait_drained(dve, m, "ys1")
                stt(cat[:, 2:6, :], sz[:, :, :], 0.5, cat[:, 2:6, :], ALU.mult, ALU.mult).then_inc(yz_r.h, 1)
                b = drain("gn")
                ts(rs2[:, 2:4, :], views(b), 1e-5, None, ALU.add).then_inc(d2v.h, 1)
                dve.wait_ge(yz_std.h, yz_std.at(m, 1))
                for g in range(2):
                    link(nc.vector.reciprocal(rs2[:, 2 + g, :], rs2[:, 2 + g, :]))
                    for t in (2 * g, 2 * g + 1):
                        ins = stt(cat[:, 2 + t, :], cat[:, 2 + t, :], q2[:, Q_NW + t:Q_NW + t + 1], rs2[:, 2 + g, :],
                                  ALU.mult, ALU.mult)
                    ins.then_inc(yn_done.h, 1)
                for j in range(4):
                    b = drain(f"wo{j}")
                    tt_(xT[:, 2 * j:2 * j + 2, :], xT[:, 2 * j:2 * j + 2, :], views(b), ALU.add).then_inc(d2v.h, 1)
                G2.wait_drained(dve, m, "wo3")

            def silu_x(m, j):
                dve.wait_ge(xc_t.h, xc_t.at(m, j + 1))
                stt(xc[:, 2 * j:2 * j + 2, :], xth[:, 2 * j:2 * j + 2, :], 1.0, xc[:, 2 * j:2 * j + 2, :],
                    ALU.add, ALU.mult).then_inc(xc_done.h, 1)

            def norm(n, dst, w):
                dve.wait_ge(nrm["full"].h, n)
                ts(rs2[:, 0, :], views(0)[:, 0, :], 1e-5, None, ALU.add).then_inc(nrm["eps"].h, 1)
                dve.wait_ge(nrm["std"].h, n)
                link(nc.vector.reciprocal(rs2[:, 0, :], rs2[:, 0, :]))
                for t in range(DT):
                    ins = stt(dst[:, t, :], xT[:, t, :], q2[:, w + t:w + t + 1], rs2[:, 0, :], ALU.mult, ALU.mult)
                    if n == 1 and t % 2:
                        ins.then_inc(h_part.h, 1)
                        if t > 1:
                            low_part(1, t // 2 - 1)
                if n == 1:
                    low_part(1, 3)
                else:
                    ins.then_inc(nrm["h"].h, 1)

            def add_sums():
                for j in range(4):
                    tt_(xT[:, 2 * j:2 * j + 2, :], xT[:, 2 * j:2 * j + 2, :], views(4 + j), ALU.add).then_inc(x_up.h, 1)

            mixer(0)
            norm(1, h, Q_NF)
            with dve.Fori(0, FD // 2) as jj:
                for half in range(2):
                    dve.wait_ge(ff_t.h, jj * 2 + (half + 1))
                    stt(tb[:, half], ta[:, half], 1.0, views(2 * half), ALU.add, ALU.mult).then_inc(ff_g.h, 1)
                    dve.wait_ge(ff_g.h, jj * 2 + (half + 1))
                    dve.wait_ge(ff_full.h, jj * 4 + (2 * half + 2))
                    stt(hf[:, half], tb[:, half], 0.5, views(2 * half + 1), ALU.mult, ALU.mult).then_inc(ff_h.h, 1)
            dve.wait_ge(ff_t.h, FD)
            stt(tb[:, 0], ta[:, 0], 1.0, views(0), ALU.add, ALU.mult).then_inc(ff_g.h, 1)
            dve.wait_ge(ff_g.h, FD)
            dve.wait_ge(ff_full.h, 2 * FD)
            stt(hf[:, 0], tb[:, 0], 0.5, views(1), ALU.mult, ALU.mult).then_inc(ff_h.h, 1)
            dve.wait_ge(ff_down.h, FD)
            add_sums()
            dve.wait_ge(x_up.h, 4)
            mixer(1)
            norm(2, h, Q_NF)

            def spread(x):
                return x.broadcast_to([P, TT, 8])

            desc = cst[:, C_DESC:C_DESC + 8].unsqueeze(1).broadcast_to([P, TT, 8])
            dve.wait_ge(rt_full.h, 1)
            link(nc.vector.tensor_copy(lg[:, :, 0, :], bank[1][:, 0:16].rearrange("p (t e) -> p t e", t=TT)))

            def choose(src, to, top):
                link(nc.vector.tensor_reduce(lg[:, :, 4, top:top + 1], lg[:, :, src, :], AX.X, ALU.max))
                link(tt_(lg[:, :, to, :], lg[:, :, src, :], spread(lg[:, :, 4, top:top + 1]), ALU.is_equal))
                link(tt_(lg[:, :, to, :], lg[:, :, to, :], desc, ALU.mult))
                link(nc.vector.tensor_reduce(lg[:, :, 4, 2:3], lg[:, :, to, :], AX.X, ALU.max))
                link(tt_(lg[:, :, to, :], lg[:, :, to, :], spread(lg[:, :, 4, 2:3]), ALU.is_equal))

            choose(0, 1, 0)
            link(stt(lg[:, :, 2, :], lg[:, :, 1, :], -3e38, lg[:, :, 0, :], ALU.mult, ALU.add))
            choose(2, 3, 1)
            tt_(lg[:, :, 5, 0:1], lg[:, :, 4, 1:2], lg[:, :, 4, 0:1], ALU.subtract).then_inc(rt_top.h, 1)
            tt_(chosen[:, :, :], lg[:, :, 1, :], lg[:, :, 3, :], ALU.add).then_inc(rt_mask.h, 1)
            dve.wait_ge(rt_exp.h, 1)
            link(ts(lg[:, :, 7, 2:3], lg[:, :, 6, 0:1], 1.0, None, ALU.add))
            link(nc.vector.reciprocal(lg[:, :, 7, 0:1], lg[:, :, 7, 2:3]))
            link(tt_(lg[:, :, 7, 1:2], lg[:, :, 6, 0:1], lg[:, :, 7, 0:1], ALU.mult))
            tt_(lg[:, :, 1, :], lg[:, :, 1, :], spread(lg[:, :, 7, 0:1]), ALU.mult)
            link(tt_(lg[:, :, 3, :], lg[:, :, 3, :], spread(lg[:, :, 7, 1:2]), ALU.mult))
            link(tt_(gmat[:, :, :], lg[:, :, 1, :], lg[:, :, 3, :], ALU.add))
            link(ts(gmat[:, :, :], gmat[:, :, :], 0.5))
            dve.wait_ge(rt_place.h, 1)
            link(tt_(place[:, :, :], bank[2][:, 0:16].rearrange("p (t e) -> p t e", t=TT), chosen[:, :, :], ALU.mult))
            link(ts(place[:, :, :], place[:, :, :], -1.0, None, ALU.add))

            slots = cst[:, C_IOTA:C_IOTA + P].unsqueeze(1).broadcast_to([P, TT, P])

            def pick_slots(turn, where, e):
                tt_(pick[:, :, :], slots, where[:, :, bass.ds(e, 1)].broadcast_to([P, TT, P]),
                    ALU.is_equal).then_inc(picked.h, 1)
                dve.wait_ge(picked.h, picked.at(turn, 1))

            def pick_gates(e):
                tt_(pickg[:, :, :], pick[:, :, :], gmat[:, :, bass.ds(e, 1)].broadcast_to([P, TT, P]),
                    ALU.mult).then_inc(picked.h, 1)

            pick_slots(0, place, 0)
            pick_gates(0)
            ts(place2[:, :, :], place[:, :, :], -float(P), None, ALU.add)
            link(ts(over[:, 0, :], bank[2][:, 16:24], P + 0.5, None, ALU.is_gt))
            link(nc.vector.tensor_reduce(over[:, 2, 0:1], over[:, 0, :], AX.X, ALU.add))
            link(tt_(over[:, 0, :], over[:, 0, :], cst[:, C_DESC:C_DESC + 8], ALU.mult))
            for k in range(OVER):
                link(nc.vector.tensor_reduce(over[:, 1, 0:1], over[:, 0, :], AX.X, ALU.max))
                link(ts(over[:, 2, k + 1:k + 2], over[:, 1, 0:1], -1.0, float(EXPERTS), ALU.mult, ALU.add))
                link(stt(over[:, 0, :], over[:, 0, :], over[:, 1, 0:1], over[:, 0, :], ALU.is_lt, ALU.mult))
            ts(over_n[:, :], over[:, 2, 0:4], float(EXPERTS - 1), None, ALU.min).then_inc(over_ready.h, 1)
            dve.wait_ge(htok_ready.h, 4)
            dve.wait_ge(over_ready.h, 1)
            nc.vector.memset(over[:, 3, :], 0.0).then_inc(comb.h, 4)

            def silu_gate(turn, s):
                dve.wait_ge(mo_t.h, turn * HS + s + 1)
                stt(tb[:, 0], ta[:, 0], 1.0, views(0), ALU.add, ALU.mult).then_inc(mo_g.h, 1)

            def times_up(turn, s):
                dve.wait_ge(mo_g.h, turn * HS + s + 1)
                dve.wait_ge(u_full.h, turn * HS + s + 1)
                tt_(hd[:, :], tb[:, 0].rearrange("p t s -> p (t s)"), bank[1][:, :], ALU.mult).then_inc(mo_h.h, 1)

            def low(turn, q, s=0):
                u = [n for n, kind in enumerate(KINDS_E) if kind == "split"][q]
                for k in (0, 2):
                    dve.wait_ge(eh_done.h, turn * 56 + s * 8 + (2 * q + k // 2 + 1))
                    tt_(quarter(ewl[:, q % 2], k), quarter(ring_e[:, slot_e(u)], k),
                        quarter(ewh[:, q % 2], k).bitcast(F32), ALU.subtract).then_inc(ev_done.h, 1)

            def gathered_low(turn, half):
                dve.wait_ge(xg_ready.h, xg_ready.at(turn, half + 1))
                part = slice(4 * half, 4 * half + 4)
                tt_(xgl[:, part, :], views(5 + half, 4), xgh[:, part, :].bitcast(F32), ALU.subtract).then_inc(
                    xgl_ready.h, 1)

            def expert(turn, ahead=None):
                if ahead is not None:
                    dve.wait_ge(xg_full.h, xg_full.at(turn, 2))
                    dve.wait_ge(picked.h, picked.at(turn, 2))
                    pick_slots(ahead, place, ahead)
                low(turn, 2)
                silu_gate(turn, 0)
                with dve.Fori(0, HS - 1) as s:
                    low(turn, 4, s)
                    times_up(turn, s)
                    low(turn, 6, s)
                    silu_gate(turn, s + 1)
                if ahead is not None:
                    low(ahead, 0)
                times_up(turn, HS - 1)
                if ahead is not None:
                    gathered_low(ahead, 0)
                    dve.wait_ge(put_full.h, put_full.at(turn, 1))
                    pick_gates(ahead)
                dve.wait_ge(ye_full.h, ye_full.at(turn, 1))
                nc.vector.tensor_copy(ye[:, 512:D], bank[4][:, :]).then_inc(ye_v.h, 1)
                if ahead is not None:
                    gathered_low(ahead, 1)
                for j, b in enumerate((0, 1, 2, 7)):
                    dve.wait_ge(comb_full.h, comb_full.at(turn, j + 1))
                    tt_(xT[:, 2 * j:2 * j + 2, :], xT[:, 2 * j:2 * j + 2, :], views(b), ALU.add).then_inc(comb.h, 1)

            low(0, 0)
            gathered_low(0, 0)
            gathered_low(0, 1)
            with dve.Fori(0, EXPERTS - 1) as e:
                expert(e, e + 1)
            expert(EXPERTS - 1)
            dve.wait_ge(comb.h, comb.at(EXPERTS, 4))
            n_over = dve.value_load(over_n[0:1, 0:1], min_val=0, max_val=OVER)
            with dve.Fori(0, OVER) as k:
                with dve.If(n_over > k):
                    e = dve.value_load(over_n[0:1, bass.ds(k + 1, 1)], min_val=0, max_val=EXPERTS - 1)
                    turn2 = k + EXPERTS
                    pick_slots(turn2, place2, e)
                    pick_gates(e)
                    low(turn2, 0)
                    gathered_low(turn2, 0)
                    gathered_low(turn2, 1)
                    expert(turn2)
                    dve.wait_ge(comb.h, comb.at(turn2 + 1, 4))
                    nc.vector.memset(over[:, 1, :], 0.0)
            nc.vector.memset(over[:, 3, :], 0.0).then_inc(x_done.h, 1)
            dve.wait_ge(x_done.h, 1)
            norm(3, cat, Q_NL)
            for n in range(4):
                dve.wait_ge(fin_full.h, n + 1)
                nc.vector.tensor_copy(h[:, 2 * n:2 * n + 2, :], views(n)).then_inc(out_full.h, 1)

        @block.gpsimd
        def _(pool):
            nc.gpsimd.memset(ones[:, 0], 1.0 / D).then_inc(ones_set, 1)
            nc.gpsimd.memset(ones[:, 1], 1.0 / Q_LORA).then_inc(ones_set, 1)
            nc.gpsimd.memset(ones[:, 2], 1.0 / KV_LORA).then_inc(ones_set, 1)
            nc.gpsimd.memset(ones[:, 3], 1.0 / P).then_inc(ones_set, 1)
            nc.gpsimd.memset(zeros[:, 0:256], 0.0).then_inc(w_free.h, RING)
            nc.gpsimd.memset(kr[0:HD, :], 0.0).then_inc(ones_set, 1)
            nc.gpsimd.memset(zeros[:, 256:512], 0.0).then_inc(ones_set, 1)
            nc.gpsimd.memset(room[:, 0:1], 0.0).then_inc(e_free.h, EARLY_PLAIN - RING)
            nc.gpsimd.memset(room[:, 1:2], 0.0).then_inc(ev_done.h, EARLY_V)
            nc.gpsimd.memset(room[:, 2:3], 0.0).then_inc(ep_done.h, EARLY_P)

            def low(slot, q_slot, hi_at):
                for t in range(2):
                    pool.wait_ge(hi_done.h, hi_at + t)
                    nc.gpsimd.tensor_tensor(half_of(wlo[:, q_slot, :], t), half_of(ring[:, slot, :], t),
                                            half_of(whi[:, q_slot, :], t).bitcast(F32), ALU.subtract).then_inc(
                        lo_done.h, 1)

            for q in range(2):
                low(SPLIT_AT[q], q, 2 * q + 1)
            with pool.Fori(0, LAYERS) as layer:
                pool.wait_ge(x_ready.h, x_ready.at(layer, DT))
                pool.dma_start(par[:, :], a["params1"][bass.ds(layer, 1), :, :].rearrange("o p c -> (o p) c")).then_inc(
                    par_in.h, 16)
                for q in range(2, len(SPLIT1) + 2):
                    u = SPLIT_AT[q] if q < len(SPLIT1) else len(UNITS1) + SPLIT_AT[q - len(SPLIT1)]
                    low(u % RING, q % 2, hi_done.at(layer, 2 * q + 1))

            def low2(i, times=0):
                n = first_units + split_at2[i]
                low(n % RING, i % 2, times + (2 * (first_splits + i) + 1))

            for m in range(LAYERS):
                if m == 0:
                    pool.wait_ge(x_ready.h, b1_end)
                    nc.gpsimd.memset(gp[:, :, 0:CONF_TAPS - 1], 0.0).then_inc(pad0, 1)
                    nc.gpsimd.memset(ap_[:, :, 0:A_TAPS - 1], 0.0).then_inc(pad0, 1)
                    nc.gpsimd.memset(xp[:, :, 0:SSD_TAPS - 1], 0.0).then_inc(pad0, 1)
                else:
                    pool.wait_ge(x_up.h, 4)

                pool.dma_start(q2[:, :], a["params2"][m, :, :]).then_inc(par2_in.h, 16)
                first = m * (len(SPLIT2) + 2 * FD)
                for i in range(first + 2, min(first + len(SPLIT2) + 2, len(split_at2))):
                    low2(i)
                if m == 0:
                    with pool.Fori(0, FD // 2) as jj:
                        for g in range(4):
                            low2(len(SPLIT2) + 2 + g, jj * 8)
                    for g in range(2 * FD, 2 * FD + 2):
                        low2(len(SPLIT2) + g)

            def low_e(turn, q, s=0):
                u = [n for n, kind in enumerate(KINDS_E) if kind == "split"][q]
                for k in (0, 2):
                    pool.wait_ge(eh_done.h, turn * 56 + s * 8 + (2 * q + k // 2 + 1))
                    nc.gpsimd.tensor_tensor(quarter(ewl[:, q % 2], k), quarter(ring_e[:, slot_e(u)], k),
                                            quarter(ewh[:, q % 2], k).bitcast(F32), ALU.subtract).then_inc(
                        ep_done.h, 1)

            def expert(turn, ahead=None):
                low_e(turn, 3)
                with pool.Fori(0, HS - 1) as s:
                    low_e(turn, 5, s)
                    low_e(turn, 7, s)
                if ahead is not None:
                    low_e(ahead, 1)

            low_e(0, 1)
            with pool.Fori(0, EXPERTS - 1) as e:
                expert(e, e + 1)
            expert(EXPERTS - 1)
            pool.wait_ge(over_ready.h, 1)
            n_over = pool.value_load(over_n[0:1, 0:1], min_val=0, max_val=OVER)
            with pool.Fori(0, OVER) as k:
                with pool.If(n_over > k):
                    low_e(k + EXPERTS, 1)
                    expert(k + EXPERTS)


_LARGE = ['x', 'p', 'w_in', 'mla_w_uq', 'mla_w_ukv', 'w_branch_a', 'w_branch_b', 'w_branch_c', 'w_merge', 'w_out',
          'w_ple_gate', 'w_ple', 'w_in_2', 'w_out_2', 'ffn_w_gate_2', 'ffn_w_up_2', 'ffn_w_down_2', 'moe_router_2',
          'moe_w_gate_2', 'moe_w_up_2', 'moe_w_down_2']
_SMALL = ['mla_q_norm_g', 'mla_kv_norm_g', 'diff_lambda', 'diff_subln_g', 'b_merge', 'ln_g', 'ln_b', 'norm_mix_2',
          'conv_a_w_2', 'conv_ssd_w_2', 'conv_ssd_b_2', 'dt_bias_2', 'a_log_2', 'd_skip_2', 'ssd_norm_w_2',
          'conv_conf_w_2', 'conv_conf_b_2', 'conf_ln_g_2', 'conf_ln_b_2', 'norm_ffn_2', 'norm_final_2']


def kernel(**inputs):
    import concourse.bacc as _bacc
    from concourse.bass_utils import run_bass_kernel_spmd as _run

    nc = _bacc.Bacc("TRN2", target_bir_lowering=False, num_devices=1)
    table = constants()
    v = {name: np.asarray(inputs[name]) for name in _SMALL}
    given = {name: np.ascontiguousarray(inputs[name]) for name in _LARGE}
    given["cst"] = table
    lam = np.broadcast_to(table[0, C_LAM:C_LAM + 4].reshape(LAYERS, 1, 2), (LAYERS, P, 2))
    given["params1"] = np.ascontiguousarray(np.concatenate(
        [by_feature(v[n]) for n in ("mla_q_norm_g", "mla_kv_norm_g", "diff_subln_g", "b_merge", "ln_g", "ln_b")]
        + [lam, on_all(v["diff_lambda"].reshape(LAYERS, -1))], axis=2))
    last = np.broadcast_to(v["norm_final_2"][None], (LAYERS, D))
    given["params2"] = np.ascontiguousarray(np.concatenate(
        [by_feature(v[n]) for n in ("norm_mix_2", "conv_a_w_2", "conv_ssd_w_2", "conv_ssd_b_2")]
        + [by_feature(np.repeat(v["d_skip_2"], HD, axis=1))]
        + [by_feature(v[n]) for n in ("ssd_norm_w_2", "conv_conf_w_2", "conv_conf_b_2", "conf_ln_g_2",
                                      "conf_ln_b_2", "norm_ffn_2")]
        + [by_feature(last), on_all(v["dt_bias_2"]), on_all(v["a_log_2"])], axis=2))
    arrays, args = {}, {}
    for name, v in given.items():
        arrays[f"in_{name}_dram"] = v
        args[name] = nc.dram_tensor(f"in_{name}_dram", v.shape, mybir.dt.from_np(v.dtype), kind="ExternalInput").ap()
    out = nc.dram_tensor("out_0_dram", (1, S, D), F32, kind="ExternalOutput").ap()
    build_kernel(nc, args, out)
    r = _run(nc, [arrays], core_ids=[0])
    return r.results[0]["out_0_dram"]
```
